# Optimizing a Trainium2 kernel written in Bass

```python
import math
import jax, jax.numpy as jnp
from jax import lax
import numpy as np

D_MODEL = 1024
BATCH = 1
SEQ = 256
DEPTH = 1

HEAD_DIM = 64
NSA_HEADS = 8
NSA_GROUPS = 2
NSA_HPG = NSA_HEADS // NSA_GROUPS
CMP_LEN = 32
CMP_STRIDE = 16
CMP_HIDDEN = 256
SEL_BLOCK = 64
SEL_TOPN = 16
WINDOW = 512
SB_HEADS = 8
Q_BLOCK = 128
ROPE_THETA = 10000.0
PEER_HEADS = 8
PEER_NKEYS = 128
PEER_N_EXPERTS = PEER_NKEYS * PEER_NKEYS
PEER_QDIM = 256
PEER_TOPK = 16
PEER_CHUNK = 128
EPS = 1e-6
NEG = -1e30

NSA_W = NSA_HEADS * HEAD_DIM
KV_W = NSA_GROUPS * HEAD_DIM
SB_W = SB_HEADS * HEAD_DIM
IN_WIDTH = NSA_W + 6 * KV_W + 3 * NSA_HEADS + 3 * SB_W + 2 * D_MODEL

kernel_name = "hybrid_nsa_stickbreaking_peer_block"

def rms_norm(x, g):
    xf = x.astype(jnp.float32)
    return xf * lax.rsqrt(jnp.mean(xf * xf, axis=-1, keepdims=True) + EPS) * g.astype(jnp.float32)

def rope(x, pos):
    half = HEAD_DIM // 2
    freqs = ROPE_THETA ** (-jnp.arange(half, dtype=jnp.float32) / half)
    ang = pos.astype(jnp.float32)[:, None] * freqs[None, :]
    cos, sin = jnp.cos(ang), jnp.sin(ang)
    x1, x2 = x[..., :half], x[..., half:]
    return jnp.concatenate([x1 * cos - x2 * sin, x2 * cos + x1 * sin], axis=-1)

def compress(tok, pos_emb, w1, w2):
    s = tok.shape[2]
    nc = (s - CMP_LEN) // CMP_STRIDE + 1
    idx = jnp.arange(nc)[:, None] * CMP_STRIDE + jnp.arange(CMP_LEN)[None, :]
    blocks = tok[:, :, idx] + pos_emb.astype(jnp.float32)
    flat = blocks.reshape(blocks.shape[0], blocks.shape[1], nc, CMP_LEN * HEAD_DIM)
    return jax.nn.gelu(flat @ w1) @ w2

def token_mixers(xn, w_in, q_norm_g, k_norm_g, cmp_pos_k, cmp_pos_v, cmp_k_w1, cmp_k_w2,
                 cmp_v_w1, cmp_v_w2, w_branch_nsa, w_branch_sb, w_out):
    b, s, _ = xn.shape
    scale = 1.0 / math.sqrt(HEAD_DIM)
    pos = jnp.arange(s)
    proj = xn @ w_in
    c0 = NSA_W
    c1 = c0 + 6 * KV_W
    c2 = c1 + 3 * NSA_HEADS
    c3 = c2 + 3 * SB_W
    q_n, kv_n, g_n, qkv_sb, br_g = jnp.split(proj, [c0, c1, c2, c3], axis=-1)

    q = q_n.reshape(b, s, NSA_GROUPS, NSA_HPG, HEAD_DIM).transpose(0, 2, 3, 1, 4)
    q = rope(rms_norm(q, q_norm_g), pos)
    kv = kv_n.reshape(b, s, 6, NSA_GROUPS, HEAD_DIM).transpose(2, 0, 3, 1, 4)
    k_c, v_c, k_s, v_s, k_w, v_w = kv[0], kv[1], kv[2], kv[3], kv[4], kv[5]
    nc = (s - CMP_LEN) // CMP_STRIDE + 1
    cmp_end = jnp.arange(nc) * CMP_STRIDE + CMP_LEN - 1
    kc = rope(rms_norm(compress(k_c, cmp_pos_k, cmp_k_w1, cmp_k_w2), k_norm_g[0]), cmp_end)
    vc = compress(v_c, cmp_pos_v, cmp_v_w1, cmp_v_w2)
    k_s = rope(rms_norm(k_s, k_norm_g[1]), pos)
    k_w = rope(rms_norm(k_w, k_norm_g[2]), pos)
    ns = s // SEL_BLOCK
    n_sel = min(SEL_TOPN, ns)
    ks_blocks = k_s.reshape(b, NSA_GROUPS, ns, SEL_BLOCK, HEAD_DIM)
    vs_blocks = v_s.reshape(b, NSA_GROUPS, ns, SEL_BLOCK, HEAD_DIM)
    pad = ((0, 0), (0, 0), (WINDOW, 0), (0, 0))
    kw_pad = jnp.pad(k_w, pad)
    vw_pad = jnp.pad(v_w, pad)
    g_nsa = jax.nn.sigmoid(g_n.reshape(b, s, 3, NSA_GROUPS, NSA_HPG).transpose(2, 0, 3, 4, 1))
    c_start = jnp.arange(nc) * CMP_STRIDE
    j_start = jnp.arange(ns) * SEL_BLOCK
    overlap = jnp.clip(jnp.minimum(c_start[:, None] + CMP_LEN, j_start[None, :] + SEL_BLOCK)
                       - jnp.maximum(c_start[:, None], j_start[None, :]), 0).astype(jnp.float32) / CMP_LEN
    bi = jnp.arange(b)[:, None, None, None]
    gi = jnp.arange(NSA_GROUPS)[None, :, None, None]
    blk = jnp.arange(ns)

    sb = qkv_sb.reshape(b, s, 3, SB_HEADS, HEAD_DIM).transpose(2, 0, 3, 1, 4)
    q_sb, k_sb, v_sb = sb[0], sb[1], sb[2]

    def block_fn(bidx):
        t0 = bidx * Q_BLOCK
        t = t0 + jnp.arange(Q_BLOCK)
        qb = lax.dynamic_slice_in_dim(q, t0, Q_BLOCK, axis=3)
        sc = jnp.einsum('bghtd,bgcd->bghtc', qb, kc) * scale
        cmask = cmp_end[None, :] <= t[:, None]
        has_c = (t >= CMP_LEN - 1).astype(jnp.float32)[:, None]
        pc = jax.nn.softmax(jnp.where(cmask, sc, NEG), axis=-1) * has_c
        o_cmp = jnp.einsum('bghtc,bgcd->bghtd', pc, vc)
        imp = jnp.einsum('bghtc,cj->bgtj', pc, overlap)
        cur = t // SEL_BLOCK
        forced = (blk[None, :] == 0) | (blk[None, :] == cur[:, None]) | (blk[None, :] == cur[:, None] - 1)
        valid = blk[None, :] * SEL_BLOCK <= t[:, None]
        score = jnp.where(forced, 1e4, jnp.where(valid, imp, -1e4))
        _, sel = lax.top_k(score, n_sel)
        ks_g = ks_blocks[bi, gi, sel]
        vs_g = vs_blocks[bi, gi, sel]
        ss = jnp.einsum('bghtd,bgtnld->bghtnl', qb, ks_g) * scale
        spos = sel[..., None] * SEL_BLOCK + jnp.arange(SEL_BLOCK)
        smask = spos <= t[None, None, :, None, None]
        ps = jax.nn.softmax(jnp.where(smask[:, :, None], ss, NEG), axis=(-2, -1))
        o_sel = jnp.einsum('bghtnl,bgtnld->bghtd', ps, vs_g)
        kwb = lax.dynamic_slice_in_dim(kw_pad, t0, WINDOW + Q_BLOCK, axis=2)
        vwb = lax.dynamic_slice_in_dim(vw_pad, t0, WINDOW + Q_BLOCK, axis=2)
        wpos = t0 - WINDOW + jnp.arange(WINDOW + Q_BLOCK)
        wmask = (wpos[None, :] >= 0) & (wpos[None, :] <= t[:, None]) & (wpos[None, :] > t[:, None] - WINDOW)
        sw = jnp.einsum('bghtd,bgkd->bghtk', qb, kwb) * scale
        pw = jax.nn.softmax(jnp.where(wmask, sw, NEG), axis=-1)
        o_win = jnp.einsum('bghtk,bgkd->bghtd', pw, vwb)
        gb = lax.dynamic_slice_in_dim(g_nsa, t0, Q_BLOCK, axis=4)[..., None]
        o_nsa = gb[0] * o_cmp + gb[1] * o_sel + gb[2] * o_win
        qsb = lax.dynamic_slice_in_dim(q_sb, t0, Q_BLOCK, axis=2)
        z = jnp.einsum('bhtd,bhsd->bhts', qsb, k_sb) * scale
        m = pos[None, :] < t[:, None]
        l1m = jnp.where(m, jax.nn.log_sigmoid(-z), 0.0)
        after = lax.cumsum(l1m, axis=3, reverse=True) - l1m
        a_w = jnp.where(m, jnp.exp(jax.nn.log_sigmoid(z) + after), 0.0)
        o_sb = jnp.einsum('bhts,bhsd->bhtd', a_w, v_sb)
        return o_nsa, o_sb

    o_nsa_all, o_sb_all = lax.map(block_fn, jnp.arange(s // Q_BLOCK))
    o_nsa = o_nsa_all.transpose(1, 0, 4, 2, 3, 5).reshape(b, s, NSA_W)
    o_sb = o_sb_all.transpose(1, 0, 3, 2, 4).reshape(b, s, SB_W)
    gate_a, gate_b = jnp.split(jax.nn.sigmoid(br_g), 2, axis=-1)
    merged = gate_a * (o_nsa @ w_branch_nsa) + gate_b * (o_sb @ w_branch_sb)
    return merged @ w_out

def peer(xn, wq, subkeys, u, v):
    d = xn.shape[-1]
    tokens = xn.reshape(-1, PEER_CHUNK, d)

    def chunk_fn(xc):
        q = (xc @ wq).reshape(PEER_CHUNK, PEER_HEADS, 2, PEER_QDIM // 2)
        sc = jnp.einsum('thpd,pkd->thpk', q, subkeys)
        sv, si = lax.top_k(sc, PEER_TOPK)
        cand = sv[:, :, 0, :, None] + sv[:, :, 1, None, :]
        cv, ci = lax.top_k(cand.reshape(PEER_CHUNK, PEER_HEADS, PEER_TOPK * PEER_TOPK), PEER_TOPK)
        i1 = jnp.take_along_axis(si[:, :, 0], ci // PEER_TOPK, axis=-1)
        i2 = jnp.take_along_axis(si[:, :, 1], ci % PEER_TOPK, axis=-1)
        e = i1 * PEER_NKEYS + i2
        g = jax.nn.softmax(cv.astype(jnp.float32), axis=-1)
        act = jax.nn.gelu(jnp.einsum('td,thkd->thk', xc, u[e]))
        return jnp.einsum('thk,thkd->td', g * act, v[e])

    return lax.map(chunk_fn, tokens).reshape(xn.shape)

def setup_inputs(seed: int = 0) -> dict:
    key = jax.random.key(seed)
    ks = jax.random.split(key, 20)
    f = jnp.float32
    nrm = lambda k, shape, sc: jax.random.normal(k, shape, f) * sc
    L = DEPTH
    return {
        "x": nrm(ks[0], (BATCH, SEQ, D_MODEL), 1.0),
        "norm1_g": 1.0 + nrm(ks[1], (L, D_MODEL), 0.02),
        "w_in": nrm(ks[2], (L, D_MODEL, IN_WIDTH), D_MODEL ** -0.5),
        "q_norm_g": 1.0 + nrm(ks[3], (L, HEAD_DIM), 0.02),
        "k_norm_g": 1.0 + nrm(ks[4], (L, 3, HEAD_DIM), 0.02),
        "cmp_pos_k": nrm(ks[5], (L, CMP_LEN, HEAD_DIM), 0.1),
        "cmp_pos_v": nrm(ks[6], (L, CMP_LEN, HEAD_DIM), 0.1),
        "cmp_k_w1": nrm(ks[7], (L, CMP_LEN * HEAD_DIM, CMP_HIDDEN), (CMP_LEN * HEAD_DIM) ** -0.5),
        "cmp_k_w2": nrm(ks[8], (L, CMP_HIDDEN, HEAD_DIM), CMP_HIDDEN ** -0.5),
        "cmp_v_w1": nrm(ks[9], (L, CMP_LEN * HEAD_DIM, CMP_HIDDEN), (CMP_LEN * HEAD_DIM) ** -0.5),
        "cmp_v_w2": nrm(ks[10], (L, CMP_HIDDEN, HEAD_DIM), CMP_HIDDEN ** -0.5),
        "w_branch_nsa": nrm(ks[11], (L, NSA_W, D_MODEL), NSA_W ** -0.5),
        "w_branch_sb": nrm(ks[12], (L, SB_W, D_MODEL), SB_W ** -0.5),
        "w_out": nrm(ks[13], (L, D_MODEL, D_MODEL), D_MODEL ** -0.5),
        "norm2_g": 1.0 + nrm(ks[14], (L, D_MODEL), 0.02),
        "peer_w_query": nrm(ks[15], (L, D_MODEL, PEER_HEADS * PEER_QDIM), D_MODEL ** -0.5),
        "peer_subkeys": nrm(ks[16], (L, 2, PEER_NKEYS, PEER_QDIM // 2), (PEER_QDIM // 2) ** -0.5),
        "peer_u": nrm(ks[17], (L, PEER_N_EXPERTS, D_MODEL), D_MODEL ** -0.5),
        "peer_v": nrm(ks[18], (L, PEER_N_EXPERTS, D_MODEL), 0.5),
    }

def reference(x, norm1_g, w_in, q_norm_g, k_norm_g, cmp_pos_k, cmp_pos_v, cmp_k_w1, cmp_k_w2,
              cmp_v_w1, cmp_v_w2, w_branch_nsa, w_branch_sb, w_out, norm2_g, peer_w_query,
              peer_subkeys, peer_u, peer_v):
    h = x.astype(jnp.float32)
    for l in range(DEPTH):
        xn = rms_norm(h, norm1_g[l])
        h = h + token_mixers(xn, w_in[l], q_norm_g[l], k_norm_g[l], cmp_pos_k[l], cmp_pos_v[l],
                             cmp_k_w1[l], cmp_k_w2[l], cmp_v_w1[l], cmp_v_w2[l],
                             w_branch_nsa[l], w_branch_sb[l], w_out[l])
        hn = rms_norm(h, norm2_g[l])
        h = h + peer(hn, peer_w_query[l], peer_subkeys[l], peer_u[l], peer_v[l])
    return h.astype(x.dtype)


_drawn_inputs = setup_inputs


def setup_inputs(seed=0):
    import zlib

    import numpy as np

    out = dict(_drawn_inputs(seed))
    spreads = {}
    factors = {'q_norm_g': 4.612, 'k_norm_g': 5.526, 'cmp_pos_k': 2.995}
    for name, (base, spread) in spreads.items():
        noise = np.random.default_rng([zlib.crc32(name.encode()), seed]).standard_normal(out[name].shape)
        drawn = base * np.exp(spread * noise) if base else spread * noise
        out[name] = __import__('jax').numpy.asarray(drawn.astype(out[name].dtype))
    for name, factor in factors.items():
        out[name] = (out[name] * factor).astype(out[name].dtype)
    return out
```

```python
from contextlib import ExitStack

import numpy as np
import concourse.bass as bass
from concourse import mybir

F32 = mybir.dt.float32
F32R = mybir.dt.float32r
U32 = mybir.dt.uint32
ALU = mybir.AluOpType
ACT = mybir.ActivationFunctionType
AXX = mybir.AxisListType.X

P = 128
D = 1024
T = 256
TB = T // P
KT = D // P
HD = 64
NH = 8
NG = 2
NC_ = (T - 32) // 16 + 1
CL = 32
CH = 256
TOPK = 16
NK = 128
NBLK = 128
EPS = 1e-6
NEG = -1e30
SCALE = 0.125

T_KC, T_VC = 0, 1
T_W1K, T_W1V = 2, 6
T_KV, T_Q = 10, 14
T_QSB, T_KSB = 18, 22
T_VSB = 26
T_GATE = 30
T_BR = 46
T_WQ = 62
N_PRE = 78
N_ALL = N_PRE + 2 * NBLK
RING = 4
UNROLL = 4
TOPK_AT, TOPK_CAND, TOPK_IDX, TOPK_END = 0, 8, 16, 24

PARAMS = dict(g1=8, g2=8, qg=64, kgc=64, kgs=128, posk=16, posv=16, w2k=128, w2v=128, subk=256, gw=192)
CONSTS = dict(cos=128, sin=128, cosc=64, sinc=64, tri=128, ones=128, mask=384 + 2 * NC_, msb=384, hasc=1)
KEPT = dict(ident=128, iota=128, iota16=16)


def offsets(table):
    out, at = {}, 0
    for k, n in table.items():
        out[k] = (at, n)
        at += n
    return out, at


PAR, NPAR = offsets(PARAMS)
CST, NCST = offsets(CONSTS)
KEP, NKEP = offsets(KEPT)


def build(nc, x_d, wpre_d, u_d, v_d, par_d, cst_d, kep_d, out_d):
    with ExitStack() as ctx:
        def sb(name, shape, dt=F32):
            return ctx.enter_context(nc.sbuf_tensor(name, shape, dt))

        def sem(name):
            return ctx.enter_context(nc.semaphore(name))

        bank = [ctx.enter_context(nc.psum_tensor(f"bank{i}", [P, 512], F32)) for i in range(8)]

        big = sb("big", [P, NBLK * T])
        raw = sb("raw", [P, RING, 1024])
        hi = sb("hi", [P, 2, 1024], F32R)
        lo = sb("lo", [P, 2, 1024], F32R)
        xhi = sb("xhi", [P, 8, T], F32R)
        xlo = sb("xlo", [P, 8, T], F32R)
        auxh = sb("auxh", [P, 960], F32R)
        auxl = sb("auxl", [P, 960], F32R)
        gwh = sb("gwh", [P, 192], F32R)
        gwl = sb("gwl", [P, 192], F32R)
        h = sb("h", [P, TB, D])
        kep = sb("kep", [P, NKEP])
        eT = sb("eT", [P, 3, T])
        oneA = sb("oneA", [P, 2, 4, P])
        oneB = sb("oneB", [P, 2, 4, P])

        at = [0]

        def carve(n, start=None):
            if start is not None:
                at[0] = start
            a = at[0]
            at[0] += n
            assert at[0] <= NBLK * T
            return big[:, a:a + n]

        par = carve(NPAR)
        cst = carve(NCST)

        def pv(k):
            a, n = PAR[k]
            return par[:, a:a + n]

        def cv_(k):
            a, n = CST[k]
            return cst[:, a:a + n]

        ident = kep[:, KEP["ident"][0]:KEP["ident"][0] + P]
        iota = kep[:, KEP["iota"][0]:KEP["iota"][0] + P]
        iota16 = kep[:, KEP["iota16"][0]:KEP["iota16"][0] + 16]

        xs = carve(TB * D).rearrange("p (b d) -> p b d", b=TB)
        st = carve(64)
        gcq, gsq = (carve(128).rearrange("p (b d) -> p b d", b=2) for _ in range(2))
        gck, gsk = (carve(256).rearrange("p (b s d) -> p b s d", b=2, s=2) for _ in range(2))
        gcc, gsc = carve(64), carve(64)
        nrm_n, nrm_a, nrm_b, nrm_q, nrm_c = carve(512), carve(512), carve(512), carve(512), carve(128)
        qrot = carve(1024).rearrange("p (b c) -> p b c", b=2)
        krdup = carve(1024).rearrange("p (b s c) -> p b s c", b=2, s=4)
        kcd = carve(256)
        vsw = carve(512).rearrange("p (b c) -> p b c", b=2)
        vcs = carve(128)
        qT = carve(1024).rearrange("p (a t) -> p a t", a=4)
        kT = carve(1024).rearrange("p (a t) -> p a t", a=4)
        kcT = carve(32).rearrange("p (g c) -> p g c", g=2)
        qsbT = carve(1024).rearrange("p (a t) -> p a t", a=4)
        ksbT = carve(1024).rearrange("p (a t) -> p a t", a=4)
        vsb = carve(1024).rearrange("p (b c) -> p b c", b=2)
        ghid = carve(120)
        stok = carve(960)
        gsig = carve(48)
        ggate = carve(48).rearrange("p (h c) -> p h c", c=6)
        sm = carve(2 * 828).rearrange("p (q c) -> p q c", q=2)
        att = carve(2 * 32).rearrange("p (q c) -> p q c", q=2)
        pT = carve(1024)
        sbt = carve(5 * 384).rearrange("p (k c) -> p k c", k=5)
        gates = carve(4096).rearrange("p (a t) -> p a t", a=16)
        oT = carve(2048).rearrange("p (a t) -> p a t", a=8)
        mrg = carve(2 * 768).rearrange("p (q c) -> p q c", q=2)
        qst = carve(1024).rearrange("p (q c) -> p q c", q=2)
        sc = carve(4096, start=24576)
        tkv, tki = carve(512), carve(512)
        cval = carve(256)
        caf, cbf = carve(256), carve(256)
        i1f, i2f = carve(256), carve(256)
        gwt = carve(256)
        stg, stg2 = carve(256), carve(256)
        stv, sti_ = carve(16), carve(16)
        sti = sti_.bitcast(U32)
        sta = carve(16).bitcast(U32)
        smx = carve(32)
        eqt = carve(256)
        assert at[0] <= NBLK * T

        loaded = [sem(f"tile_loaded{i}") for i in range(RING)]
        small_in = sem("small_in")
        x_in = sem("x_in")
        hi_done = sem("hi_done")
        lo_done = sem("lo_done")
        tile_used = sem("tile_used")
        dve_step = sem("dve_step")
        act_step = sem("act_step")
        N = {}

        def S(name):
            if name not in N:
                N[name] = sem(name)
            return N[name]

        block = ctx.enter_context(nc.Block())

        @block.sync
        def _(sp):
            sp.dma_start(cst, cst_d).then_inc(small_in, 16)
            sp.dma_start(par, par_d).then_inc(small_in, 16)
            sp.dma_start(kep[:, :], kep_d).then_inc(small_in, 16)

            def load(slot, src):
                sp.dma_start(raw[:, slot, :], src).then_inc(loaded[slot], 16)

            for n in range(RING):
                load(n, wpre_d[n])
            with sp.Fori(1, N_PRE // RING) as i:
                for j in range(RING):
                    sp.wait_ge(lo_done, i * RING + (j - RING + 1))
                    load(j, wpre_d[bass.ds(i * RING + j, 1)].rearrange("a p c -> (a p) c"))
            for n in range(N_PRE // RING * RING, N_PRE):
                sp.wait_ge(lo_done, n - RING + 1)
                load(n % RING, wpre_d[n])
            for src, first in ((u_d, N_PRE), (v_d, N_PRE + NBLK)):
                with sp.Fori(0, NBLK // RING) as i:
                    for j in range(RING):
                        sp.wait_ge(lo_done, i * RING + (first + j - RING + 1))
                        load((first + j) % RING, src[bass.ds(i * RING + j, 1)].rearrange("a p c -> (a p) c"))
            for b in range(TB):
                sp.wait_ge(S("out_ready"), 2 * (b + 1))
                sp.dma_start(out_d[b * P:(b + 1) * P, :], h[:, b, :]).then_inc(S("stored"), 16)
            sp.wait_ge(S("stored"), 16 * TB)

        @block.tensor
        def _(pe):
            def need(n):
                pe.wait_ge(hi_done, n + 1)
                pe.wait_ge(lo_done, n + 1)

            def tposed(n, out):
                need(n)
                s = n % 2
                for k in range(KT):
                    wh, wl = hi[:, s, k * P:(k + 1) * P], lo[:, s, k * P:(k + 1) * P]
                    pe.matmul(out, wh, xhi[:, k, :], start=(k == 0), stop=False)
                    pe.matmul(out, wh, xlo[:, k, :], start=False, stop=False)
                    m = pe.matmul(out, wl, xhi[:, k, :], start=False, stop=(k == KT - 1))
                m.then_inc(tile_used, 1)

            def normal(n, i, outs):
                need(n)
                s = n % 2
                for b in range(TB):
                    for kk in range(2):
                        k = 2 * i + kk
                        wh, wl = hi[:, s, kk * 512:kk * 512 + 512], lo[:, s, kk * 512:kk * 512 + 512]
                        xh, xl = xhi[:, k, b * P:(b + 1) * P], xlo[:, k, b * P:(b + 1) * P]
                        pe.matmul(outs[b], xh, wh, start=(k == 0), stop=False)
                        pe.matmul(outs[b], xh, wl, start=False, stop=False)
                        m = pe.matmul(outs[b], xl, wh, start=False, stop=(k == KT - 1))
                m.then_inc(tile_used, 1)

            def transpose_x(which):
                for k in range(KT):
                    for b in range(TB):
                        m = pe.transpose(bank[4 + k // 2][:, (k % 2) * T + b * P:(k % 2) * T + (b + 1) * P],
                                         xs[:, b, k * P:(k + 1) * P], ident)
                    if k % 2:
                        m.then_inc(S("xT_ready"), 1)

            pe.wait_ge(small_in, 48)
            pe.wait_ge(S("xs_ready"), 1)
            transpose_x(0)
            pe.wait_ge(S("xlo_ready"), KT)
            tposed(T_KC, bank[0][:, 0:T])
            tposed(T_VC, bank[3][:, 0:T])
            m = None
            for w, first in ((0, T_W1K), (1, T_W1V)):
                if w == 0:
                    pe.wait_ge(S("tok_split"), 1)
                for i in range(4):
                    n = first + i
                    need(n)
                    s = n % 2
                    for hb in range(2):
                        out = bank[1 + hb][:, w * 32:w * 32 + 30]
                        for jj in range(4):
                            j = 4 * i + jj
                            c0 = jj * 256 + hb * P
                            wh, wl = hi[:, s, c0:c0 + P], lo[:, s, c0:c0 + P]
                            a = w * 480 + j * 30
                            pe.matmul(out, wh, auxh[:, a:a + 30], start=(j == 0), stop=False)
                            pe.matmul(out, wh, auxl[:, a:a + 30], start=False, stop=False)
                            m = pe.matmul(out, wl, auxh[:, a:a + 30], start=False, stop=(j == 15))
                    m.then_inc(tile_used, 1)
            for i in range(4):
                normal(T_KV + i, i, [bank[6][:, :], bank[7][:, :]])
            pe.wait_ge(S("ghid"), 1)
            for w in range(2):
                w2 = pv("w2k" if w == 0 else "w2v")
                for g in range(NG):
                    for hb in range(2):
                        a = (w * 2 + hb) * 30 + g * NC_
                        m = pe.matmul(bank[1][0:NC_, P + (w * 2 + g) * HD:P + (w * 2 + g + 1) * HD],
                                      ghid[:, a:a + NC_], w2[:, hb * HD:(hb + 1) * HD],
                                      start=(hb == 0), stop=(hb == 1))
            m.then_inc(S("cmp_ready"), 1)
            pe.wait_ge(S("gw_split"), 1)
            for b in range(TB):
                out = bank[2][:, 128 + 32 * b:128 + 32 * b + 24]
                for k in range(KT):
                    xh, xl = xhi[:, k, b * P:(b + 1) * P], xlo[:, k, b * P:(b + 1) * P]
                    pe.matmul(out, xh, gwh[:, 24 * k:24 * k + 24], start=(k == 0), stop=False)
                    pe.matmul(out, xh, gwl[:, 24 * k:24 * k + 24], start=False, stop=False)
                    m = pe.matmul(out, xl, gwh[:, 24 * k:24 * k + 24], start=False, stop=(k == KT - 1))
            m.then_inc(S("gn_ready"), 1)
            for i in range(4):
                normal(T_Q + i, i, [bank[4][:, :], bank[5][:, :]])
            for i in range(4):
                if i == 0:
                    pe.wait_ge(S("tok_split"), 1)
                if i >= 2:
                    pe.wait_ge(S("qksb_out"), i - 1)
                b = bank[(0, 3)[i % 2]]
                tposed(T_QSB + 2 * i, b[:, 0:T])
                tposed(T_QSB + 2 * i + 1, b[:, T:2 * T])
            pe.wait_ge(S("krot"), 1)
            for s in range(4):
                for b in range(TB):
                    m = pe.transpose(bank[6 + s // 2][:, (s % 2) * T + b * P:(s % 2) * T + (b + 1) * P],
                                     krdup[:, b, s, :], ident)
            m.then_inc(S("kT_ready"), 1)
            pe.wait_ge(S("kcrot"), 1)
            pe.wait_ge(S("vc_out"), 1)
            for g in range(NG):
                m = pe.transpose(bank[1][:, 400 + 16 * g:400 + 16 * g + NC_],
                                 kcd[0:NC_, g * P:(g + 1) * P], ident[0:NC_, 0:NC_])
            m.then_inc(S("kcT_ready"), 1)
            pe.wait_ge(S("gates_n"), 1)
            pe.wait_ge(S("kcT_out"), 1)
            pe.wait_ge(S("vc_out"), 1)
            for i in range(4):
                normal(T_VSB + i, i, [bank[2][:, :], bank[1][:, :]])
            pe.wait_ge(S("qrot"), 1)
            for a in range(4):
                for b in range(TB):
                    m = pe.transpose(bank[4 + a // 2][:, (a % 2) * T + b * P:(a % 2) * T + (b + 1) * P],
                                     qrot[:, b, a * P:(a + 1) * P], ident)
            m.then_inc(S("qT_ready"), 1)

            def scores(hh):
                r0, a, g = 64 * (hh % 2), hh // 2, hh // 4
                r = slice(r0, r0 + HD)
                if hh == 0:
                    pe.wait_ge(S("qkT_out"), 3)
                else:
                    pe.wait_ge(S("masked"), hh)
                for br, o in ((0, bank[4]), (1, bank[5])):
                    k = kT[r, 2 * br + g, :]
                    pe.matmul(o[:, 0:P], qT[r, a, 0:P], k[:, 0:P], start=True, stop=True)
                    m = pe.matmul(o[:, P:384], qT[r, a, P:T], k[:, 0:T], start=True, stop=True)
                for b in range(TB):
                    m = pe.matmul(bank[4][:, 384 + NC_ * b:384 + NC_ * (b + 1)], qT[r, a, b * P:(b + 1) * P],
                                  kcT[r, g, 0:NC_], start=True, stop=True)
                m.then_inc(S("scores"), 1)

            def sticks(hh):
                r0, a = 64 * (hh % 2), hh // 2
                r = slice(r0, r0 + HD)
                if hh == 0:
                    pe.wait_ge(S("qksb_out"), 4)
                    pe.wait_ge(S("vsb_out"), 1)
                else:
                    pe.wait_ge(S("x_ready"), hh)
                pe.matmul(bank[2][:, 0:T], ksbT[r, a, 0:P], qsbT[r, a, :], start=True, stop=True)
                m = pe.matmul(bank[2][:, T:384], ksbT[r, a, P:T], qsbT[r, a, P:T], start=True, stop=True)
                m.then_inc(S("z_ready"), 1)

            def gate_tile(g):
                if g >= 2:
                    pe.wait_ge(S("gate_exp"), g - 1)
                else:
                    pe.wait_ge(S("vsb_out"), 2)
                tposed(T_GATE + g, bank[g % 2][:, 0:T])

            scores(0)
            sticks(0)
            for hh in range(NH):
                r0, a, g = 64 * (hh % 2), hh // 2, hh // 4
                gate_tile(2 * hh)
                pe.wait_ge(S("probs"), hh + 1)
                if hh == 0:
                    pe.wait_ge(S("qksb_out"), 4)
                else:
                    pe.wait_ge(S("pT_out"), 2 * hh)
                    pe.wait_ge(S("cmpT_out"), hh)
                    pe.wait_ge(S("osb_out"), hh)
                q = hh % 2
                for br in range(2):
                    for c in range(3):
                        m = pe.transpose(bank[6 + br][:, c * P:(c + 1) * P],
                                         sm[:, q, 414 * br + c * P:414 * br + (c + 1) * P], ident)
                m.then_inc(S("pT"), 1)
                for b in range(TB):
                    m = pe.transpose(bank[3][0:NC_, b * P:(b + 1) * P],
                                     sm[:, q, 384 + NC_ * b:384 + NC_ * (b + 1)], ident)
                m.then_inc(S("cmpT"), 1)
                pe.wait_ge(S("l_masked"), hh + 1)
                L = sbt[:, 1, :]
                pe.matmul(bank[2][:, 0:T], cv_("tri"), L[:, 0:T], start=True, stop=False)
                pe.matmul(bank[2][:, P:T], cv_("ones"), L[:, T:384], start=False, stop=True)
                m = pe.matmul(bank[2][:, T:384], cv_("tri"), L[:, T:384], start=True, stop=True)
                m.then_inc(S("after"), 1)
                gate_tile(2 * hh + 1)
                if hh + 1 < NH:
                    scores(hh + 1)
                    sticks(hh + 1)
                pe.wait_ge(S("pT_out"), 2 * hh + 2)
                pe.wait_ge(S("cmpT_out"), hh + 1)
                o = bank[3][r0:r0 + HD, 0:T]
                for br in range(2):
                    vcol = slice((2 * br + g) * HD, (2 * br + g + 1) * HD)
                    p0 = 384 * br
                    pe.matmul(o, vsw[:, 0, vcol], pT[:, p0:p0 + T], start=(br == 0), stop=False)
                    pe.matmul(o[:, P:T], vsw[:, 1, vcol], pT[:, p0 + T:p0 + 384], start=False, stop=False)
                m = pe.matmul(o, vcs[0:NC_, g * HD:(g + 1) * HD], pT[0:NC_, 768:1024], start=False, stop=True)
                m.then_inc(S("onsa"), 1)
                pe.wait_ge(S("a_ready"), hh + 1)
                o = bank[3][r0:r0 + HD, T:2 * T]
                vcol = slice(hh * HD, (hh + 1) * HD)
                pe.matmul(o, vsb[:, 0, vcol], sbt[:, 4, 0:T], start=True, stop=False)
                m = pe.matmul(o[:, P:T], vsb[:, 1, vcol], sbt[:, 4, T:384], start=False, stop=True)
                m.then_inc(S("osb"), 1)

            pe.wait_ge(S("oT_split"), 1)
            pe.wait_ge(S("gate_exp"), 16)
            for i in range(8):
                n = T_BR + 2 * i
                if i == 0:
                    pe.wait_ge(S("masked"), NH)
                if i >= 2:
                    pe.wait_ge(S("mrg_read"), i - 1)
                need(n)
                s = n % 2
                for br in range(2):
                    out = bank[4 + i % 2][:, br * T:(br + 1) * T]
                    for k in range(4):
                        c0 = (br * 4 + k) * P
                        wh, wl = hi[:, s, c0:c0 + P], lo[:, s, c0:c0 + P]
                        pe.matmul(out, wh, xhi[:, 4 * br + k, :], start=(k == 0), stop=False)
                        pe.matmul(out, wh, xlo[:, 4 * br + k, :], start=False, stop=False)
                        m = pe.matmul(out, wl, xhi[:, 4 * br + k, :], start=False, stop=(k == 3))
                m.then_inc(tile_used, 1)
                n += 1
                need(n)
                pe.wait_ge(S("mrg_split"), i + 1)
                if i == 0:
                    pe.wait_ge(S("osb_out"), NH)
                s = n % 2
                for b in range(TB):
                    c0 = (i % 2) * T + b * P
                    mh, ml = auxh[:, c0:c0 + P], auxl[:, c0:c0 + P]
                    for st_, (a_, w_) in enumerate(((mh, hi), (mh, lo), (ml, hi))):
                        for f in range(2):
                            m = pe.matmul(bank[2 * b + f][:, :], a_, w_[:, s, f * 512:(f + 1) * 512],
                                          start=(i == 0 and st_ == 0), stop=(i == 7 and st_ == 2))
                m.then_inc(tile_used, 1)
            def key_scores(j):
                pe.wait_ge(S("bank45_read"), j + 1)
                if j >= 2:
                    pe.wait_ge(S("sc_out"), j - 1)
                for p_ in range(2):
                    for b in range(TB):
                        c0 = p_ * T + b * P
                        m = pe.matmul(bank[6 + j % 2][:, c0:c0 + P], qst[:, j % 2, c0:c0 + P],
                                      pv("subk")[:, p_ * P:(p_ + 1) * P], start=True, stop=True)
                m.then_inc(S("key_scores"), 1)

            pe.wait_ge(S("xs_ready"), 2)
            pe.wait_ge(S("mrg_read"), 8)
            transpose_x(1)
            pe.wait_ge(S("xlo_ready"), 2 * KT)
            for i in range(NH):
                if i >= 2:
                    pe.wait_ge(S("bank45_read"), i - 1)
                for p_ in range(2):
                    tposed(T_WQ + 2 * i + p_, bank[4 + i % 2][:, p_ * T:(p_ + 1) * T])
                if i >= 1:
                    key_scores(i - 1)
            key_scores(NH - 1)

            def u_tiles(i):
                for j in range(UNROLL):
                    n0 = N_PRE + j
                    if j % 2 == 0:
                        pe.wait_ge(S("bank45_read"), i * 2 + (j // 2 + NH - 1))
                    pe.wait_ge(hi_done, i * UNROLL + (n0 + 1))
                    pe.wait_ge(lo_done, i * UNROLL + (n0 + 1))
                    s = n0 % 2
                    out = bank[4 + j // 2][:, (j % 2) * T:(j % 2 + 1) * T]
                    for k in range(KT):
                        wh, wl = hi[:, s, k * P:(k + 1) * P], lo[:, s, k * P:(k + 1) * P]
                        pe.matmul(out, wh, xhi[:, k, :], start=(k == 0), stop=False)
                        pe.matmul(out, wh, xlo[:, k, :], start=False, stop=False)
                        m = pe.matmul(out, wl, xhi[:, k, :], start=False, stop=(k == KT - 1))
                    m.then_inc(tile_used, 1)

            with pe.Fori(0, TOPK_END) as i:
                u_tiles(i)
            pe.wait_ge(S("router"), 1)
            for w, src in enumerate((i1f, i2f, gwt)):
                for b in range(TB):
                    m = pe.transpose(bank[6 + w // 2][:, (w % 2) * T + b * P:(w % 2) * T + (b + 1) * P],
                                     src[:, b * P:(b + 1) * P], ident)
            m.then_inc(S("routerT"), 1)
            with pe.Fori(TOPK_END, NBLK // UNROLL) as i:
                u_tiles(i)

            pe.wait_ge(S("bank67_read"), 2)
            with pe.Fori(0, T // 8) as i:
                for q in range(2):
                    pe.wait_ge(S("oneA_ready"), i * 2 + (q + 1))
                    pe.wait_ge(S("oneB_ready"), i * 2 + (q + 1))
                    pe.wait_ge(S("bank67_read"), i * 2 + (q + 1))
                    for t in range(4):
                        m = pe.matmul(bank[6 + q][:, t * P:(t + 1) * P], oneB[:, q, t, :], oneA[:, q, t, :],
                                      start=True, stop=True)
                    m.then_inc(S("g_ready"), 1)

            def v_tiles(i, first=False, last=False):
                for j in range(UNROLL):
                    n0 = N_PRE + NBLK + j
                    s = n0 % 2
                    pe.wait_ge(hi_done, i * UNROLL + (n0 + 1))
                    pe.wait_ge(lo_done, i * UNROLL + (n0 + 1))
                    pe.wait_ge(S("wlo_done"), i * UNROLL + (j + 1))
                    for b in range(TB):
                        c0 = (j % 2) * T + b * P
                        wh, wl = auxh[:, c0:c0 + P], auxl[:, c0:c0 + P]
                        for st_, (a_, w_) in enumerate(((wh, hi), (wh, lo), (wl, hi))):
                            for f in range(2):
                                m = pe.matmul(bank[2 * b + f][:, :], a_, w_[:, s, f * 512:(f + 1) * 512],
                                              start=(first and j == 0 and st_ == 0),
                                              stop=(last and j == UNROLL - 1 and st_ == 2),
                                              skip_group_check=True)
                    m.then_inc(tile_used, 1)

            v_tiles(0, first=True)
            with pe.Fori(1, NBLK // UNROLL - 1) as i:
                v_tiles(i)
            v_tiles(NBLK // UNROLL - 1, last=True)

        @block.scalar
        def _(act):
            own = [0]

            def link(ins):
                own[0] += 1
                ins.then_inc(act_step, 1)
                act.wait_ge(act_step, own[0])

            act.dma_start(h[:, :, :], x_d.rearrange("(b p) d -> p b d", p=P)).then_inc(x_in, 16)

            def split_hi(n):
                act.wait_ge(loaded[n % RING], 16 * (n // RING + 1))
                if n >= 2:
                    act.wait_ge(tile_used, n - 1)
                act.activation(hi[:, n % 2, :], raw[:, n % RING, :], ACT.Copy).then_inc(hi_done, 1)

            def squares(b, first):
                act.activation(xs[:, b, :], h[:, b, :], ACT.Square, accum_out=st[:, b:b + 1]).then_inc(S("sq"), 1)

            def rstd(u, v):
                act.wait_ge(S("var"), u)
                link(act.activation(v, v, ACT.Ln))
                act.activation(v, v, ACT.Exp, scale=-0.5).then_inc(S("rs"), 1)

            def x_hi(k, which):
                act.wait_ge(S("xT_ready"), (which * KT + k) // 2 + 1)
                act.activation(xhi[:, k, :], bank[4 + k // 2][:, (k % 2) * T:(k % 2 + 1) * T], ACT.Copy,
                               scale=pv("g1" if which == 0 else "g2")[:, k:k + 1]).then_inc(S("xhi_ready"), 1)

            act.wait_ge(x_in, 16)
            squares(0, True)
            squares(1, True)
            act.wait_ge(small_in, 48)
            act.activation(gwh[:, :], pv("gw"), ACT.Copy).then_inc(S("gw_hi"), 1)
            split_hi(0)
            rstd(1, st[:, 8:10])
            split_hi(1)
            for k in range(KT):
                x_hi(k, 0)
            split_hi(2)
            split_hi(3)
            act.wait_ge(S("tok"), 1)
            act.activation(auxh[:, :], stok, ACT.Copy).then_inc(S("tok_hi"), 1)
            for n in range(4, 12):
                split_hi(n)
            act.wait_ge(tile_used, T_W1V + 4)
            for w in range(2):
                for hb in range(2):
                    a = (w * 2 + hb) * 30
                    m = act.activation(ghid[:, a:a + 30], bank[1 + hb][:, w * 32:w * 32 + 30], ACT.Gelu_apprx_tanh)
            m.then_inc(S("ghid"), 1)
            for n in range(12, 16):
                split_hi(n)
            for b in range(TB):
                m = act.activation(nrm_a[:, b * T:(b + 1) * T], bank[6 + b][:, 0:T], ACT.Square)
            m.then_inc(S("sqk"), 1)
            for b in range(TB):
                m = act.activation(vsw[:, b, :], bank[6 + b][:, T:512], ACT.Copy)
            m.then_inc(S("vsw"), 1)
            act.wait_ge(S("cmp_ready"), 1)
            act.activation(nrm_c[0:NC_, :], bank[1][0:NC_, P:2 * P], ACT.Square).then_inc(S("sqk"), 1)
            act.activation(vcs[0:NC_, :], bank[1][0:NC_, 2 * P:3 * P], ACT.Copy).then_inc(S("vc_out"), 1)
            act.wait_ge(S("gn_ready"), 1)
            act.activation(gsig.rearrange("p (b c) -> p b c", b=2),
                           bank[2][:, P:P + 64].rearrange("p (b c) -> p b c", b=2)[:, :, 0:24],
                           ACT.Exp, scale=-1.0).then_inc(S("gn_exp"), 1)
            split_hi(16)
            rstd(2, st[:, 16:24])
            rstd(3, st[0:NC_, 24:26])
            for n in range(17, 20):
                split_hi(n)
            act.wait_ge(S("k_normed"), 1)
            for b in range(TB):
                m = act.activation(nrm_a[:, 0:512] if b == 0 else nrm_q, bank[4 + b][:, :], ACT.Square)
            m.then_inc(S("sqk"), 1)
            split_hi(20)
            split_hi(21)
            rstd(4, st[:, 32:48])

            def qksb_out(i):
                act.wait_ge(tile_used, T_QSB + 2 * i + 2)
                dst = (qsbT if i < 2 else ksbT)[:, 2 * (i % 2):2 * (i % 2) + 2, :]
                act.activation(dst, bank[(0, 3)[i % 2]][:, :].rearrange("p (a t) -> p a t", a=2), ACT.Copy,
                               scale=SCALE if i < 2 else 1.0).then_inc(S("qksb_out"), 1)

            qksb_out(0)
            split_hi(22)
            split_hi(23)
            qksb_out(1)
            split_hi(24)
            split_hi(25)
            qksb_out(2)
            split_hi(26)
            split_hi(27)
            qksb_out(3)
            act.wait_ge(S("kT_ready"), 1)
            for s in range(2):
                m = act.activation(kT[:, 2 * s:2 * s + 2, :], bank[6 + s][:, :].rearrange("p (a t) -> p a t", a=2), ACT.Copy)
            m.then_inc(S("qkT_out"), 1)
            act.wait_ge(S("kcT_ready"), 1)
            act.activation(kcT[:, :, 0:NC_], bank[1][:, 400:432].rearrange("p (g c) -> p g c", g=2)[:, :, 0:NC_],
                           ACT.Copy).then_inc(S("kcT_out"), 1)
            for n in range(28, 32):
                split_hi(n)
            act.wait_ge(tile_used, T_VSB + 4)
            act.activation(vsb[:, 0, :], bank[2][:, :], ACT.Copy).then_inc(S("vsb_out"), 1)
            act.activation(vsb[:, 1, :], bank[1][:, :], ACT.Copy).then_inc(S("vsb_out"), 1)
            act.wait_ge(S("qT_ready"), 1)
            for s in range(2):
                act.activation(qT[:, 2 * s:2 * s + 2, :], bank[4 + s][:, :].rearrange("p (a t) -> p a t", a=2),
                               ACT.Copy).then_inc(S("qkT_out"), 1)

            def softplus(hh):
                act.wait_ge(S("z_ready"), hh + 1)
                if hh:
                    act.wait_ge(S("z_read"), hh)
                sp_ = sbt[:, 2, :]
                link(act.activation(sp_, bank[2][:, 0:384], ACT.Abs))
                link(act.activation(sp_, sp_, ACT.Exp, scale=-1.0))
                act.activation(sp_, sp_, ACT.Ln, bias=1.0).then_inc(S("softplus"), 1)

            def gate_exp(g):
                act.wait_ge(tile_used, T_GATE + g + 1)
                act.activation(gates[:, g, :], bank[g % 2][:, 0:T], ACT.Exp,
                               scale=-1.0).then_inc(S("gate_exp"), 1)

            softplus(0)
            for hh in range(NH):
                q, r0, a = hh % 2, 64 * (hh % 2), hh // 2
                act.wait_ge(S("negmax"), hh + 1)
                for c, (c0, w_) in enumerate(((0, P), (P, T), (414, P), (414 + P, T), (384, NC_), (384 + NC_, NC_))):
                    x_ = sm[:, q, c0:c0 + w_]
                    m = act.activation(x_, x_, ACT.Exp, bias=att[:, q, 6 + c:7 + c], scale=SCALE,
                                       accum_out=att[:, q, 12 + c:13 + c])
                m.then_inc(S("exped"), 1)
                split_hi(T_GATE + 2 * hh + 2)
                act.wait_ge(S("pT"), hh + 1)
                if hh:
                    act.wait_ge(S("onsa"), hh)
                for br in range(2):
                    act.activation(pT[:, 384 * br:384 * (br + 1)], bank[6 + br][:, 0:384],
                                   ACT.Copy).then_inc(S("pT_out"), 1)
                act.wait_ge(S("x_ready"), hh + 1)
                act.activation(sbt[:, 0, :], sbt[:, 0, :], ACT.Exp).then_inc(S("x_exp"), 1)
                gate_exp(2 * hh)
                if hh + 1 < NH:
                    softplus(hh + 1)
                split_hi(T_GATE + 2 * hh + 3)
                gate_exp(2 * hh + 1)
                act.wait_ge(S("osb"), hh + 1)
                act.activation(oT.rearrange("p (k a) t -> p k a t", k=2)[r0:r0 + HD, :, a, :],
                               bank[3][r0:r0 + HD, :].rearrange("p (k t) -> p k t", k=2), ACT.Copy).then_inc(S("osb_out"), 1)
            act.wait_ge(S("osb_out"), NH)
            act.wait_ge(tile_used, T_GATE + 16)
            act.activation(xhi[:, :, :], oT, ACT.Copy).then_inc(S("oT_hi"), 1)
            for i in range(8):
                act.wait_ge(S("merged"), i + 1)
                if i >= 2:
                    act.wait_ge(tile_used, T_BR + 2 * i - 2)
                act.activation(auxh[:, (i % 2) * T:(i % 2 + 1) * T], mrg[:, i % 2, 512:768],
                               ACT.Copy).then_inc(S("mrg_hi"), 1)
                split_hi(T_BR + 2 * i + 2)
                split_hi(T_BR + 2 * i + 3)
            for b in range(TB):
                act.wait_ge(S("h_ready"), b + 1)
                squares(b, False)
            rstd(5, st[:, 8:10])
            for k in range(KT):
                x_hi(k, 1)
            for i in range(NH):
                split_hi(T_WQ + 2 * i + 2)
                split_hi(T_WQ + 2 * i + 3)
                if i >= 2:
                    act.wait_ge(S("key_scores"), i - 1)
                act.activation(qst[:, i % 2, :], bank[4 + i % 2][:, :], ACT.Copy).then_inc(S("bank45_read"), 1)

            def loop_hi(i, j, base):
                n = base + j
                act.wait_ge(loaded[n % RING], i * 16 + 16 * (n // RING + 1))
                act.wait_ge(tile_used, i * UNROLL + (n - 1))
                act.activation(hi[:, n % 2, :], raw[:, n % RING, :], ACT.Copy).then_inc(hi_done, 1)

            def u_step(i):
                for pair in range(2):
                    loop_hi(i, 2 * pair + 2, N_PRE)
                    loop_hi(i, 2 * pair + 3, N_PRE)
                    act.wait_ge(tile_used, i * UNROLL + (N_PRE + 2 * pair + 2))
                    act.activation(big[:, bass.ds(i * (UNROLL * T) + pair * 512, 512)], bank[4 + pair][:, :],
                                   ACT.Gelu_apprx_tanh).then_inc(S("bank45_read"), 1)

            with act.Fori(0, TOPK_END) as i:
                u_step(i)
            act.wait_ge(S("router_d"), 1)
            act.activation(gwt, gwt, ACT.Exp).then_inc(S("router_exp"), 1)
            act.wait_ge(S("bank67_read"), 2)
            with act.Fori(TOPK_END, NBLK // UNROLL) as i:
                u_step(i)

            with act.Fori(0, T // 8) as i:
                for q in range(2):
                    act.wait_ge(S("dist"), i * 2 + (q + 1))
                    act.activation(oneB[:, q, :, :], oneB[:, q, :, :], ACT.Square).then_inc(S("dist_sq"), 1)
                    act.wait_ge(S("dist_sq"), i * 2 + (q + 1))
                    act.activation(oneB[:, q, :, :], oneB[:, q, :, :], ACT.Relu, bias=1.0,
                                   scale=-1.0).then_inc(S("oneB_ready"), 1)

            V0 = N_PRE + NBLK

            def w_hi(i, j):
                act.activation(auxh[:, (j % 2) * T:(j % 2 + 1) * T], big[:, bass.ds(i * (UNROLL * T) + j * T, T)],
                               ACT.Copy).then_inc(S("whi_done"), 1)

            act.wait_ge(S("bank67_read"), 2 + T // 4)
            act.activation(auxh[:, 0:T], big[:, 0:T], ACT.Copy).then_inc(S("whi_done"), 1)
            act.activation(auxh[:, T:2 * T], big[:, T:2 * T], ACT.Copy).then_inc(S("whi_done"), 1)
            with act.Fori(0, NBLK // UNROLL - 1) as i:
                for j in range(UNROLL):
                    loop_hi(i, j + 2, V0)
                    w_hi(i, j + 2)
            for b in (NBLK - 2, NBLK - 1):
                split_hi(V0 + b)
                act.activation(auxh[:, (b % 2) * T:(b % 2 + 1) * T], big[:, b * T:(b + 1) * T],
                               ACT.Copy).then_inc(S("whi_done"), 1)

        @block.vector
        def _(dve):
            own = [0]

            def link(ins):
                own[0] += 1
                ins.then_inc(dve_step, 1)
                dve.wait_ge(dve_step, own[0])

            def split_lo(n):
                dve.wait_ge(hi_done, n + 1)
                dve.tensor_tensor(lo[:, n % 2, :], raw[:, n % RING, :], hi[:, n % 2, :].bitcast(F32),
                                  ALU.subtract).then_inc(lo_done, 1)

            def sharpen(v, y, t):
                link(dve.tensor_tensor(t, y, y, ALU.mult))
                link(dve.tensor_tensor(t, t, v, ALU.mult))
                link(dve.tensor_scalar(t, t, -0.5, 1.5, ALU.mult, ALU.add))
                link(dve.tensor_tensor(y, y, t, ALU.mult))

            def var(ssq, v, y, n):
                link(dve.tensor_scalar(v, ssq, 1.0 / n, EPS, ALU.mult, ALU.add))
                dve.tensor_copy(y, v).then_inc(S("var"), 1)

            def norm_x(which):
                dve.wait_ge(S("sq"), 2 * which + 2)
                if which:
                    dve.wait_ge(S("xlo_ready"), KT)
                var(st[:, 0:2], st[:, 2:4], st[:, 8:10], D)
                dve.wait_ge(S("rs"), 1 if which == 0 else 5)
                sharpen(st[:, 2:4], st[:, 8:10], st[:, 4:6])
                for b in range(TB):
                    m = dve.tensor_scalar(xs[:, b, :], h[:, b, :], st[:, 8 + b:9 + b], None, ALU.mult)
                m.then_inc(S("xs_ready"), 1)

            def x_lo(k, which):
                dve.wait_ge(S("xhi_ready"), which * KT + 2 * (k // 2) + 2)
                dve.scalar_tensor_tensor(xlo[:, k, :], bank[4 + k // 2][:, (k % 2) * T:(k % 2 + 1) * T],
                                         pv("g1" if which == 0 else "g2")[:, k:k + 1],
                                         xhi[:, k, :].bitcast(F32), ALU.mult, ALU.subtract).then_inc(S("xlo_ready"), 1)

            norm_x(0)
            split_lo(0)
            for k in range(KT):
                x_lo(k, 0)
            split_lo(1)
            dve.wait_ge(small_in, 48)
            cosT = cv_("cos").rearrange("p (b d) -> p b d", b=2)
            sinT = cv_("sin").rearrange("p (b d) -> p b d", b=2)
            for b in range(TB):
                for dst_c, dst_s, g_ in [(gcq[:, b, :], gsq[:, b, :], pv("qg"))] + [
                        (gck[:, b, s, :], gsk[:, b, s, :], pv("kgs")[:, s * HD:(s + 1) * HD]) for s in range(2)]:
                    dve.tensor_tensor(dst_c, cosT[:, b, :], g_, ALU.mult)
                    dve.tensor_tensor(dst_s[:, 0:32], sinT[:, b, 0:32], g_[:, 32:64], ALU.mult)
                    dve.tensor_tensor(dst_s[:, 32:64], sinT[:, b, 32:64], g_[:, 0:32], ALU.mult)
            dve.tensor_tensor(gcc, cv_("cosc"), pv("kgc"), ALU.mult)
            dve.tensor_tensor(gsc[:, 0:32], cv_("sinc")[:, 0:32], pv("kgc")[:, 32:64], ALU.mult)
            link(dve.tensor_tensor(gsc[:, 32:64], cv_("sinc")[:, 32:64], pv("kgc")[:, 0:32], ALU.mult))
            tok = stok.rearrange("p (w j g c) -> p w j g c", w=2, j=16, g=2)
            for w in range(2):
                dve.wait_ge(tile_used, w + 1)
                pos = pv("posk" if w == 0 else "posv")
                for g in range(NG):
                    for l2 in range(2):
                        src = bank[3 * w][g * HD:(g + 1) * HD, l2:T]
                        win = bass.AP(src.tensor, src.offset, [list(src.ap[0]), [2, 16], [16, NC_]])
                        r = slice(l2 * HD, (l2 + 1) * HD)
                        m = dve.tensor_tensor(tok[r, w, :, g, :], win,
                                              pos[r, :].unsqueeze(2).broadcast_to([HD, 16, NC_]), ALU.add)
            m.then_inc(S("tok"), 1)
            dve.wait_ge(S("tok_hi"), 1)
            dve.tensor_tensor(auxl[:, :], stok, auxh[:, :].bitcast(F32), ALU.subtract).then_inc(S("tok_split"), 1)
            split_lo(2)
            split_lo(3)
            dve.wait_ge(S("gw_hi"), 1)
            dve.tensor_tensor(gwl[:, :], pv("gw"), gwh[:, :].bitcast(F32), ALU.subtract).then_inc(S("gw_split"), 1)
            for n in range(4, 16):
                split_lo(n)

            def rotate(p_, n, a_, b_, src, y, gc, gs, outs, done):
                nh = src.shape[1]
                yb = y.unsqueeze(2).broadcast_to([p_, nh, HD])
                link(dve.tensor_tensor(n, src, yb, ALU.mult))
                dve.tensor_tensor(a_, n, gc, ALU.mult)
                dve.tensor_tensor(b_[:, :, 0:32], n[:, :, 32:64], gs[:, :, 0:32], ALU.mult)
                link(dve.tensor_tensor(b_[:, :, 32:64], n[:, :, 0:32], gs[:, :, 32:64], ALU.mult))
                for k, o in enumerate(outs):
                    m = dve.tensor_tensor(o, a_, b_, ALU.add)
                if done is None:
                    link(m)
                else:
                    m.then_inc(done, 1)

            def heads(ap_, nh):
                return ap_.rearrange("p (a d) -> p a d", a=nh)

            def per_slot(tab, p_, rep):
                return tab.unsqueeze(2).broadcast_to([p_, tab.shape[1], rep, HD])

            dve.wait_ge(S("sqk"), 1)
            link(dve.tensor_reduce(st[:, 48:56], heads(nrm_a, 8), AXX, ALU.add))
            var(st[:, 48:56], st[:, 48:56], st[:, 16:24], HD)
            split_lo(16)
            dve.wait_ge(S("sqk"), 2)
            link(dve.tensor_reduce(st[0:NC_, 26:28], heads(nrm_c[0:NC_, :], 2), AXX, ALU.add))
            var(st[0:NC_, 26:28], st[0:NC_, 26:28], st[0:NC_, 24:26], HD)
            dve.wait_ge(S("rs"), 2)
            sharpen(st[:, 48:56], st[:, 16:24], st[:, 56:64])
            for b in range(TB):
                n, a_, b_ = (heads(z[:, 0:T], 4) for z in (nrm_n, nrm_q, nrm_b))
                yb = st[:, 16 + 4 * b:20 + 4 * b].unsqueeze(2).broadcast_to([P, 4, HD])
                link(dve.tensor_tensor(n, heads(bank[6 + b][:, 0:T], 4), yb, ALU.mult))
                for s in range(2):
                    gc = gck[:, b, s, :].unsqueeze(1).broadcast_to([P, 2, HD])
                    gs = gsk[:, b, s, :].unsqueeze(1).broadcast_to([P, 2, HD])
                    two = slice(2 * s, 2 * s + 2)
                    dve.tensor_tensor(a_[:, two, :], n[:, two, :], gc, ALU.mult)
                    dve.tensor_tensor(b_[:, two, 0:32], n[:, two, 32:64], gs[:, :, 0:32], ALU.mult)
                    m = dve.tensor_tensor(b_[:, two, 32:64], n[:, two, 0:32], gs[:, :, 32:64], ALU.mult)
                link(m)
                for d_ in range(2):
                    m = dve.tensor_tensor(krdup[:, b, :, d_ * HD:(d_ + 1) * HD], a_, b_, ALU.add)
                link(m)
            split_lo(17)
            dve.wait_ge(S("rs"), 3)
            sharpen(st[0:NC_, 26:28], st[0:NC_, 24:26], st[0:NC_, 28:30])
            n, a_, b_ = (heads(z[0:NC_, 0:P], 2) for z in (nrm_n, nrm_q, nrm_b))
            kd = kcd[0:NC_, :].rearrange("p (g c) -> p g c", g=2)
            rotate(NC_, n, a_, b_, heads(bank[1][0:NC_, P:2 * P], 2), st[0:NC_, 24:26],
                   gcc[0:NC_, :].unsqueeze(1).broadcast_to([NC_, 2, HD]),
                   gsc[0:NC_, :].unsqueeze(1).broadcast_to([NC_, 2, HD]),
                   [kd[:, :, 0:HD], kd[:, :, HD:2 * HD]], S("kcrot"))
            dve.wait_ge(S("kcrot"), 1)
            dve.wait_ge(S("vsw"), 1)
            dve.tensor_copy(st[:, 62:63], st[:, 16:17]).then_inc(S("krot"), 1)
            dve.wait_ge(S("gn_exp"), 1)
            link(dve.tensor_scalar(gsig, gsig, 1.0, None, ALU.add))
            link(dve.reciprocal(gsig, gsig))
            gsv = gsig.rearrange("p (b r h) -> p b r h", b=2, r=3)
            for br, c0 in ((1, 0), (2, 2), (0, 4)):
                m = dve.tensor_copy(ggate[:, :, c0:c0 + 2], gsv[:, :, br, :].rearrange("p b h -> p h b"))
            link(m)
            dve.tensor_scalar(ggate[:, :, 4:5], ggate[:, :, 4:5], cv_("hasc"), None, ALU.mult).then_inc(S("gates_n"), 1)
            dve.wait_ge(S("gates_n"), 1)
            dve.tensor_copy(st[:, 63:64], st[:, 16:17]).then_inc(S("k_normed"), 1)
            split_lo(18)
            split_lo(19)
            dve.wait_ge(S("sqk"), 3)
            dve.tensor_reduce(st[:, 48:56], heads(nrm_a, 8), AXX, ALU.add)
            link(dve.tensor_reduce(st[:, 56:64], heads(nrm_q, 8), AXX, ALU.add))
            var(st[:, 48:64], st[:, 48:64], st[:, 32:48], HD)
            split_lo(20)
            split_lo(21)
            dve.wait_ge(S("rs"), 4)
            sharpen(st[:, 48:64], st[:, 32:48], st[:, 0:16])
            for b in range(TB):
                n, a_, b_ = (heads(z, 8) for z in (nrm_n, nrm_a, nrm_b))
                rotate(P, n, a_, b_, heads(bank[4 + b][:, :], 8), st[:, 32 + 8 * b:40 + 8 * b],
                       gcq[:, b, :].unsqueeze(1).broadcast_to([P, 8, HD]),
                       gsq[:, b, :].unsqueeze(1).broadcast_to([P, 8, HD]),
                       [heads(qrot[:, b, :], 8)], S("qrot") if b else None)
            for n in range(22, 32):
                split_lo(n)

            def mask_scores(hh):
                q = hh % 2
                dve.wait_ge(S("scores"), hh + 1)
                if hh >= 2:
                    dve.wait_ge(S("cmpT"), hh - 1)
                dve.tensor_tensor(sm[:, q, 0:414], bank[4][:, 0:414], cv_("mask"), ALU.add)
                dve.tensor_tensor(sm[:, q, 414:798], bank[5][:, 0:384], cv_("mask")[:, 0:384],
                                  ALU.add).then_inc(S("masked"), 1)
                dve.wait_ge(S("masked"), hh + 1)
                both = sm[:, q, :].rearrange("p (r c) -> p r c", c=414)
                mx = att[:, q, 0:4].rearrange("p (r b) -> p r b", b=2)
                dve.tensor_reduce(mx[:, :, 0:1], both[:, :, 0:P], AXX, ALU.max)
                dve.tensor_reduce(mx[:, :, 1:2], both[:, :, P:384], AXX, ALU.max)
                link(dve.tensor_reduce(att[:, q, 4:6], sm[:, q, 384:414].rearrange("p (b c) -> p b c", b=2), AXX, ALU.max))
                dve.tensor_scalar(att[:, q, 6:12], att[:, q, 0:6], -SCALE, None, ALU.mult).then_inc(S("negmax"), 1)

            def stick_logs(hh):
                dve.wait_ge(S("softplus"), hh + 1)
                if hh:
                    dve.wait_ge(S("a_ready"), hh)
                dve.scalar_tensor_tensor(sbt[:, 0, :], bank[2][:, 0:384], 0.0, sbt[:, 2, :], ALU.max, ALU.add)
                dve.scalar_tensor_tensor(sbt[:, 3, :], bank[2][:, 0:384], 0.0, sbt[:, 2, :], ALU.min,
                                         ALU.subtract).then_inc(S("z_read"), 1)

            mask_scores(0)
            stick_logs(0)
            for hh in range(NH):
                q = hh % 2
                dve.wait_ge(S("exped"), hh + 1)
                link(dve.reciprocal(att[:, q, 18:24], att[:, q, 12:18]))
                link(dve.tensor_tensor(att[:, q, 18:24], att[:, q, 18:24], ggate[:, hh, :], ALU.mult))
                for c, (c0, w_) in enumerate(((0, P), (P, T), (414, P), (414 + P, T), (384, NC_), (384 + NC_, NC_))):
                    x_ = sm[:, q, c0:c0 + w_]
                    m = dve.tensor_scalar(x_, x_, att[:, q, 18 + c:19 + c], None, ALU.mult)
                m.then_inc(S("probs"), 1)
                split_lo(T_GATE + 2 * hh + 2)
                dve.wait_ge(S("cmpT"), hh + 1)
                if hh:
                    dve.wait_ge(S("onsa"), hh)
                dve.tensor_copy(pT[0:NC_, 768:1024], bank[3][0:NC_, 0:T]).then_inc(S("cmpT_out"), 1)
                dve.wait_ge(S("after"), hh + 1)
                dve.tensor_tensor(sbt[:, 0, :], sbt[:, 3, :], bank[2][:, 0:384], ALU.add).then_inc(S("x_ready"), 1)
                if hh + 1 < NH:
                    mask_scores(hh + 1)
                    stick_logs(hh + 1)
                split_lo(T_GATE + 2 * hh + 3)
                dve.wait_ge(S("gate_exp"), 2 * hh + 2)
                two = gates[:, 2 * hh:2 * hh + 2, :]
                link(dve.tensor_scalar(two, two, 1.0, None, ALU.add))
                dve.reciprocal(two, two).then_inc(S("gate_sig"), 1)
            dve.wait_ge(S("oT_hi"), 1)
            dve.tensor_tensor(xlo[:, :, :], oT, xhi[:, :, :].bitcast(F32), ALU.subtract).then_inc(S("oT_split"), 1)
            dve.wait_ge(S("gate_sig"), 8)
            for i in range(8):
                q = i % 2
                dve.wait_ge(tile_used, T_BR + 2 * i + 1)
                if i >= 2:
                    dve.wait_ge(S("mrg_hi"), i - 1)
                ab = mrg[:, q, 0:512].rearrange("p (r t) -> p r t", r=2)
                gate = gates.rearrange("p (r a) t -> p r a t", r=2)[:, :, i, :]
                dve.tensor_tensor(ab, bank[4 + q][:, :].rearrange("p (r t) -> p r t", r=2), gate,
                                  ALU.mult).then_inc(S("mrg_read"), 1)
                dve.wait_ge(S("mrg_read"), i + 1)
                dve.tensor_tensor(mrg[:, q, 512:768], mrg[:, q, 0:T], mrg[:, q, T:512], ALU.add).then_inc(S("merged"), 1)
                dve.wait_ge(S("mrg_hi"), i + 1)
                dve.tensor_tensor(auxl[:, q * T:(q + 1) * T], mrg[:, q, 512:768],
                                  auxh[:, q * T:(q + 1) * T].bitcast(F32), ALU.subtract).then_inc(S("mrg_split"), 1)
                split_lo(T_BR + 2 * i + 2)
                split_lo(T_BR + 2 * i + 3)
            dve.wait_ge(tile_used, T_WQ)
            for b in range(TB):
                for f in range(2):
                    c = slice(f * 512, (f + 1) * 512)
                    m = dve.tensor_tensor(h[:, b, c], h[:, b, c], bank[2 * b + f][:, :], ALU.add)
                m.then_inc(S("h_ready"), 1)
            norm_x(1)
            for k in range(KT):
                x_lo(k, 1)

            def sc_out(j):
                dve.wait_ge(S("key_scores"), j + 1)
                dst = sc.rearrange("p (b h s k) -> p h s b k", b=2, h=8, s=2)[:, j]
                dve.tensor_copy(dst, bank[6 + j % 2][:, :].rearrange("p (s b k) -> p s b k", s=2, b=2)).then_inc(S("sc_out"), 1)

            for i in range(NH):
                split_lo(T_WQ + 2 * i + 2)
                split_lo(T_WQ + 2 * i + 3)
                if i:
                    sc_out(i - 1)
            sc_out(NH - 1)

            def loop_lo(i, j, base):
                n = base + j
                dve.wait_ge(hi_done, i * UNROLL + (n + 1))
                dve.tensor_tensor(lo[:, n % 2, :], raw[:, n % RING, :], hi[:, n % 2, :].bitcast(F32),
                                  ALU.subtract).then_inc(lo_done, 1)

            def top16(src, vals, w_):
                link(dve.max(vals[:, 0:8], src))
                dve.max_index(sti[:, 0:8], vals[:, 0:8], src)
                link(dve.match_replace(stg2[:, 0:w_], vals[:, 0:8], src, -3e38))
                link(dve.max(vals[:, 8:16], stg2[:, 0:w_]))
                link(dve.max_index(sti[:, 8:16], vals[:, 8:16], stg2[:, 0:w_]))

            dve.wait_ge(S("sc_out"), NH)
            for c in range(32):
                loop_lo(c // UNROLL, c % UNROLL + 2, N_PRE)
                c16 = slice(c * 16, c * 16 + 16)
                top16(sc[:, c * P:(c + 1) * P], tkv[:, c16], P)
                link(dve.tensor_copy(tki[:, c16], sti))
            for c in range(16):
                i, j = TOPK_CAND + c // 2, c % 2
                loop_lo(i, 2 * j + 2, N_PRE)
                s1 = tkv[:, c * 32:c * 32 + 16].unsqueeze(2).broadcast_to([P, 16, 16])
                s2 = tkv[:, c * 32 + 16:c * 32 + 32].unsqueeze(1).broadcast_to([P, 16, 16])
                link(dve.tensor_tensor(stg.rearrange("p (a b) -> p a b", a=16), s1, s2, ALU.add))
                loop_lo(i, 2 * j + 3, N_PRE)
                c16 = slice(c * 16, c * 16 + 16)
                top16(stg, cval[:, c16], 256)
                link(dve.tensor_scalar(sta, sti, 4, None, ALU.logical_shift_right))
                link(dve.tensor_copy(caf[:, c16], sta))
                link(dve.tensor_scalar(sta, sti, 15, None, ALU.bitwise_and))
                link(dve.tensor_copy(cbf[:, c16], sta))
            step = S("key_numbers")
            with dve.Fori(0, TOPK_END - TOPK_IDX) as i:
                at_ = [0]

                def nxt(ins):
                    at_[0] += 1
                    ins.then_inc(step, 1)
                    dve.wait_ge(step, i * 12 + at_[0])

                eq = eqt.rearrange("p (k a) -> p k a", k=16)
                places = iota16.unsqueeze(1).broadcast_to([P, 16, 16])
                for j in range(2):
                    loop_lo(i, 4 * TOPK_IDX + 2 * j + 2, N_PRE)
                    c16, c32 = i * 32 + j * 16, i * 64 + j * 32
                    for side, (pl, dst) in enumerate(((caf, i1f), (cbf, i2f))):
                        at_pl = pl[:, bass.ds(c16, 16)].unsqueeze(2).broadcast_to([P, 16, 16])
                        keys = tki[:, bass.ds(c32 + 16 * side, 16)].unsqueeze(1).broadcast_to([P, 16, 16])
                        nxt(dve.tensor_tensor(eq, places, at_pl, ALU.is_equal))
                        nxt(dve.tensor_tensor(eq, eq, keys, ALU.mult))
                        nxt(dve.tensor_reduce(dst[:, bass.ds(c16, 16)], eq, AXX, ALU.add))
                    loop_lo(i, 4 * TOPK_IDX + 2 * j + 3, N_PRE)
                assert at_[0] == 12
            cv3 = cval.rearrange("p (c k) -> p c k", k=16)
            g3 = gwt.rearrange("p (c k) -> p c k", k=16)
            dve.tensor_tensor(g3, cv3, cv3[:, :, 0:1].broadcast_to([P, 16, 16]), ALU.subtract).then_inc(S("router_d"), 1)
            dve.wait_ge(S("router_exp"), 1)
            link(dve.tensor_reduce(smx[:, 0:16], g3, AXX, ALU.add))
            link(dve.reciprocal(smx[:, 16:32], smx[:, 0:16]))
            dve.tensor_tensor(g3, g3, smx[:, 16:32].unsqueeze(2).broadcast_to([P, 16, 16]), ALU.mult).then_inc(S("router"), 1)
            dve.wait_ge(S("routerT"), 1)
            dve.tensor_copy(eT[:, 0:2, :], bank[6][:, :].rearrange("p (w t) -> p w t", w=2)).then_inc(S("bank67_read"), 1)
            dve.tensor_copy(eT[:, 2, :], bank[7][:, 0:T]).then_inc(S("bank67_read"), 1)
            dve.wait_ge(S("bank67_read"), 2)
            with dve.Fori(0, NBLK // UNROLL - TOPK_END) as i:
                for j in range(UNROLL):
                    loop_lo(i, 4 * TOPK_END + j + 2, N_PRE)

            def rows_a(i, q, first=False):
                if not first:
                    dve.wait_ge(S("g_ready"), i * 2 + (q - 1))
                for t in range(4):
                    tok_ = bass.ds(i * 8 + (4 * q + t), 1)
                    m = dve.tensor_scalar(oneA[:, q, t, :], iota, eT[:, 0, tok_], eT[:, 2, tok_],
                                          ALU.is_equal, ALU.mult)
                m.then_inc(S("oneA_ready"), 1)

            by_token = big[:, :].rearrange("p (e t) -> p t e", t=T)

            def weigh(i, q):
                dve.wait_ge(S("g_ready"), i * 2 + (q + 1))
                w4 = by_token[:, bass.ds(i * 8 + 4 * q, 4), :]
                dve.tensor_tensor(w4, bank[6 + q][:, :].rearrange("p (t e) -> p t e", t=4), w4,
                                  ALU.mult).then_inc(S("bank67_read"), 1)

            rows_a(0, 0, first=True)
            rows_a(0, 1, first=True)
            dve.wait_ge(S("bank45_read"), NH + NBLK // 2)
            with dve.Fori(1, T // 8) as i:
                weigh(i - 1, 0)
                rows_a(i, 0)
                weigh(i - 1, 1)
                rows_a(i, 1)
            weigh(T // 8 - 1, 0)
            weigh(T // 8 - 1, 1)

            V0 = N_PRE + NBLK
            last = NBLK // UNROLL - 1

            def w_lo(i, j):
                dve.wait_ge(S("whi_done"), i * UNROLL + (j + 1))
                dve.tensor_tensor(auxl[:, (j % 2) * T:(j % 2 + 1) * T], big[:, bass.ds(i * (UNROLL * T) + j * T, T)],
                                  auxh[:, (j % 2) * T:(j % 2 + 1) * T].bitcast(F32), ALU.subtract).then_inc(S("wlo_done"), 1)

            w_lo(0, 0)
            w_lo(0, 1)
            with dve.Fori(0, last) as i:
                for j in range(UNROLL):
                    loop_lo(i, j + 2, V0)
                    w_lo(i, j + 2)
            for j in range(2):
                split_lo(V0 + last * UNROLL + j + 2)
                w_lo(last, j + 2)
            dve.wait_ge(tile_used, N_ALL)
            for b in range(TB):
                for f in range(2):
                    c = slice(f * 512, (f + 1) * 512)
                    dve.tensor_tensor(h[:, b, c], h[:, b, c], bank[2 * b + f][:, :], ALU.add).then_inc(S("out_ready"), 1)

        @block.gpsimd
        def _(pool):
            for hh in range(NH):
                pool.wait_ge(S("z_read"), hh + 1)
                if hh:
                    pool.wait_ge(S("after"), hh)
                pool.tensor_tensor(sbt[:, 1, :], sbt[:, 0, :], cv_("msb"), ALU.mult).then_inc(S("l_masked"), 1)
                pool.wait_ge(S("x_exp"), hh + 1)
                if hh:
                    pool.wait_ge(S("osb"), hh)
                pool.tensor_tensor(sbt[:, 4, :], sbt[:, 0, :], cv_("msb"), ALU.mult).then_inc(S("a_ready"), 1)

            def distances(i, q, first=False):
                if not first:
                    pool.wait_ge(S("g_ready"), i * 2 + (q - 1))
                i2 = eT[:, 1, bass.ds(i * 8 + 4 * q, 4)].unsqueeze(2).broadcast_to([P, 4, P])
                pool.tensor_tensor(oneB[:, q, :, :], iota.unsqueeze(1).broadcast_to([P, 4, P]), i2,
                                   ALU.subtract).then_inc(S("dist"), 1)

            pool.wait_ge(S("bank67_read"), 2)
            distances(0, 0, first=True)
            distances(0, 1, first=True)
            with pool.Fori(1, T // 8) as i:
                distances(i, 0)
                distances(i, 1)

    return nc


def lay_out(a):
    f = np.float32
    win = a["w_in"][0]
    col = {}
    at = 0
    for name, n in (("q", 512), ("kc", 128), ("vc", 128), ("ks", 128), ("vs", 128), ("kw", 128), ("vw", 128),
                    ("gn", 24), ("qsb", 512), ("ksb", 512), ("vsb", 512), ("br", 2 * D)):
        col[name] = win[:, at:at + n]
        at += n
    assert at == win.shape[1]

    def stationary(w):
        return w.reshape(KT, P, -1, P).transpose(2, 1, 0, 3).reshape(-1, P, 1024)

    def moving(w):
        return w.reshape(4, 2, P, 512).transpose(0, 2, 1, 3).reshape(4, P, 1024)

    def compress(w):
        return w.reshape(4, 4, P, CH).transpose(0, 2, 1, 3).reshape(4, P, 1024)

    bn, bs, wo = a["w_branch_nsa"][0], a["w_branch_sb"][0], a["w_out"][0]
    both = np.concatenate([bn, bs], 0)
    br = stationary(both)
    mix = np.stack([br, wo.reshape(8, P, D)], 1).reshape(16, P, 1024)
    wpre = np.concatenate([
        stationary(col["kc"]), stationary(col["vc"]), compress(a["cmp_k_w1"][0]), compress(a["cmp_v_w1"][0]),
        moving(np.concatenate([col["ks"], col["kw"], col["vs"], col["vw"]], 1)), moving(col["q"]),
        stationary(col["qsb"]), stationary(col["ksb"]), moving(col["vsb"]), stationary(col["br"]),
        mix, stationary(a["peer_w_query"][0])], 0)
    assert wpre.shape[0] == N_PRE
    u = a["peer_u"][0].reshape(NBLK, P, KT, P).transpose(0, 3, 2, 1).reshape(NBLK, P, 1024)
    v = a["peer_v"][0].reshape(NBLK, P, D)

    par = np.zeros((P, NPAR), f)

    def put(name, x):
        at, n = PAR[name]
        par[:, at:at + n] = x

    put("g1", a["norm1_g"][0].reshape(KT, P).T)
    put("g2", a["norm2_g"][0].reshape(KT, P).T)
    put("qg", a["q_norm_g"][0][None])
    put("kgc", a["k_norm_g"][0, 0][None])
    put("kgs", a["k_norm_g"][0, 1:3].reshape(1, 128))
    put("posk", a["cmp_pos_k"][0].reshape(16, P).T)
    put("posv", a["cmp_pos_v"][0].reshape(16, P).T)
    put("w2k", a["cmp_k_w2"][0].reshape(2, P, HD).transpose(1, 0, 2).reshape(P, 128))
    put("w2v", a["cmp_v_w2"][0].reshape(2, P, HD).transpose(1, 0, 2).reshape(P, 128))
    put("subk", a["peer_subkeys"][0].transpose(2, 0, 1).reshape(P, 256))
    put("gw", col["gn"].reshape(KT, P, 24).transpose(1, 0, 2).reshape(P, 192))
    return np.ascontiguousarray(wpre), np.ascontiguousarray(u), np.ascontiguousarray(v), par


def constants():
    f = np.float32
    cst, kep = np.zeros((P, NCST), f), np.zeros((P, NKEP), f)

    def put(name, x):
        at, n = CST[name]
        cst[:, at:at + n] = x

    half = HD // 2
    freqs = (f(10000.0) ** (-np.arange(half, dtype=f) / f(half))).astype(f)

    def table(pos):
        ang = pos.astype(f)[:, None] * freqs[None]
        c, s = np.cos(ang).astype(f), np.sin(ang).astype(f)
        return np.concatenate([c, c], 1), np.concatenate([-s, s], 1)

    c, s = table(np.arange(T))
    put("cos", c.reshape(TB, P, HD).transpose(1, 0, 2).reshape(P, 128))
    put("sin", s.reshape(TB, P, HD).transpose(1, 0, 2).reshape(P, 128))
    c, s = table(np.arange(P) * 16 + CL - 1)
    put("cosc", c)
    put("sinc", s)
    r, k = np.arange(P)[:, None], np.arange(P)[None]
    put("tri", np.where(r > k, -1.0, 0.0))
    put("ones", -1.0)
    causal = np.where(k <= r, 0.0, NEG)
    end = np.arange(NC_)[None] * 16 + CL - 1
    put("mask", np.concatenate([causal, np.zeros((P, P)), causal, np.where(end <= r, 0.0, NEG),
                                np.where(end <= r + P, 0.0, NEG)], 1))
    strict = np.where(r < k, 1.0, 0.0)
    put("msb", np.concatenate([strict, np.ones((P, P)), strict], 1))
    put("hasc", np.where(r >= CL - 1, 1.0, 0.0))
    kep[:, KEP["ident"][0]:KEP["ident"][0] + P] = np.eye(P)
    kep[:, KEP["iota"][0]:KEP["iota"][0] + P] = k
    kep[:, KEP["iota16"][0]:KEP["iota16"][0] + 16] = np.arange(16)[None]
    return cst, kep


def kernel(**inputs):
    import concourse.bacc as bacc
    from concourse.bass_utils import run_bass_kernel_spmd

    a = {k: np.asarray(v) for k, v in inputs.items()}
    wpre, u, v, par = lay_out(a)
    cst, kep = constants()
    arrays = dict(x_d=np.ascontiguousarray(a["x"][0]), wpre_d=wpre, u_d=u, v_d=v, par_d=par, cst_d=cst, kep_d=kep)
    nc = bacc.Bacc("TRN2", target_bir_lowering=False, num_devices=1)
    args = [nc.dram_tensor(k, x.shape, mybir.dt.from_np(x.dtype), kind="ExternalInput").ap() for k, x in arrays.items()]
    args.append(nc.dram_tensor("out_d", (T, D), F32, kind="ExternalOutput").ap())
    build(nc, *args)
    r = run_bass_kernel_spmd(nc, [arrays], core_ids=[0])
    return r.results[0]["out_d"].reshape(1, T, D)
```

```python
from contextlib import ExitStack

import numpy as np
import concourse.bass as bass
from concourse import mybir

F32 = mybir.dt.float32
F32R = mybir.dt.float32r
U32 = mybir.dt.uint32
ALU = mybir.AluOpType
ACT = mybir.ActivationFunctionType
AXX = mybir.AxisListType.X

P = 128
D = 1024
T = 256
TB = T // P
KT = D // P
HD = 64
NH = 8
NG = 2
NC_ = (T - 32) // 16 + 1
CL = 32
CH = 256
TOPK = 16
NK = 128
NBLK = 128
EPS = 1e-6
NEG = -1e30
SCALE = 0.125

T_KC, T_VC = 0, 1
T_KV, T_Q = 2, 6
T_W1K, T_W1V = 10, 14
T_QSB, T_KSB = 18, 22
T_VSB = 26
T_GATE = 30
T_BR = 46
T_WQ = 62
N_PRE = 78
N_ALL = N_PRE + 2 * NBLK
RING = 4
SPLIT = 3
UNROLL = 12
U1 = 66
NGRP = T // 4
HALF = NBLK // 2
TILES_KEYS, TILES_PAIRS = 22, 24
TILES_NUMBERS = U1 - 2 - TILES_KEYS - TILES_PAIRS

PARAMS = dict(g1=8, g2=8, qg=64, kgc=64, kgs=128, posk=16, posv=16, w2k=128, w2v=128, subk=256, gw=192)
CONSTS = dict(cos=128, sin=128, cosc=64, sinc=64, tri=128, ones=128, mask=384 + 2 * NC_, msb=384, hasc=1)
KEPT = dict(ident=128, iota=128, iota16=16)


def offsets(table):
    out, at = {}, 0
    for k, n in table.items():
        out[k] = (at, n)
        at += n
    return out, at


PAR, NPAR = offsets(PARAMS)
CST, NCST = offsets(CONSTS)
KEP, NKEP = offsets(KEPT)


def build(nc, x_d, wpre_d, u_d, v_d, par_d, cst_d, kep_d, out_d):
    with ExitStack() as ctx:
        def sb(name, shape, dt=F32):
            return ctx.enter_context(nc.sbuf_tensor(name, shape, dt))

        def sem(name):
            return ctx.enter_context(nc.semaphore(name))

        bank = [ctx.enter_context(nc.psum_tensor(f"bank{i}", [P, 512], F32)) for i in range(8)]

        u_bank = (bank[4], bank[5], bank[3])

        big = sb("big", [P, NBLK * T])
        raw = sb("raw", [P, RING, 1024])
        hi = sb("hi", [P, SPLIT, 1024], F32R)
        lo = sb("lo", [P, SPLIT, 1024], F32R)
        xhi = sb("xhi", [P, 8, T], F32R)
        xlo = sb("xlo", [P, 8, T], F32R)
        auxh = sb("auxh", [P, SPLIT * T], F32R)
        auxl = sb("auxl", [P, SPLIT * T], F32R)
        kep = sb("kep", [P, NKEP])
        eT = sb("eT", [P, 3, T])
        gw2 = sb("gw2", [P, T, 2], F32R)
        same = sb("same", [P, 2, 4, HALF])
        oneA = sb("oneA", [P, 2, 4, 2, HALF], F32R)
        gsum = sb("gsum", [P, 4, HALF])
        oneB = sb("oneB", [P, 2, 4, P], F32R)

        gwh, gwl = (gw2[:, :, :].rearrange("p t r -> p (t r)")[:, z * 192:(z + 1) * 192] for z in range(2))
        at = [0]

        def carve(n, start=None):
            if start is not None:
                at[0] = start
            a = at[0]
            at[0] += n
            assert at[0] <= NBLK * T
            return big[:, a:a + n]

        h = carve(TB * D).rearrange("p (b d) -> p b d", b=TB)
        par = carve(NPAR)
        cst = carve(NCST)

        def pv(k):
            a, n = PAR[k]
            return par[:, a:a + n]

        def cv_(k):
            a, n = CST[k]
            return cst[:, a:a + n]

        ident = kep[:, KEP["ident"][0]:KEP["ident"][0] + P]
        iota = kep[:, KEP["iota"][0]:KEP["iota"][0] + P]
        iota16 = kep[:, KEP["iota16"][0]:KEP["iota16"][0] + 16]

        xs = carve(TB * D).rearrange("p (b d) -> p b d", b=TB)
        st = carve(64)
        gcq, gsq = (carve(128).rearrange("p (b d) -> p b d", b=2) for _ in range(2))
        gck, gsk = (carve(256).rearrange("p (b s d) -> p b s d", b=2, s=2) for _ in range(2))
        gcc, gsc = carve(64), carve(64)
        nrm_n, nrm_a, nrm_b, nrm_q, nrm_c = carve(512), carve(512), carve(512), carve(512), carve(128)
        qrot = carve(1024).rearrange("p (b c) -> p b c", b=2)
        krdup = carve(1024).rearrange("p (b s c) -> p b s c", b=2, s=4)
        kcd = carve(256)
        vsw = carve(512).rearrange("p (b c) -> p b c", b=2)
        vcs = carve(128)
        qT = carve(1024).rearrange("p (a t) -> p a t", a=4)
        kT = carve(1024).rearrange("p (a t) -> p a t", a=4)
        kcT = carve(32).rearrange("p (g c) -> p g c", g=2)
        qsbT = carve(1024).rearrange("p (a t) -> p a t", a=4)
        ksbT = carve(1024).rearrange("p (a t) -> p a t", a=4)
        vsb = carve(1024).rearrange("p (b c) -> p b c", b=2)
        ghid = carve(120)
        hidn = carve(2 * CH)[0:30, :]
        gsig = carve(48)
        gexpT = carve(T)[0:24, :]
        ggate = carve(48).rearrange("p (h c) -> p h c", c=6)
        sm = carve(2 * 828).rearrange("p (q c) -> p q c", q=2)
        att = carve(2 * 32).rearrange("p (q c) -> p q c", q=2)
        pT = carve(1024)
        sbt = carve(5 * 384).rearrange("p (k c) -> p k c", k=5)
        gates_at = at[0]
        gates = carve(4096).rearrange("p (a t) -> p a t", a=16)
        stok = big[:, gates_at:gates_at + 960]
        oT = carve(2048).rearrange("p (a t) -> p a t", a=8)
        mrg = carve(2 * 768).rearrange("p (q c) -> p q c", q=2)
        qst = cst[:, 0:1024].rearrange("p (q c) -> p q c", q=2)
        sc = carve(4096, start=24064)
        tkv, tki = carve(512), carve(512)
        cval = carve(256)
        caf, cbf = carve(256), carve(256)
        i1f, i2f = carve(256), carve(256)
        gwt = carve(256)
        stg, stg2, eqt = ([carve(256) for _ in range(2)] for _ in range(3))
        sti, sta, stb = ([carve(16).bitcast(U32) for _ in range(2)] for _ in range(3))
        smx = carve(32)
        assert at[0] <= NBLK * T

        loaded = [sem(f"tile_loaded{i}") for i in range(RING)]
        small_in = sem("small_in")
        x_in = sem("x_in")
        hi_done = sem("hi_done")
        lo_done = sem("lo_done")
        tile_used = sem("tile_used")
        dve_step = sem("dve_step")
        act_step = sem("act_step")
        N = {}

        def S(name):
            if name not in N:
                N[name] = sem(name)
            return N[name]

        def is_split(n):
            return not T_W1K <= n < T_W1V + 4

        def splits(n):
            return n - min(max(n - T_W1K, 0), 8)

        def slot_user(n):
            n -= SPLIT
            while not is_split(n):
                n -= SPLIT
            return n

        def branch_tile(i):
            return T_BR + max(2 * i - 1, 0)

        def out_tile(i):
            return T_BR + min(2 * i + 2, 15)

        def mix_splits(i):
            first = branch_tile(i) + SPLIT
            return range(first, first + (1 if i == 0 else 3 if i == 7 else 2))

        def each_tile(eng, count, body):
            steps = count // UNROLL
            if steps > 1:
                with eng.Fori(0, steps) as i:
                    for j in range(UNROLL):
                        body(i, j)
                for j in range(count - steps * UNROLL):
                    body(steps, j)
            else:
                for j in range(count):
                    body(0, j)

        block = ctx.enter_context(nc.Block())

        @block.sync
        def _(sp):
            sp.dma_start(h[:, :, :], x_d.rearrange("(b p) d -> p b d", p=P)).then_inc(x_in, 16)
            sp.dma_start(cst, cst_d).then_inc(small_in, 16)
            sp.dma_start(par, par_d).then_inc(small_in, 16)
            sp.dma_start(kep[:, :], kep_d).then_inc(small_in, 16)

            def load(slot, src):
                sp.dma_start(raw[:, slot, :], src).then_inc(loaded[slot], 16)

            for n in range(RING):
                load(n, wpre_d[n])

            for n in range(RING, T_W1V + 4 + RING):
                if is_split(n - RING):
                    sp.wait_ge(lo_done, splits(n - RING + 1))
                else:
                    sp.wait_ge(tile_used, n - RING + 1)
                load(n % RING, wpre_d[n])

            def stream(src, first, at_, count):
                def one(i, j):
                    sp.wait_ge(lo_done, i * UNROLL + splits(first + at_ + j - RING + 1))
                    load((first + at_ + j) % RING,
                         src[bass.ds(i * UNROLL + (at_ + j), 1)].rearrange("a p c -> (a p) c"))
                each_tile(sp, count, one)

            begin = T_W1V + 4 + RING
            stream(wpre_d, 0, begin, T_WQ + 8 - begin)
            sp.wait_ge(S("h_ready"), TB)
            for b in range(TB):
                sp.dma_start(out_d[b * P:(b + 1) * P, :], h[:, b, :]).then_inc(S("h_saved"), 16)
            stream(wpre_d, 0, T_WQ + 8, N_PRE - T_WQ - 8)
            stream(u_d, N_PRE, 0, NBLK)
            stream(v_d, N_PRE + NBLK, 0, HALF)
            sp.wait_ge(S("h_saved"), 16 * TB)
            sp.wait_ge(tile_used, N_PRE + NBLK + T // 32)
            for b in range(TB):
                sp.dma_start(h[:, b, :], out_d[b * P:(b + 1) * P, :]).then_inc(S("h_back"), 16)
            stream(v_d, N_PRE + NBLK, HALF, HALF)
            for b in range(TB):
                sp.wait_ge(S("out_ready"), 2 * (b + 1))
                sp.dma_start(out_d[b * P:(b + 1) * P, :], h[:, b, :]).then_inc(S("stored"), 16)
            sp.wait_ge(S("stored"), 16 * TB)

        @block.tensor
        def _(pe):
            def need(n):
                pe.wait_ge(hi_done, splits(n + 1))
                pe.wait_ge(lo_done, splits(n + 1))

            def tposed(n, out):
                need(n)
                s = n % SPLIT
                for k in range(KT):
                    wh, wl = hi[:, s, k * P:(k + 1) * P], lo[:, s, k * P:(k + 1) * P]
                    pe.matmul(out, wh, xhi[:, k, :], start=(k == 0), stop=False)
                    pe.matmul(out, wh, xlo[:, k, :], start=False, stop=False)
                    m = pe.matmul(out, wl, xhi[:, k, :], start=False, stop=(k == KT - 1))
                m.then_inc(tile_used, 1)

            def normal(n, i, outs):
                need(n)
                s = n % SPLIT
                for b in range(TB):
                    for kk in range(2):
                        k = 2 * i + kk
                        wh, wl = hi[:, s, kk * 512:kk * 512 + 512], lo[:, s, kk * 512:kk * 512 + 512]
                        xh, xl = xhi[:, k, b * P:(b + 1) * P], xlo[:, k, b * P:(b + 1) * P]
                        pe.matmul(outs[b], xh, wh, start=(k == 0), stop=False)
                        pe.matmul(outs[b], xh, wl, start=False, stop=False)
                        m = pe.matmul(outs[b], xl, wh, start=False, stop=(k == KT - 1))
                m.then_inc(tile_used, 1)

            def transpose_x(which):
                for k in range(KT):
                    for b in range(TB):
                        m = pe.matmul(bank[4 + k // 2][:, (k % 2) * T + b * P:(k % 2) * T + (b + 1) * P],
                                      h[:, b, k * P:(k + 1) * P], xs[:, b, 0:P], start=True, stop=True)
                    if k % 2:
                        m.then_inc(S("xT_ready"), 1)

            pe.wait_ge(small_in, 48)
            pe.wait_ge(S("xs_ready"), 1)
            transpose_x(0)
            pe.wait_ge(S("xlo_ready"), KT)
            tposed(T_KC, bank[0][:, 0:T])
            tposed(T_VC, bank[3][:, 0:T])
            for i in range(4):
                normal(T_KV + i, i, [bank[6][:, :], bank[7][:, :]])
            pe.wait_ge(S("gw_split"), 1)
            out = bank[2][0:24, 0:T]
            for k in range(KT):
                wh, wl = gwh[:, 24 * k:24 * k + 24], gwl[:, 24 * k:24 * k + 24]
                pe.matmul(out, wh, xhi[:, k, :], start=(k == 0), stop=False)
                pe.matmul(out, wh, xlo[:, k, :], start=False, stop=False)
                m = pe.matmul(out, wl, xhi[:, k, :], start=False, stop=(k == KT - 1))
            m.then_inc(S("gn_ready"), 1)
            for i in range(4):
                normal(T_Q + i, i, [bank[4][:, :], bank[5][:, :]])
            pe.wait_ge(S("gn_exp"), 1)
            pe.wait_ge(S("tok"), 1)
            for b in range(TB):
                m = pe.transpose(bank[3][:, 32 * b:32 * b + 24], gexpT[:, b * P:(b + 1) * P], ident[0:24, 0:24])
            m.then_inc(S("gnT_ready"), 1)
            for w, first in ((0, T_W1K), (1, T_W1V)):
                for i in range(4):
                    n = first + i
                    pe.wait_ge(loaded[n % RING], 16 * (n // RING + 1))
                    for jj in range(4):
                        j = 4 * i + jj
                        a = w * 480 + j * 30
                        m = pe.matmul(bank[1 + w][0:30, 0:CH], stok[:, a:a + 30],
                                      raw[:, n % RING, jj * CH:(jj + 1) * CH], start=(j == 0), stop=(j == 15))
                    m.then_inc(tile_used, 1)
            for i in range(4):
                if i == 1:
                    pe.wait_ge(S("hid"), 2)
                    for z in range(4):
                        m = pe.transpose(bank[1][:, CH + 32 * z:CH + 32 * z + 30], hidn[:, z * P:(z + 1) * P],
                                         ident[0:30, 0:30])
                    m.then_inc(S("hidT_ready"), 1)
                    pe.wait_ge(S("gates_n"), 1)
                if i == 2:
                    pe.wait_ge(S("ghid"), 1)
                    for w in range(2):
                        w2 = pv("w2k" if w == 0 else "w2v")
                        for g in range(NG):
                            for hb in range(2):
                                a = (w * 2 + hb) * 30 + g * NC_
                                m = pe.matmul(bank[1][0:NC_, P + (w * 2 + g) * HD:P + (w * 2 + g + 1) * HD],
                                              ghid[:, a:a + NC_], w2[:, hb * HD:(hb + 1) * HD],
                                              start=(hb == 0), stop=(hb == 1))
                    m.then_inc(S("cmp_ready"), 1)
                if i >= 2:
                    pe.wait_ge(S("qksb_out"), i - 1)
                b = bank[(0, 3)[i % 2]]
                tposed(T_QSB + 2 * i, b[:, 0:T])
                tposed(T_QSB + 2 * i + 1, b[:, T:2 * T])
            pe.wait_ge(S("krot"), 1)
            pe.wait_ge(S("vsw"), 1)
            for s in range(4):
                for b in range(TB):
                    m = pe.transpose(bank[6 + s // 2][:, (s % 2) * T + b * P:(s % 2) * T + (b + 1) * P],
                                     krdup[:, b, s, :], ident)
            m.then_inc(S("kT_ready"), 1)
            pe.wait_ge(S("kcrot"), 1)
            pe.wait_ge(S("vc_out"), 1)
            for g in range(NG):
                m = pe.transpose(bank[1][:, 400 + 16 * g:400 + 16 * g + NC_],
                                 kcd[0:NC_, g * P:(g + 1) * P], ident[0:NC_, 0:NC_])
            m.then_inc(S("kcT_ready"), 1)
            pe.wait_ge(S("kcT_out"), 1)
            pe.wait_ge(S("vc_out"), 1)
            for i in range(4):
                normal(T_VSB + i, i, [bank[2][:, :], bank[1][:, :]])
            pe.wait_ge(S("qrot"), 1)
            for a in range(4):
                for b in range(TB):
                    m = pe.transpose(bank[4 + a // 2][:, (a % 2) * T + b * P:(a % 2) * T + (b + 1) * P],
                                     qrot[:, b, a * P:(a + 1) * P], ident)
            m.then_inc(S("qT_ready"), 1)

            def scores(hh):
                r0, a, g = 64 * (hh % 2), hh // 2, hh // 4
                r = slice(r0, r0 + HD)
                if hh == 0:
                    pe.wait_ge(S("qkT_out"), 3)
                else:
                    pe.wait_ge(S("masked"), hh)
                for br, o in ((0, bank[4]), (1, bank[5])):
                    k = kT[r, 2 * br + g, :]
                    pe.matmul(o[:, 0:P], qT[r, a, 0:P], k[:, 0:P], start=True, stop=True)
                    m = pe.matmul(o[:, P:384], qT[r, a, P:T], k[:, 0:T], start=True, stop=True)
                for b in range(TB):
                    m = pe.matmul(bank[4][:, 384 + NC_ * b:384 + NC_ * (b + 1)], qT[r, a, b * P:(b + 1) * P],
                                  kcT[r, g, 0:NC_], start=True, stop=True)
                m.then_inc(S("scores"), 1)

            def sticks(hh):
                r0, a = 64 * (hh % 2), hh // 2
                r = slice(r0, r0 + HD)
                if hh == 0:
                    pe.wait_ge(S("qksb_out"), 4)
                    pe.wait_ge(S("vsb_out"), 1)
                else:
                    pe.wait_ge(S("x_ready"), hh)
                pe.matmul(bank[2][:, 0:T], ksbT[r, a, 0:P], qsbT[r, a, :], start=True, stop=True)
                m = pe.matmul(bank[2][:, T:384], ksbT[r, a, P:T], qsbT[r, a, P:T], start=True, stop=True)
                m.then_inc(S("z_ready"), 1)

            def gate_tile(g):
                if g >= 2:
                    pe.wait_ge(S("gate_exp"), g - 1)
                else:
                    pe.wait_ge(S("vsb_out"), 2)
                tposed(T_GATE + g, bank[g % 2][:, 0:T])

            scores(0)
            sticks(0)
            for hh in range(NH):
                r0, a, g = 64 * (hh % 2), hh // 2, hh // 4
                gate_tile(2 * hh)
                pe.wait_ge(S("probs"), hh + 1)
                if hh == 0:
                    pe.wait_ge(S("qksb_out"), 4)
                else:
                    pe.wait_ge(S("pT_out"), 2 * hh)
                    pe.wait_ge(S("cmpT_out"), hh)
                    pe.wait_ge(S("osb_out"), hh)
                q = hh % 2
                for br in range(2):
                    for c in range(3):
                        m = pe.transpose(bank[6 + br][:, c * P:(c + 1) * P],
                                         sm[:, q, 414 * br + c * P:414 * br + (c + 1) * P], ident)
                m.then_inc(S("pT"), 1)
                for b in range(TB):
                    m = pe.transpose(bank[3][0:NC_, b * P:(b + 1) * P],
                                     sm[:, q, 384 + NC_ * b:384 + NC_ * (b + 1)], ident)
                m.then_inc(S("cmpT"), 1)
                pe.wait_ge(S("l_masked"), hh + 1)
                L = sbt[:, 1, :]
                pe.matmul(bank[2][:, 0:T], cv_("tri"), L[:, 0:T], start=True, stop=False)
                pe.matmul(bank[2][:, P:T], cv_("ones"), L[:, T:384], start=False, stop=True)
                m = pe.matmul(bank[2][:, T:384], cv_("tri"), L[:, T:384], start=True, stop=True)
                m.then_inc(S("after"), 1)
                gate_tile(2 * hh + 1)
                if hh + 1 < NH:
                    scores(hh + 1)
                    sticks(hh + 1)
                pe.wait_ge(S("pT_out"), 2 * hh + 2)
                pe.wait_ge(S("cmpT_out"), hh + 1)
                o = bank[3][r0:r0 + HD, 0:T]
                for br in range(2):
                    vcol = slice((2 * br + g) * HD, (2 * br + g + 1) * HD)
                    p0 = 384 * br
                    pe.matmul(o, vsw[:, 0, vcol], pT[:, p0:p0 + T], start=(br == 0), stop=False)
                    pe.matmul(o[:, P:T], vsw[:, 1, vcol], pT[:, p0 + T:p0 + 384], start=False, stop=False)
                m = pe.matmul(o, vcs[0:NC_, g * HD:(g + 1) * HD], pT[0:NC_, 768:1024], start=False, stop=True)
                m.then_inc(S("onsa"), 1)
                pe.wait_ge(S("a_ready"), hh + 1)
                o = bank[3][r0:r0 + HD, T:2 * T]
                vcol = slice(hh * HD, (hh + 1) * HD)
                pe.matmul(o, vsb[:, 0, vcol], sbt[:, 4, 0:T], start=True, stop=False)
                m = pe.matmul(o[:, P:T], vsb[:, 1, vcol], sbt[:, 4, T:384], start=False, stop=True)
                m.then_inc(S("osb"), 1)

            pe.wait_ge(S("gate_exp"), 16)
            def branch(i):
                n = branch_tile(i)
                if i == 0:
                    pe.wait_ge(S("masked"), NH)
                if i >= 2:
                    pe.wait_ge(S("mrg_read"), i - 1)
                need(n)
                s = n % SPLIT
                for br in range(2):
                    if i == 0:
                        pe.wait_ge(S("oT_split"), br + 1)
                    out = bank[4 + i % 2][:, br * T:(br + 1) * T]
                    for k in range(4):
                        c0 = (br * 4 + k) * P
                        wh, wl = hi[:, s, c0:c0 + P], lo[:, s, c0:c0 + P]
                        pe.matmul(out, wh, xhi[:, 4 * br + k, :], start=(k == 0), stop=False)
                        pe.matmul(out, wh, xlo[:, 4 * br + k, :], start=False, stop=False)
                        m = pe.matmul(out, wl, xhi[:, 4 * br + k, :], start=False, stop=(k == 3))
                m.then_inc(tile_used, 1)

            branch(0)
            for i in range(8):
                if i + 1 < 8:
                    branch(i + 1)
                n = out_tile(i)
                need(n)
                pe.wait_ge(S("mrg_split"), i + 1)
                if i == 0:
                    pe.wait_ge(S("osb_out"), NH)
                s = n % SPLIT
                for b in range(TB):
                    c0 = (i % 2) * T + b * P
                    mh, ml = auxh[:, c0:c0 + P], auxl[:, c0:c0 + P]
                    for st_, (a_, w_) in enumerate(((mh, hi), (mh, lo), (ml, hi))):
                        for f in range(2):
                            m = pe.matmul(bank[2 * b + f][:, :], a_, w_[:, s, f * 512:(f + 1) * 512],
                                          start=(i == 0 and st_ == 0), stop=(i == 7 and st_ == 2))
                m.then_inc(tile_used, 1)

            def key_scores(j):
                pe.wait_ge(S("bank45_read"), j + 1)
                if j >= 2:
                    pe.wait_ge(S("sc_out"), j - 1)
                for p_ in range(2):
                    for b in range(TB):
                        c0 = p_ * T + b * P
                        m = pe.matmul(bank[6 + j % 2][:, c0:c0 + P], qst[:, j % 2, c0:c0 + P],
                                      pv("subk")[:, p_ * P:(p_ + 1) * P], start=True, stop=True)
                m.then_inc(S("key_scores"), 1)

            pe.wait_ge(S("xs_ready"), 2)
            pe.wait_ge(S("mrg_read"), 8)
            transpose_x(1)
            pe.wait_ge(S("xlo_ready"), 2 * KT)
            for i in range(NH):
                if i >= 2:
                    pe.wait_ge(S("bank45_read"), i - 1)
                for p_ in range(2):
                    tposed(T_WQ + 2 * i + p_, bank[4 + i % 2][:, p_ * T:(p_ + 1) * T])
                if i >= 1:
                    key_scores(i - 1)
            key_scores(NH - 1)

            V0 = N_PRE + NBLK

            def loop_need(i, n):
                pe.wait_ge(hi_done, i * UNROLL + splits(n + 1))
                pe.wait_ge(lo_done, i * UNROLL + splits(n + 1))

            def u_tile(i, j, base):
                n, pair = N_PRE + base + j, (base + j) // 2
                if (base + j) % 2 == 0:
                    pe.wait_ge(S("bank45_read"), i * (UNROLL // 2) + (pair + NH - 2))
                loop_need(i, n)
                s = n % SPLIT
                out = u_bank[pair % 3][:, ((base + j) % 2) * T:((base + j) % 2 + 1) * T]
                for k in range(KT):
                    wh, wl = hi[:, s, k * P:(k + 1) * P], lo[:, s, k * P:(k + 1) * P]
                    pe.matmul(out, wh, xhi[:, k, :], start=(k == 0), stop=False)
                    pe.matmul(out, wh, xlo[:, k, :], start=False, stop=False)
                    m = pe.matmul(out, wl, xhi[:, k, :], start=False, stop=(k == KT - 1))
                m.then_inc(tile_used, 1)

            def g_group(i, j, base):
                g = base + j
                pe.wait_ge(S("oneA_ready"), i * UNROLL + (g + 1))
                pe.wait_ge(S("oneB_ready"), i * UNROLL + (g + 1))
                pe.wait_ge(S("bank67_read"), i * UNROLL + (g + 1))
                for t in range(4):
                    m = pe.matmul(bank[6 + g % 2][:, 2 * t * HALF:2 * (t + 1) * HALF], oneB[:, g % 2, t, :],
                                  oneA[:, g % 2, t, :, :], start=True, stop=True)
                m.then_inc(S("g_ready"), 1)

            pe.wait_ge(S("bank45_read"), NH)
            each_tile(pe, U1, lambda i, j: u_tile(i, j, 0))
            pe.wait_ge(S("router"), 1)
            for w, src in enumerate((i1f, i2f, gwt)):
                for b in range(TB):
                    m = pe.transpose(bank[6 + w // 2][:, (w % 2) * T + b * P:(w % 2) * T + (b + 1) * P],
                                     src[:, b * P:(b + 1) * P], ident)
            m.then_inc(S("routerT"), 1)

            def u_and_g(i, j):
                u_tile(i, j, U1)
                g_group(i, j, 0)

            each_tile(pe, NBLK - U1, u_and_g)
            for g in range(NBLK - U1, NGRP):
                g_group(0, 0, g)

            def v_tile(i, j, base, first=False, last=False):
                n = V0 + base + j
                s = n % SPLIT
                loop_need(i, n)
                pe.wait_ge(S("wlo_done"), i * UNROLL + (base + j + 1))
                for b in range(TB):
                    c0 = s * T + b * P
                    wh, wl = auxh[:, c0:c0 + P], auxl[:, c0:c0 + P]
                    for st_, (a_, w_) in enumerate(((wh, hi), (wh, lo), (wl, hi))):
                        for f in range(2):
                            m = pe.matmul(bank[2 * b + f][:, :], a_, w_[:, s, f * 512:(f + 1) * 512],
                                          start=(first and st_ == 0), stop=(last and st_ == 2),
                                          skip_group_check=True)
                m.then_inc(tile_used, 1)

            def v_and_g(i, j):
                v_tile(i, j, 1)
                g_group(i, j, NGRP + 1)

            v_tile(0, 0, 0, first=True)
            g_group(0, 0, NGRP)
            each_tile(pe, HALF - 1, v_and_g)
            each_tile(pe, HALF - 1, lambda i, j: v_tile(i, j, HALF))
            v_tile(0, 0, NBLK - 1, last=True)

        @block.scalar
        def _(act):
            own = [0]

            def link(ins):
                own[0] += 1
                ins.then_inc(act_step, 1)
                act.wait_ge(act_step, own[0])

            def split_hi(n):
                act.wait_ge(loaded[n % RING], 16 * (n // RING + 1))
                if n >= SPLIT:
                    act.wait_ge(tile_used, slot_user(n) + 1)
                act.activation(hi[:, n % SPLIT, :], raw[:, n % RING, :], ACT.Copy).then_inc(hi_done, 1)

            def squares(b, first):
                act.activation(xs[:, b, :], h[:, b, :], ACT.Square, accum_out=st[:, b:b + 1]).then_inc(S("sq"), 1)

            def rstd(u, v):
                act.wait_ge(S("var"), u)
                link(act.activation(v, v, ACT.Ln))
                act.activation(v, v, ACT.Exp, scale=-0.5).then_inc(S("rs"), 1)

            def x_hi(k, which):
                act.wait_ge(S("xT_ready"), (which * KT + k) // 2 + 1)
                act.activation(xhi[:, k, :], bank[4 + k // 2][:, (k % 2) * T:(k % 2 + 1) * T], ACT.Copy,
                               scale=pv("g1" if which == 0 else "g2")[:, k:k + 1]).then_inc(S("xhi_ready"), 1)

            LN_EXP, GELU = "natural_log_exp_and_others", "gelu_apprx_tanh_and_others"
            act.preload_act_table_set(LN_EXP)
            act.wait_ge(x_in, 16)
            squares(0, True)
            squares(1, True)
            act.wait_ge(small_in, 48)
            act.activation(gwh, pv("gw"), ACT.Copy).then_inc(S("gw_hi"), 1)
            split_hi(0)
            rstd(1, st[:, 8:10])
            split_hi(1)
            split_hi(2)
            for k in range(KT):
                x_hi(k, 0)
            for n in range(3, 9):
                split_hi(n)
            act.wait_ge(tile_used, T_KV + 4)
            for b in range(TB):
                m = act.activation(nrm_a[:, b * T:(b + 1) * T], bank[6 + b][:, 0:T], ACT.Square)
            m.then_inc(S("sqk"), 1)
            for b in range(TB):
                m = act.activation(vsw[:, b, :], bank[6 + b][:, T:512], ACT.Copy)
            m.then_inc(S("vsw"), 1)
            act.wait_ge(S("gn_ready"), 1)
            act.activation(gexpT, bank[2][0:24, 0:T], ACT.Exp, scale=-1.0).then_inc(S("gn_exp"), 1)
            split_hi(9)
            rstd(2, st[:, 16:24])
            act.wait_ge(tile_used, T_Q + 4)
            act.wait_ge(S("krot"), 1)
            for b in range(TB):
                m = act.activation(nrm_a[:, 0:512] if b == 0 else nrm_q, bank[4 + b][:, :], ACT.Square)
            m.then_inc(S("sqk"), 1)
            rstd(3, st[:, 32:48])
            act.preload_act_table_set(GELU)
            for w in range(2):
                act.wait_ge(tile_used, T_W1K + 4 * w + 4)
                act.activation(hidn[:, w * CH:(w + 1) * CH], bank[1 + w][0:30, 0:CH],
                               ACT.Gelu_apprx_tanh).then_inc(S("hid"), 1)
                if w == 0:
                    split_hi(18)
            split_hi(19)
            act.preload_act_table_set(LN_EXP)
            split_hi(20)
            act.wait_ge(S("hidT_ready"), 1)
            act.activation(ghid.rearrange("p (z c) -> p z c", z=4),
                           bank[1][:, CH:CH + P].rearrange("p (z c) -> p z c", z=4)[:, :, 0:30],
                           ACT.Copy).then_inc(S("ghid"), 1)
            split_hi(21)
            split_hi(22)

            def qksb_out(i):
                act.wait_ge(tile_used, T_QSB + 2 * i + 2)
                dst = (qsbT if i < 2 else ksbT)[:, 2 * (i % 2):2 * (i % 2) + 2, :]
                act.activation(dst, bank[(0, 3)[i % 2]][:, :].rearrange("p (a t) -> p a t", a=2), ACT.Copy,
                               scale=SCALE if i < 2 else 1.0).then_inc(S("qksb_out"), 1)

            qksb_out(0)
            split_hi(23)
            split_hi(24)
            act.wait_ge(S("cmp_ready"), 1)
            act.activation(nrm_c[0:NC_, :], bank[1][0:NC_, P:2 * P], ACT.Square).then_inc(S("sqk"), 1)
            act.activation(vcs[0:NC_, :], bank[1][0:NC_, 2 * P:3 * P], ACT.Copy).then_inc(S("vc_out"), 1)
            qksb_out(1)
            rstd(4, st[0:NC_, 24:26])
            split_hi(25)
            split_hi(26)
            qksb_out(2)
            split_hi(27)
            split_hi(28)
            qksb_out(3)
            act.wait_ge(S("kT_ready"), 1)
            for s in range(2):
                m = act.activation(kT[:, 2 * s:2 * s + 2, :], bank[6 + s][:, :].rearrange("p (a t) -> p a t", a=2), ACT.Copy)
            m.then_inc(S("qkT_out"), 1)
            act.wait_ge(S("kcT_ready"), 1)
            act.activation(kcT[:, :, 0:NC_], bank[1][:, 400:432].rearrange("p (g c) -> p g c", g=2)[:, :, 0:NC_],
                           ACT.Copy).then_inc(S("kcT_out"), 1)
            for n in range(29, 33):
                split_hi(n)
            act.wait_ge(tile_used, T_VSB + 4)
            act.activation(vsb[:, 0, :], bank[2][:, :], ACT.Copy).then_inc(S("vsb_out"), 1)
            act.activation(vsb[:, 1, :], bank[1][:, :], ACT.Copy).then_inc(S("vsb_out"), 1)
            act.wait_ge(S("qT_ready"), 1)
            for s in range(2):
                act.activation(qT[:, 2 * s:2 * s + 2, :], bank[4 + s][:, :].rearrange("p (a t) -> p a t", a=2),
                               ACT.Copy).then_inc(S("qkT_out"), 1)

            def softplus(hh):
                act.wait_ge(S("z_ready"), hh + 1)
                if hh:
                    act.wait_ge(S("z_read"), hh)
                sp_ = sbt[:, 2, :]
                link(act.activation(sp_, bank[2][:, 0:384], ACT.Abs))
                link(act.activation(sp_, sp_, ACT.Exp, scale=-1.0))
                act.activation(sp_, sp_, ACT.Ln, bias=1.0).then_inc(S("softplus"), 1)

            def gate_exp(g):
                act.wait_ge(tile_used, T_GATE + g + 1)
                act.activation(gates[:, g, :], bank[g % 2][:, 0:T], ACT.Exp,
                               scale=-1.0).then_inc(S("gate_exp"), 1)

            softplus(0)
            for hh in range(NH):
                q, r0, a = hh % 2, 64 * (hh % 2), hh // 2
                act.wait_ge(S("negmax"), hh + 1)
                for c, (c0, w_) in enumerate(((0, P), (P, T), (414, P), (414 + P, T), (384, NC_), (384 + NC_, NC_))):
                    x_ = sm[:, q, c0:c0 + w_]
                    m = act.activation(x_, x_, ACT.Exp, bias=att[:, q, 6 + c:7 + c], scale=SCALE,
                                       accum_out=att[:, q, 12 + c:13 + c])
                m.then_inc(S("exped"), 1)
                split_hi(T_GATE + 2 * hh + 3)
                act.wait_ge(S("pT"), hh + 1)
                if hh:
                    act.wait_ge(S("onsa"), hh)
                for br in range(2):
                    act.activation(pT[:, 384 * br:384 * (br + 1)], bank[6 + br][:, 0:384],
                                   ACT.Copy).then_inc(S("pT_out"), 1)
                act.wait_ge(S("x_ready"), hh + 1)
                act.activation(sbt[:, 0, :], sbt[:, 0, :], ACT.Exp).then_inc(S("x_exp"), 1)
                gate_exp(2 * hh)
                if hh + 1 < NH:
                    softplus(hh + 1)
                split_hi(T_GATE + 2 * hh + 4)
                gate_exp(2 * hh + 1)
                act.wait_ge(S("osb"), hh + 1)
                act.activation(oT.rearrange("p (k a) t -> p k a t", k=2)[r0:r0 + HD, :, a, :],
                               bank[3][r0:r0 + HD, :].rearrange("p (k t) -> p k t", k=2), ACT.Copy).then_inc(S("osb_out"), 1)
            act.wait_ge(S("osb_out"), NH)
            act.wait_ge(tile_used, T_GATE + 16)
            for br in range(2):
                act.activation(xhi[:, 4 * br:4 * br + 4, :], oT[:, 4 * br:4 * br + 4, :], ACT.Copy).then_inc(S("oT_hi"), 1)

            def gate_sigmoid(i):
                two = gates.rearrange("p (r a) t -> p r a t", r=2)[:, :, i, :]
                link(act.activation(two, two, ACT.Ln, bias=1.0))
                act.activation(two, two, ACT.Exp, scale=-1.0).then_inc(S("gate_sig"), 1)

            gate_sigmoid(0)
            for i in range(8):
                act.wait_ge(S("merged"), i + 1)
                if i >= 2:
                    act.wait_ge(tile_used, out_tile(i - 2) + 1)
                act.activation(auxh[:, (i % 2) * T:(i % 2 + 1) * T], mrg[:, i % 2, 512:768],
                               ACT.Copy).then_inc(S("mrg_hi"), 1)
                for n in mix_splits(i)[:2]:
                    split_hi(n)
                if i + 1 < 8:
                    gate_sigmoid(i + 1)
            split_hi(mix_splits(7)[2])
            for b in range(TB):
                act.wait_ge(S("h_ready"), b + 1)
                squares(b, False)
            rstd(5, st[:, 8:10])
            for k in range(KT):
                x_hi(k, 1)
            for i in range(NH):
                split_hi(T_WQ + 2 * i + 3)
                split_hi(T_WQ + 2 * i + 4)
                if i >= 2:
                    act.wait_ge(S("key_scores"), i - 1)
                act.activation(qst[:, i % 2, :], bank[4 + i % 2][:, :], ACT.Copy).then_inc(S("bank45_read"), 1)

            V0 = N_PRE + NBLK

            def loop_hi(i, n):
                act.wait_ge(loaded[n % RING], i * (16 * (UNROLL // RING)) + 16 * (n // RING + 1))
                act.wait_ge(tile_used, i * UNROLL + (n - SPLIT + 1))
                act.activation(hi[:, n % SPLIT, :], raw[:, n % RING, :], ACT.Copy).then_inc(hi_done, 1)

            def gelu_pair(i, j, base):
                if (base + j) % 2:
                    act.wait_ge(tile_used, i * UNROLL + (N_PRE + base + j + 1))
                    act.activation(big[:, bass.ds(i * (UNROLL * T) + (base + j - 1) * T, 2 * T)],
                                   u_bank[(base + j) // 2 % 3][:, :], ACT.Gelu_apprx_tanh).then_inc(S("bank45_read"), 1)

            def one_hot_b(i, j, base):
                g = base + j
                act.wait_ge(S("dist"), i * UNROLL + (g + 1))
                B = oneB[:, g % 2, :, :].bitcast(F32)
                act.activation(oneB[:, g % 2, :, :], B, ACT.Square).then_inc(S("dist_sq"), 1)
                act.wait_ge(S("dist_sq"), i * UNROLL + (g + 1))
                act.activation(oneB[:, g % 2, :, :], B, ACT.Relu, bias=1.0,
                               scale=-1.0).then_inc(S("oneB_ready"), 1)

            def w_hi(i, b):
                s = (V0 + b) % SPLIT
                act.activation(auxh[:, s * T:(s + 1) * T], big[:, bass.ds(i * (UNROLL * T) + b * T, T)],
                               ACT.Copy).then_inc(S("whi_done"), 1)

            def u_step(i, j):
                loop_hi(i, N_PRE + j + SPLIT)
                gelu_pair(i, j, 0)

            def u_step_g(i, j):
                one_hot_b(i, j, 0)
                loop_hi(i, N_PRE + U1 + j + SPLIT)
                gelu_pair(i, j, U1)

            act.preload_act_table_set(GELU)
            act.wait_ge(S("h_saved"), 16 * TB)
            each_tile(act, U1 - 2, u_step)
            act.preload_act_table_set(LN_EXP)
            act.wait_ge(S("router_d"), 1)
            act.activation(gwt, gwt, ACT.Exp).then_inc(S("router_exp"), 1)
            act.preload_act_table_set(GELU)
            for j in range(U1 - 2, U1):
                u_step(0, j)
            act.wait_ge(S("bank67_read"), 2)
            act.activation(gw2[:, :, 0], eT[:, 2, :], ACT.Copy).then_inc(S("gw2_hi"), 1)
            each_tile(act, NBLK - U1, u_step_g)
            for g in range(NBLK - U1, NGRP):
                one_hot_b(0, 0, g)

            act.wait_ge(S("weighed"), 1 + NGRP)
            for b in range(SPLIT):
                w_hi(0, b)

            def v_step(i, j):
                loop_hi(i, V0 + HALF + j + SPLIT)
                w_hi(i, HALF + j + SPLIT)

            def v_step_g(i, j):
                one_hot_b(i, j, NGRP)
                loop_hi(i, V0 + j + SPLIT)
                w_hi(i, j + SPLIT)

            each_tile(act, HALF - SPLIT, v_step_g)
            for j in range(HALF - SPLIT, HALF):
                one_hot_b(0, j, NGRP)
                loop_hi(0, V0 + j + SPLIT)
            act.wait_ge(S("weighed"), 1 + 2 * NGRP)
            for b in range(HALF, HALF + SPLIT):
                w_hi(0, b)
            each_tile(act, HALF - SPLIT, v_step)

        @block.vector
        def _(dve):
            own = [0]

            def link(ins):
                own[0] += 1
                ins.then_inc(dve_step, 1)
                dve.wait_ge(dve_step, own[0])

            def split_lo(n):
                dve.wait_ge(hi_done, splits(n + 1))
                dve.tensor_tensor(lo[:, n % SPLIT, :], raw[:, n % RING, :], hi[:, n % SPLIT, :].bitcast(F32),
                                  ALU.subtract).then_inc(lo_done, 1)

            def sharpen(v, y, t):
                link(dve.tensor_tensor(t, y, y, ALU.mult))
                link(dve.tensor_tensor(t, t, v, ALU.mult))
                link(dve.tensor_scalar(t, t, -0.5, 1.5, ALU.mult, ALU.add))
                link(dve.tensor_tensor(y, y, t, ALU.mult))

            def var(ssq, v, y, n):
                link(dve.tensor_scalar(v, ssq, 1.0 / n, EPS, ALU.mult, ALU.add))
                dve.tensor_copy(y, v).then_inc(S("var"), 1)

            def norm_x(which):
                dve.wait_ge(S("sq"), 2 * which + 2)
                if which:
                    dve.wait_ge(S("xlo_ready"), KT)
                var(st[:, 0:2], st[:, 2:4], st[:, 8:10], D)
                dve.wait_ge(S("rs"), 1 if which == 0 else 5)
                sharpen(st[:, 2:4], st[:, 8:10], st[:, 4:6])
                for b in range(TB):
                    m = dve.tensor_scalar(xs[:, b, 0:P], ident, st[:, 8 + b:9 + b], None, ALU.mult)
                m.then_inc(S("xs_ready"), 1)

            def x_lo(k, which):
                dve.wait_ge(S("xhi_ready"), which * KT + 2 * (k // 2) + 2)
                dve.scalar_tensor_tensor(xlo[:, k, :], bank[4 + k // 2][:, (k % 2) * T:(k % 2 + 1) * T],
                                         pv("g1" if which == 0 else "g2")[:, k:k + 1],
                                         xhi[:, k, :].bitcast(F32), ALU.mult, ALU.subtract).then_inc(S("xlo_ready"), 1)

            dve.wait_ge(small_in, 48)
            norm_x(0)
            split_lo(0)
            for k in range(KT):
                x_lo(k, 0)
            for n in range(1, 4):
                split_lo(n)
            dve.wait_ge(S("gw_hi"), 1)
            dve.tensor_tensor(gwl, pv("gw"), gwh.bitcast(F32), ALU.subtract).then_inc(S("gw_split"), 1)
            cosT = cv_("cos").rearrange("p (b d) -> p b d", b=2)
            sinT = cv_("sin").rearrange("p (b d) -> p b d", b=2)
            for b in range(TB):
                for dst_c, dst_s, g_ in [(gcq[:, b, :], gsq[:, b, :], pv("qg"))] + [
                        (gck[:, b, s, :], gsk[:, b, s, :], pv("kgs")[:, s * HD:(s + 1) * HD]) for s in range(2)]:
                    dve.tensor_tensor(dst_c, cosT[:, b, :], g_, ALU.mult)
                    dve.tensor_tensor(dst_s[:, 0:32], sinT[:, b, 0:32], g_[:, 32:64], ALU.mult)
                    dve.tensor_tensor(dst_s[:, 32:64], sinT[:, b, 32:64], g_[:, 0:32], ALU.mult)
                split_lo(4 + b)
            dve.tensor_tensor(gcc, cv_("cosc"), pv("kgc"), ALU.mult)
            dve.tensor_tensor(gsc[:, 0:32], cv_("sinc")[:, 0:32], pv("kgc")[:, 32:64], ALU.mult)
            link(dve.tensor_tensor(gsc[:, 32:64], cv_("sinc")[:, 32:64], pv("kgc")[:, 0:32], ALU.mult))
            tok = stok.rearrange("p (w j g c) -> p w j g c", w=2, j=16, g=2)
            for w in range(2):
                dve.wait_ge(tile_used, w + 1)
                pos = pv("posk" if w == 0 else "posv")
                for g in range(NG):
                    for l2 in range(2):
                        src = bank[3 * w][g * HD:(g + 1) * HD, l2:T]
                        win = bass.AP(src.tensor, src.offset, [list(src.ap[0]), [2, 16], [16, NC_]])
                        r = slice(l2 * HD, (l2 + 1) * HD)
                        m = dve.tensor_tensor(tok[r, w, :, g, :], win,
                                              pos[r, :].unsqueeze(2).broadcast_to([HD, 16, NC_]), ALU.add)
                if w:
                    m.then_inc(S("tok"), 1)
                split_lo(6 + w)
            split_lo(8)

            def rotate(p_, n, a_, b_, src, y, gc, gs, outs, done):
                nh = src.shape[1]
                yb = y.unsqueeze(2).broadcast_to([p_, nh, HD])
                link(dve.tensor_tensor(n, src, yb, ALU.mult))
                dve.tensor_tensor(a_, n, gc, ALU.mult)
                dve.tensor_tensor(b_[:, :, 0:32], n[:, :, 32:64], gs[:, :, 0:32], ALU.mult)
                link(dve.tensor_tensor(b_[:, :, 32:64], n[:, :, 0:32], gs[:, :, 32:64], ALU.mult))
                for k, o in enumerate(outs):
                    m = dve.tensor_tensor(o, a_, b_, ALU.add)
                if done is None:
                    link(m)
                else:
                    m.then_inc(done, 1)

            def heads(ap_, nh):
                return ap_.rearrange("p (a d) -> p a d", a=nh)

            def per_slot(tab, p_, rep):
                return tab.unsqueeze(2).broadcast_to([p_, tab.shape[1], rep, HD])

            dve.wait_ge(S("sqk"), 1)
            link(dve.tensor_reduce(st[:, 48:56], heads(nrm_a, 8), AXX, ALU.add))
            var(st[:, 48:56], st[:, 48:56], st[:, 16:24], HD)
            split_lo(9)
            dve.wait_ge(S("rs"), 2)
            sharpen(st[:, 48:56], st[:, 16:24], st[:, 56:64])
            for b in range(TB):
                n, a_, b_ = (heads(z[:, 0:T], 4) for z in (nrm_n, nrm_q, nrm_b))
                yb = st[:, 16 + 4 * b:20 + 4 * b].unsqueeze(2).broadcast_to([P, 4, HD])
                link(dve.tensor_tensor(n, heads(bank[6 + b][:, 0:T], 4), yb, ALU.mult))
                for s in range(2):
                    gc = gck[:, b, s, :].unsqueeze(1).broadcast_to([P, 2, HD])
                    gs = gsk[:, b, s, :].unsqueeze(1).broadcast_to([P, 2, HD])
                    two = slice(2 * s, 2 * s + 2)
                    dve.tensor_tensor(a_[:, two, :], n[:, two, :], gc, ALU.mult)
                    dve.tensor_tensor(b_[:, two, 0:32], n[:, two, 32:64], gs[:, :, 0:32], ALU.mult)
                    m = dve.tensor_tensor(b_[:, two, 32:64], n[:, two, 0:32], gs[:, :, 32:64], ALU.mult)
                link(m)
                for d_ in range(2):
                    m = dve.tensor_tensor(krdup[:, b, :, d_ * HD:(d_ + 1) * HD], a_, b_, ALU.add)
                if b:
                    m.then_inc(S("krot"), 1)
                else:
                    link(m)
            dve.wait_ge(S("krot"), 1)
            dve.wait_ge(S("sqk"), 2)
            dve.tensor_reduce(st[:, 48:56], heads(nrm_a, 8), AXX, ALU.add)
            link(dve.tensor_reduce(st[:, 56:64], heads(nrm_q, 8), AXX, ALU.add))
            var(st[:, 48:64], st[:, 48:64], st[:, 32:48], HD)
            dve.wait_ge(S("gnT_ready"), 1)
            link(dve.tensor_scalar(gsig.rearrange("p (b c) -> p b c", b=2),
                                   bank[3][:, 0:64].rearrange("p (b c) -> p b c", b=2)[:, :, 0:24], 1.0, None, ALU.add))
            link(dve.reciprocal(gsig, gsig))
            gsv = gsig.rearrange("p (b r h) -> p b r h", b=2, r=3)
            for br, c0 in ((1, 0), (2, 2), (0, 4)):
                m = dve.tensor_copy(ggate[:, :, c0:c0 + 2], gsv[:, :, br, :].rearrange("p b h -> p h b"))
            link(m)
            dve.tensor_scalar(ggate[:, :, 4:5], ggate[:, :, 4:5], cv_("hasc"), None, ALU.mult).then_inc(S("gates_n"), 1)
            dve.wait_ge(S("rs"), 3)
            sharpen(st[:, 48:64], st[:, 32:48], st[:, 0:16])
            for b in range(TB):
                n, a_, b_ = (heads(z, 8) for z in (nrm_n, nrm_a, nrm_b))
                rotate(P, n, a_, b_, heads(bank[4 + b][:, :], 8), st[:, 32 + 8 * b:40 + 8 * b],
                       gcq[:, b, :].unsqueeze(1).broadcast_to([P, 8, HD]),
                       gsq[:, b, :].unsqueeze(1).broadcast_to([P, 8, HD]),
                       [heads(qrot[:, b, :], 8)], S("qrot") if b else None)
            dve.wait_ge(S("qrot"), 1)
            for n in range(18, 25):
                split_lo(n)
            dve.wait_ge(S("sqk"), 3)
            link(dve.tensor_reduce(st[0:NC_, 26:28], heads(nrm_c[0:NC_, :], 2), AXX, ALU.add))
            var(st[0:NC_, 26:28], st[0:NC_, 26:28], st[0:NC_, 24:26], HD)
            dve.wait_ge(S("rs"), 4)
            sharpen(st[0:NC_, 26:28], st[0:NC_, 24:26], st[0:NC_, 28:30])
            n, a_, b_ = (heads(z[0:NC_, 0:P], 2) for z in (nrm_n, nrm_q, nrm_b))
            kd = kcd[0:NC_, :].rearrange("p (g c) -> p g c", g=2)
            rotate(NC_, n, a_, b_, heads(bank[1][0:NC_, P:2 * P], 2), st[0:NC_, 24:26],
                   gcc[0:NC_, :].unsqueeze(1).broadcast_to([NC_, 2, HD]),
                   gsc[0:NC_, :].unsqueeze(1).broadcast_to([NC_, 2, HD]),
                   [kd[:, :, 0:HD], kd[:, :, HD:2 * HD]], S("kcrot"))
            dve.wait_ge(S("kcrot"), 1)
            dve.wait_ge(S("gates_n"), 1)
            for n in range(25, 33):
                split_lo(n)

            def mask_scores(hh):
                q = hh % 2
                dve.wait_ge(S("scores"), hh + 1)
                if hh >= 2:
                    dve.wait_ge(S("cmpT"), hh - 1)
                dve.tensor_tensor(sm[:, q, 0:414], bank[4][:, 0:414], cv_("mask"), ALU.add)
                dve.tensor_tensor(sm[:, q, 414:798], bank[5][:, 0:384], cv_("mask")[:, 0:384],
                                  ALU.add).then_inc(S("masked"), 1)
                dve.wait_ge(S("masked"), hh + 1)
                both = sm[:, q, :].rearrange("p (r c) -> p r c", c=414)
                mx = att[:, q, 0:4].rearrange("p (r b) -> p r b", b=2)
                dve.tensor_reduce(mx[:, :, 0:1], both[:, :, 0:P], AXX, ALU.max)
                dve.tensor_reduce(mx[:, :, 1:2], both[:, :, P:384], AXX, ALU.max)
                link(dve.tensor_reduce(att[:, q, 4:6], sm[:, q, 384:414].rearrange("p (b c) -> p b c", b=2), AXX, ALU.max))
                dve.tensor_scalar(att[:, q, 6:12], att[:, q, 0:6], -SCALE, None, ALU.mult).then_inc(S("negmax"), 1)

            def stick_logs(hh):
                dve.wait_ge(S("softplus"), hh + 1)
                if hh:
                    dve.wait_ge(S("a_ready"), hh)
                dve.scalar_tensor_tensor(sbt[:, 0, :], bank[2][:, 0:384], 0.0, sbt[:, 2, :], ALU.max, ALU.add)
                dve.scalar_tensor_tensor(sbt[:, 3, :], bank[2][:, 0:384], 0.0, sbt[:, 2, :], ALU.min,
                                         ALU.subtract).then_inc(S("z_read"), 1)

            mask_scores(0)
            stick_logs(0)
            for hh in range(NH):
                q = hh % 2
                dve.wait_ge(S("exped"), hh + 1)
                link(dve.reciprocal(att[:, q, 18:24], att[:, q, 12:18]))
                link(dve.tensor_tensor(att[:, q, 18:24], att[:, q, 18:24], ggate[:, hh, :], ALU.mult))
                for c, (c0, w_) in enumerate(((0, P), (P, T), (414, P), (414 + P, T), (384, NC_), (384 + NC_, NC_))):
                    x_ = sm[:, q, c0:c0 + w_]
                    m = dve.tensor_scalar(x_, x_, att[:, q, 18 + c:19 + c], None, ALU.mult)
                m.then_inc(S("probs"), 1)
                split_lo(T_GATE + 2 * hh + 3)
                dve.wait_ge(S("cmpT"), hh + 1)
                if hh:
                    dve.wait_ge(S("onsa"), hh)
                dve.tensor_copy(pT[0:NC_, 768:1024], bank[3][0:NC_, 0:T]).then_inc(S("cmpT_out"), 1)
                dve.wait_ge(S("after"), hh + 1)
                dve.tensor_tensor(sbt[:, 0, :], sbt[:, 3, :], bank[2][:, 0:384], ALU.add).then_inc(S("x_ready"), 1)
                if hh + 1 < NH:
                    mask_scores(hh + 1)
                    stick_logs(hh + 1)
                split_lo(T_GATE + 2 * hh + 4)
            for br in range(2):
                dve.wait_ge(S("oT_hi"), br + 1)
                dve.tensor_tensor(xlo[:, 4 * br:4 * br + 4, :], oT[:, 4 * br:4 * br + 4, :],
                                  xhi[:, 4 * br:4 * br + 4, :].bitcast(F32), ALU.subtract).then_inc(S("oT_split"), 1)
            for i in range(8):
                q = i % 2
                dve.wait_ge(S("gate_sig"), i + 1)
                dve.wait_ge(tile_used, branch_tile(i) + 1)
                if i >= 2:
                    dve.wait_ge(S("mrg_hi"), i - 1)
                ab = mrg[:, q, 0:512].rearrange("p (r t) -> p r t", r=2)
                gate = gates.rearrange("p (r a) t -> p r a t", r=2)[:, :, i, :]
                dve.tensor_tensor(ab, bank[4 + q][:, :].rearrange("p (r t) -> p r t", r=2), gate,
                                  ALU.mult).then_inc(S("mrg_read"), 1)
                dve.wait_ge(S("mrg_read"), i + 1)
                dve.tensor_tensor(mrg[:, q, 512:768], mrg[:, q, 0:T], mrg[:, q, T:512], ALU.add).then_inc(S("merged"), 1)
                dve.wait_ge(S("mrg_hi"), i + 1)
                dve.tensor_tensor(auxl[:, q * T:(q + 1) * T], mrg[:, q, 512:768],
                                  auxh[:, q * T:(q + 1) * T].bitcast(F32), ALU.subtract).then_inc(S("mrg_split"), 1)
                for n in mix_splits(i)[:2]:
                    split_lo(n)
            dve.wait_ge(tile_used, T_WQ)
            for b in range(TB):
                for f in range(2):
                    c = slice(f * 512, (f + 1) * 512)
                    m = dve.tensor_tensor(h[:, b, c], h[:, b, c], bank[2 * b + f][:, :], ALU.add)
                m.then_inc(S("h_ready"), 1)
            split_lo(mix_splits(7)[2])
            norm_x(1)
            for k in range(KT):
                x_lo(k, 1)

            def sc_out(j):
                dve.wait_ge(S("key_scores"), j + 1)
                dst = sc.rearrange("p (b h s k) -> p h s b k", b=2, h=8, s=2)[:, j]
                dve.tensor_copy(dst, bank[6 + j % 2][:, :].rearrange("p (s b k) -> p s b k", s=2, b=2)).then_inc(S("sc_out"), 1)

            for i in range(NH):
                split_lo(T_WQ + 2 * i + 3)
                split_lo(T_WQ + 2 * i + 4)
                if i:
                    sc_out(i - 1)
            sc_out(NH - 1)

            def loop_lo(i, n):
                dve.wait_ge(hi_done, i * UNROLL + splits(n + 1))
                dve.tensor_tensor(lo[:, n % SPLIT, :], raw[:, n % RING, :], hi[:, n % SPLIT, :].bitcast(F32),
                                  ALU.subtract).then_inc(lo_done, 1)

            def chains(ops):
                first = own[0]
                for k, op in enumerate(ops):
                    if k >= 2:
                        dve.wait_ge(dve_step, first + k - 1)
                    own[0] += 1
                    op().then_inc(dve_step, 1)
                dve.wait_ge(dve_step, own[0])

            def top16(pair, w_):
                ops = [lambda c=c, s_=s_, v_=v_: dve.max(v_[:, 0:8], s_) for c, (s_, v_) in enumerate(pair)]
                ops += [lambda c=c, s_=s_, v_=v_: dve.max_index(sti[c][:, 0:8], v_[:, 0:8], s_)
                        for c, (s_, v_) in enumerate(pair)]
                ops += [lambda c=c, s_=s_, v_=v_: dve.match_replace(stg2[c][:, 0:w_], v_[:, 0:8], s_, -3e38)
                        for c, (s_, v_) in enumerate(pair)]
                ops += [lambda c=c, v_=v_: dve.max(v_[:, 8:16], stg2[c][:, 0:w_]) for c, (s_, v_) in enumerate(pair)]
                ops += [lambda c=c, v_=v_: dve.max_index(sti[c][:, 8:16], v_[:, 8:16], stg2[c][:, 0:w_])
                        for c, (s_, v_) in enumerate(pair)]
                return ops

            nxt_tile = [0]

            def spread(upto):
                while nxt_tile[0] < upto:
                    loop_lo(0, N_PRE + nxt_tile[0] + SPLIT)
                    nxt_tile[0] += 1

            for c in range(16):
                k2 = [slice((2 * c + p_) * 16, (2 * c + p_ + 1) * 16) for p_ in range(2)]
                ops = top16([(sc[:, (2 * c + p_) * P:(2 * c + p_ + 1) * P], tkv[:, k2[p_]]) for p_ in range(2)], P)
                ops += [lambda p_=p_: dve.tensor_copy(tki[:, k2[p_]], sti[p_]) for p_ in range(2)]
                chains(ops)
                spread(TILES_KEYS * (c + 1) // 16)
            for c in range(0, 16, 2):
                cc = (c, c + 1)
                for x in range(2):
                    s1 = tkv[:, cc[x] * 32:cc[x] * 32 + 16].unsqueeze(2).broadcast_to([P, 16, 16])
                    s2 = tkv[:, cc[x] * 32 + 16:cc[x] * 32 + 32].unsqueeze(1).broadcast_to([P, 16, 16])
                    m = dve.tensor_tensor(stg[x].rearrange("p (a b) -> p a b", a=16), s1, s2, ALU.add)
                link(m)
                c16 = [slice(z * 16, z * 16 + 16) for z in cc]
                chains(top16([(stg[x], cval[:, c16[x]]) for x in range(2)], 256))
                spread(TILES_KEYS + (TILES_PAIRS * (c + 1)) // 16)
                for x in range(2):
                    dve.tensor_scalar(sta[x], sti[x], 4, None, ALU.logical_shift_right)
                    m = dve.tensor_scalar(stb[x], sti[x], 15, None, ALU.bitwise_and)
                link(m)
                for x in range(2):
                    dve.tensor_copy(caf[:, c16[x]], sta[x])
                    m = dve.tensor_copy(cbf[:, c16[x]], stb[x])
                link(m)
                spread(TILES_KEYS + (TILES_PAIRS * (c + 2)) // 16)
            places = iota16.unsqueeze(1).broadcast_to([P, 16, 16])
            eq = [z.rearrange("p (k a) -> p k a", k=16) for z in eqt]
            for c in range(16):
                c16 = slice(c * 16, c * 16 + 16)
                ops = []
                for side, pl in enumerate((caf, cbf)):
                    ops.append(lambda side=side, pl=pl: dve.tensor_tensor(
                        eq[side], places, pl[:, c16].unsqueeze(2).broadcast_to([P, 16, 16]), ALU.is_equal))
                for side in range(2):
                    ks_ = tki[:, c * 32 + 16 * side:c * 32 + 16 * side + 16].unsqueeze(1).broadcast_to([P, 16, 16])
                    ops.append(lambda side=side, ks_=ks_: dve.tensor_tensor(eq[side], eq[side], ks_, ALU.mult))
                for side, dst in enumerate((i1f, i2f)):
                    ops.append(lambda side=side, dst=dst: dve.tensor_reduce(dst[:, c16], eq[side], AXX, ALU.add))
                chains(ops)
                spread(TILES_KEYS + TILES_PAIRS + (TILES_NUMBERS * (c + 1)) // 16)
            cv3 = cval.rearrange("p (c k) -> p c k", k=16)
            g3 = gwt.rearrange("p (c k) -> p c k", k=16)
            dve.tensor_tensor(g3, cv3, cv3[:, :, 0:1].broadcast_to([P, 16, 16]), ALU.subtract).then_inc(S("router_d"), 1)
            dve.wait_ge(S("router_exp"), 1)
            link(dve.tensor_reduce(smx[:, 0:16], g3, AXX, ALU.add))
            link(dve.reciprocal(smx[:, 16:32], smx[:, 0:16]))
            dve.tensor_tensor(g3, g3, smx[:, 16:32].unsqueeze(2).broadcast_to([P, 16, 16]), ALU.mult).then_inc(S("router"), 1)
            spread(U1)
            dve.wait_ge(S("routerT"), 1)
            dve.tensor_copy(eT[:, 0:2, :], bank[6][:, :].rearrange("p (w t) -> p w t", w=2)).then_inc(S("bank67_read"), 1)
            dve.tensor_copy(eT[:, 2, :], bank[7][:, 0:T]).then_inc(S("bank67_read"), 1)
            dve.wait_ge(S("bank67_read"), 2)

            by_token = big[:, :].rearrange("p (e t) -> p t e", t=T)

            def keys_equal(i, j, base):
                g = base + j
                e0 = 0 if g < NGRP else HALF
                if g >= 2:
                    dve.wait_ge(S("oneA_ready"), i * UNROLL + (g - 1))
                i1 = eT[:, 0, bass.ds(i * (4 * UNROLL) + 4 * (g % NGRP), 4)].unsqueeze(2).broadcast_to([P, 4, HALF])
                dve.tensor_tensor(same[:, g % 2, :, :], iota[:, e0:e0 + HALF].unsqueeze(1).broadcast_to([P, 4, HALF]),
                                  i1, ALU.is_equal).then_inc(S("same"), 1)

            def rows_a(i, j, base):
                g = base + j
                dve.wait_ge(S("same"), i * UNROLL + (g + 1))
                eq_ = same[:, g % 2, :, :].unsqueeze(2).broadcast_to([P, 4, 2, HALF])
                w_ = gw2[:, bass.ds(i * (4 * UNROLL) + 4 * (g % NGRP), 4), :].bitcast(F32)
                dve.tensor_tensor(oneA[:, g % 2, :, :, :], eq_, w_.unsqueeze(3).broadcast_to([P, 4, 2, HALF]),
                                  ALU.mult).then_inc(S("oneA_ready"), 1)

            def add_parts(i, j, base):
                g = base + j
                dve.wait_ge(S("g_ready"), i * UNROLL + (g + 1))
                dve.wait_ge(S("weighed"), i * UNROLL + (g + 1))
                parts = bank[6 + g % 2][:, :].rearrange("p (t r e) -> p t e r", t=4, r=2)
                dve.tensor_reduce(gsum[:, :, :], parts, AXX, ALU.add).then_inc(S("bank67_read"), 1)

            def weigh(i, j, base):
                g = base + j
                e0 = 0 if g < NGRP else HALF
                dve.wait_ge(S("bank67_read"), i * UNROLL + (g + 3))
                w4 = by_token[:, bass.ds(i * (4 * UNROLL) + 4 * (g % NGRP), 4), e0:e0 + HALF]
                dve.tensor_tensor(w4, gsum[:, :, :], w4, ALU.mult).then_inc(S("weighed"), 1)

            dve.wait_ge(S("gw2_hi"), 1)
            link(dve.tensor_tensor(gw2[:, :, 1], eT[:, 2, :], gw2[:, :, 0].bitcast(F32), ALU.subtract))
            keys_equal(0, 0, 0)
            keys_equal(0, 1, 0)
            rows_a(0, 0, 0)
            keys_equal(0, 2, 0)
            rows_a(0, 1, 0)
            loop_lo(0, N_PRE + U1 + SPLIT)
            dve.wait_ge(S("bank45_read"), NH + HALF // 2)
            dve.tensor_copy(gsum[:, 0, 0:1], eT[:, 2, 0:1]).then_inc(S("weighed"), 1)

            def group_step(i, j, base, keys=True, rows=True):
                add_parts(i, j, base)
                if keys:
                    keys_equal(i, j, base + 3)
                weigh(i, j, base)
                if rows:
                    rows_a(i, j, base + 2)

            def u_step_g(i, j):
                group_step(i, j, 0)
                loop_lo(i, N_PRE + U1 + 1 + j + SPLIT)

            each_tile(dve, NBLK - U1 - 1, u_step_g)
            for g in range(NBLK - U1 - 1, NGRP):
                group_step(0, g, 0)

            V0 = N_PRE + NBLK
            loop_lo(0, V0 + SPLIT)
            dve.wait_ge(S("bank45_read"), NH + NBLK // 2)

            def v_step_g(i, j):
                group_step(i, j, NGRP)
                loop_lo(i, V0 + 1 + j + SPLIT)

            each_tile(dve, NGRP - 3, v_step_g)
            for j in range(NGRP - 3, NGRP):
                group_step(0, j, NGRP, keys=False, rows=j < NGRP - 2)
                if j < NGRP - 1:
                    loop_lo(0, V0 + 1 + j + SPLIT)
            each_tile(dve, HALF - SPLIT, lambda i, j: loop_lo(i, V0 + HALF + j + SPLIT))
            dve.wait_ge(tile_used, N_ALL)
            dve.wait_ge(S("h_back"), 16 * TB)
            for b in range(TB):
                for f in range(2):
                    c = slice(f * 512, (f + 1) * 512)
                    dve.tensor_tensor(h[:, b, c], h[:, b, c], bank[2 * b + f][:, :], ALU.add).then_inc(S("out_ready"), 1)

        @block.gpsimd
        def _(pool):
            for hh in range(NH):
                pool.wait_ge(S("z_read"), hh + 1)
                if hh:
                    pool.wait_ge(S("after"), hh)
                pool.tensor_tensor(sbt[:, 1, :], sbt[:, 0, :], cv_("msb"), ALU.mult).then_inc(S("l_masked"), 1)
                pool.wait_ge(S("x_exp"), hh + 1)
                if hh:
                    pool.wait_ge(S("osb"), hh)
                pool.tensor_tensor(sbt[:, 4, :], sbt[:, 0, :], cv_("msb"), ALU.mult).then_inc(S("a_ready"), 1)

            def distances(i, j, base):
                g = base + j
                if g >= 2:
                    pool.wait_ge(S("g_ready"), i * UNROLL + (g - 1))
                i2 = eT[:, 1, bass.ds(i * (4 * UNROLL) + 4 * (g % NGRP), 4)].unsqueeze(2).broadcast_to([P, 4, P])
                pool.tensor_tensor(oneB[:, g % 2, :, :], iota.unsqueeze(1).broadcast_to([P, 4, P]), i2,
                                   ALU.subtract).then_inc(S("dist"), 1)

            pool.wait_ge(S("bank67_read"), 2)
            distances(0, 0, 0)
            distances(0, 1, 0)
            each_tile(pool, NGRP - 2, lambda i, j: distances(i, j, 2))
            distances(0, 0, NGRP)
            distances(0, 1, NGRP)
            V0 = N_PRE + NBLK

            def w_lo(i, b):
                s = (V0 + b) % SPLIT
                pool.wait_ge(S("whi_done"), i * UNROLL + (b + 1))
                pool.tensor_tensor(auxl[:, s * T:(s + 1) * T], big[:, bass.ds(i * (UNROLL * T) + b * T, T)],
                                   auxh[:, s * T:(s + 1) * T].bitcast(F32), ALU.subtract).then_inc(S("wlo_done"), 1)

            def v_step_g(i, j):
                distances(i, j, NGRP + 2)
                w_lo(i, SPLIT + j)

            for b in range(SPLIT):
                w_lo(0, b)
            each_tile(pool, HALF - SPLIT, v_step_g)
            distances(0, HALF - 1, NGRP)
            for b in range(HALF, HALF + SPLIT):
                w_lo(0, b)
            each_tile(pool, HALF - SPLIT, lambda i, j: w_lo(i, HALF + SPLIT + j))

    return nc


def lay_out(a):
    f = np.float32
    win = a["w_in"][0]
    col = {}
    at = 0
    for name, n in (("q", 512), ("kc", 128), ("vc", 128), ("ks", 128), ("vs", 128), ("kw", 128), ("vw", 128),
                    ("gn", 24), ("qsb", 512), ("ksb", 512), ("vsb", 512), ("br", 2 * D)):
        col[name] = win[:, at:at + n]
        at += n
    assert at == win.shape[1]

    def stationary(w):
        return w.reshape(KT, P, -1, P).transpose(2, 1, 0, 3).reshape(-1, P, 1024)

    def moving(w):
        return w.reshape(4, 2, P, 512).transpose(0, 2, 1, 3).reshape(4, P, 1024)

    def compress(w):
        return w.reshape(4, 4, P, CH).transpose(0, 2, 1, 3).reshape(4, P, 1024)

    bn, bs, wo = a["w_branch_nsa"][0], a["w_branch_sb"][0], a["w_out"][0]
    both = np.concatenate([bn, bs], 0)
    br = stationary(both)
    wo = wo.reshape(8, P, D)
    mix = np.stack([br[0]] + [t for i in range(7) for t in (br[i + 1], wo[i])] + [wo[7]], 0)
    wpre = np.concatenate([
        stationary(col["kc"]), stationary(col["vc"]),
        moving(np.concatenate([col["ks"], col["kw"], col["vs"], col["vw"]], 1)), moving(col["q"]),
        compress(a["cmp_k_w1"][0]), compress(a["cmp_v_w1"][0]),
        stationary(col["qsb"]), stationary(col["ksb"]), moving(col["vsb"]), stationary(col["br"]),
        mix, stationary(a["peer_w_query"][0])], 0)
    assert wpre.shape[0] == N_PRE
    u = a["peer_u"][0].reshape(NBLK, P, KT, P).transpose(0, 3, 2, 1).reshape(NBLK, P, 1024)
    v = a["peer_v"][0].reshape(NBLK, P, D)

    par = np.zeros((P, NPAR), f)

    def put(name, x):
        at, n = PAR[name]
        par[:, at:at + n] = x

    put("g1", a["norm1_g"][0].reshape(KT, P).T)
    put("g2", a["norm2_g"][0].reshape(KT, P).T)
    put("qg", a["q_norm_g"][0][None])
    put("kgc", a["k_norm_g"][0, 0][None])
    put("kgs", a["k_norm_g"][0, 1:3].reshape(1, 128))
    put("posk", a["cmp_pos_k"][0].reshape(16, P).T)
    put("posv", a["cmp_pos_v"][0].reshape(16, P).T)
    put("w2k", a["cmp_k_w2"][0].reshape(2, P, HD).transpose(1, 0, 2).reshape(P, 128))
    put("w2v", a["cmp_v_w2"][0].reshape(2, P, HD).transpose(1, 0, 2).reshape(P, 128))
    put("subk", a["peer_subkeys"][0].transpose(2, 0, 1).reshape(P, 256))
    put("gw", col["gn"].reshape(KT, P, 24).transpose(1, 0, 2).reshape(P, 192))
    return np.ascontiguousarray(wpre), np.ascontiguousarray(u), np.ascontiguousarray(v), par


def constants():
    f = np.float32
    cst, kep = np.zeros((P, NCST), f), np.zeros((P, NKEP), f)

    def put(name, x):
        at, n = CST[name]
        cst[:, at:at + n] = x

    half = HD // 2
    freqs = (f(10000.0) ** (-np.arange(half, dtype=f) / f(half))).astype(f)

    def table(pos):
        ang = pos.astype(f)[:, None] * freqs[None]
        c, s = np.cos(ang).astype(f), np.sin(ang).astype(f)
        return np.concatenate([c, c], 1), np.concatenate([-s, s], 1)

    c, s = table(np.arange(T))
    put("cos", c.reshape(TB, P, HD).transpose(1, 0, 2).reshape(P, 128))
    put("sin", s.reshape(TB, P, HD).transpose(1, 0, 2).reshape(P, 128))
    c, s = table(np.arange(P) * 16 + CL - 1)
    put("cosc", c)
    put("sinc", s)
    r, k = np.arange(P)[:, None], np.arange(P)[None]
    put("tri", np.where(r > k, -1.0, 0.0))
    put("ones", -1.0)
    causal = np.where(k <= r, 0.0, NEG)
    end = np.arange(NC_)[None] * 16 + CL - 1
    put("mask", np.concatenate([causal, np.zeros((P, P)), causal, np.where(end <= r, 0.0, NEG),
                                np.where(end <= r + P, 0.0, NEG)], 1))
    strict = np.where(r < k, 1.0, 0.0)
    put("msb", np.concatenate([strict, np.ones((P, P)), strict], 1))
    put("hasc", np.where(r >= CL - 1, 1.0, 0.0))
    kep[:, KEP["ident"][0]:KEP["ident"][0] + P] = np.eye(P)
    kep[:, KEP["iota"][0]:KEP["iota"][0] + P] = k
    kep[:, KEP["iota16"][0]:KEP["iota16"][0] + 16] = np.arange(16)[None]
    return cst, kep


def kernel(**inputs):
    import concourse.bacc as bacc
    from concourse.bass_utils import run_bass_kernel_spmd

    a = {k: np.asarray(v) for k, v in inputs.items()}
    wpre, u, v, par = lay_out(a)
    cst, kep = constants()
    arrays = dict(x_d=np.ascontiguousarray(a["x"][0]), wpre_d=wpre, u_d=u, v_d=v, par_d=par, cst_d=cst, kep_d=kep)
    nc = bacc.Bacc("TRN2", target_bir_lowering=False, num_devices=1)
    args = [nc.dram_tensor(k, x.shape, mybir.dt.from_np(x.dtype), kind="ExternalInput").ap() for k, x in arrays.items()]
    args.append(nc.dram_tensor("out_d", (T, D), F32, kind="ExternalOutput").ap())
    build(nc, *args)
    r = run_bass_kernel_spmd(nc, [arrays], core_ids=[0])
    return r.results[0]["out_d"].reshape(1, T, D)
```

```python
from contextlib import ExitStack

import numpy as np
import concourse.bass as bass
from concourse import mybir

F32 = mybir.dt.float32
F32R = mybir.dt.float32r
U32 = mybir.dt.uint32
ALU = mybir.AluOpType
ACT = mybir.ActivationFunctionType
AXX = mybir.AxisListType.X

P = 128
D = 1024
T = 256
TB = T // P
KT = D // P
HD = 64
NH = 8
NG = 2
NC_ = (T - 32) // 16 + 1
CL = 32
CH = 256
TOPK = 16
NK = 128
NBLK = 128
EPS = 1e-6
NEG = -1e30
SCALE = 0.125

T_KC, T_VC = 0, 1
T_KV, T_Q = 2, 6
T_W1K, T_W1V = 10, 14
T_QSB, T_KSB = 18, 22
T_VSB = 26
T_GATE = 30
T_BR = 46
T_WQ = 62
N_PRE = 78
N_ALL = N_PRE + 2 * NBLK
RING = 4
SPLIT = 3
UNROLL = 12
ROUTER = 62
NGRP = T // 4
HALF = NBLK // 2
EARLY = 7
TILES_KEYS, TILES_PAIRS = 14, 25
TILES_NUMBERS = ROUTER - 2 - TILES_KEYS - TILES_PAIRS

PARAMS = dict(g1=8, g2=8, qg=64, kgc=64, kgs=128, posk=16, posv=16, w2k=128, w2v=128, subk=256, gw=192)
CONSTS = dict(cos=128, sin=128, cosc=64, sinc=64, tri=128, ones=128, mask=384 + 2 * NC_, msb=384, hasc=1)
KEPT = dict(ident=128, iota=128, iota16=16)


def offsets(table):
    out, at = {}, 0
    for k, n in table.items():
        out[k] = (at, n)
        at += n
    return out, at


PAR, NPAR = offsets(PARAMS)
CST, NCST = offsets(CONSTS)
KEP, NKEP = offsets(KEPT)


def build(nc, x_d, wpre_d, u_d, v_d, par_d, cst_d, kep_d, out_d):
    with ExitStack() as ctx:
        def sb(name, shape, dt=F32):
            return ctx.enter_context(nc.sbuf_tensor(name, shape, dt))

        def sem(name):
            return ctx.enter_context(nc.semaphore(name))

        bank = [ctx.enter_context(nc.psum_tensor(f"bank{i}", [P, 512], F32)) for i in range(8)]

        u_bank = (bank[4], bank[5], bank[3])

        big = sb("big", [P, NBLK * T])
        raw = sb("raw", [P, RING, 1024])
        hi = sb("hi", [P, SPLIT, 1024], F32R)
        lo = sb("lo", [P, SPLIT, 1024], F32R)
        xhi = sb("xhi", [P, 8, T], F32R)
        xlo = sb("xlo", [P, 8, T], F32R)
        auxh = sb("auxh", [P, SPLIT * T], F32R)
        auxl = sb("auxl", [P, SPLIT * T], F32R)
        kep = sb("kep", [P, NKEP])
        eT = sb("eT", [P, 3, T])
        gw2 = sb("gw2", [P, T, 2], F32R)
        same = sb("same", [P, 2, 4, HALF])
        oneA = sb("oneA", [P, 2, 4, 2, HALF], F32R)
        gsum = sb("gsum", [P, 4, HALF])
        oneB = sb("oneB", [P, 2, 4, P], F32R)

        flatA, flatB = (oneA[:, :, :, :, :].rearrange("p q t r k -> p (q t r k)"),
                        oneB[:, :, :, :].rearrange("p q t k -> p (q t k)"))
        ohi = (flatB.rearrange("p (k t) -> p k t", k=4), xhi[:, 4:8, :])
        olo = (flatA.rearrange("p (k t) -> p k t", k=4), xlo[:, 4:8, :])
        gwh, gwl = (gw2[:, :, :].rearrange("p t r -> p (t r)")[:, z * 192:(z + 1) * 192] for z in range(2))
        at = [0]

        def carve(n, start=None):
            if start is not None:
                at[0] = start
            a = at[0]
            at[0] += n
            assert at[0] <= NBLK * T
            return big[:, a:a + n]

        h = carve(TB * D).rearrange("p (b d) -> p b d", b=TB)
        par = carve(NPAR)
        cst = carve(NCST)

        def pv(k):
            a, n = PAR[k]
            return par[:, a:a + n]

        def cv_(k):
            a, n = CST[k]
            return cst[:, a:a + n]

        ident = kep[:, KEP["ident"][0]:KEP["ident"][0] + P]
        iota = kep[:, KEP["iota"][0]:KEP["iota"][0] + P]
        iota16 = kep[:, KEP["iota16"][0]:KEP["iota16"][0] + 16]

        xs = carve(TB * D).rearrange("p (b d) -> p b d", b=TB)
        st = carve(64)
        gcq, gsq = (carve(128).rearrange("p (b d) -> p b d", b=2) for _ in range(2))
        gck, gsk = (carve(256).rearrange("p (b s d) -> p b s d", b=2, s=2) for _ in range(2))
        gcc, gsc = carve(64), carve(64)
        nrm_n, nrm_a, nrm_b, nrm_q, nrm_c = carve(512), carve(512), carve(512), carve(512), carve(128)
        qrot = carve(1024).rearrange("p (b c) -> p b c", b=2)
        krdup = carve(1024).rearrange("p (b s c) -> p b s c", b=2, s=4)
        kcd = carve(256)
        vsw = carve(512).rearrange("p (b c) -> p b c", b=2)
        vcs = carve(128)
        qT = carve(1024).rearrange("p (a t) -> p a t", a=4)
        kT = carve(1024).rearrange("p (a t) -> p a t", a=4)
        kcT = carve(32).rearrange("p (g c) -> p g c", g=2)
        qsbT = carve(1024).rearrange("p (a t) -> p a t", a=4)
        ksbT = carve(1024).rearrange("p (a t) -> p a t", a=4)
        vsb = carve(1024).rearrange("p (b c) -> p b c", b=2)
        ghid = carve(120)
        hidn = carve(2 * CH)[0:30, :]
        gsig = carve(48)
        gexpT = carve(T)[0:24, :]
        ggate = carve(48).rearrange("p (h c) -> p h c", c=6)
        sm = carve(2 * 828).rearrange("p (q c) -> p q c", q=2)
        att = carve(2 * 32).rearrange("p (q c) -> p q c", q=2)
        pT = carve(1024)
        sbt = carve(5 * 384).rearrange("p (k c) -> p k c", k=5)
        gates_at = at[0]
        gates = carve(4096).rearrange("p (a t) -> p a t", a=16)
        stok = big[:, gates_at:gates_at + 960]
        oT = carve(2048).rearrange("p (a t) -> p a t", a=8)
        mrg = carve(2 * 768).rearrange("p (q c) -> p q c", q=2)
        qst = cst[:, 0:1024].rearrange("p (q c) -> p q c", q=2)
        sc = carve(4096, start=23040)
        tkv, tki = carve(512), carve(512)
        cval = carve(256)
        caf, cbf = carve(256), carve(256)
        i1f, i2f = carve(256), carve(256)
        gwt = carve(256)
        stg2 = [carve(256) for _ in range(2)]
        stg = [carve(256) for _ in range(4)]
        eqt = [[carve(256) for _ in range(2)] for _ in range(2)]
        sti, sta, stb = ([carve(16).bitcast(U32) for _ in range(2)] for _ in range(3))
        smx = carve(32)
        assert at[0] <= NBLK * T

        loaded = [sem(f"tile_loaded{i}") for i in range(RING)]
        small_in = sem("small_in")
        x_in = [sem(f"x_in{b}") for b in range(TB)]
        kep_in = sem("kep_in")
        hi_done = sem("hi_done")
        lo_done = sem("lo_done")
        tile_used = sem("tile_used")
        dve_step = sem("dve_step")
        act_step = sem("act_step")
        N = {}

        def S(name):
            if name not in N:
                N[name] = sem(name)
            return N[name]

        def is_split(n):
            return not T_W1K <= n < T_W1V + 4

        def splits(n):
            return n - min(max(n - T_W1K, 0), 8)

        def slot_user(n):
            n -= SPLIT
            while not is_split(n):
                n -= SPLIT
            return n

        def branch_tile(i):
            return T_BR + max(2 * i - 1, 0)

        def out_tile(i):
            return T_BR + min(2 * i + 2, 15)

        def mix_splits(i):
            first = branch_tile(i) + SPLIT
            return range(first, first + (1 if i == 0 else 3 if i == 7 else 2))

        def each_tile(eng, count, body):
            steps = count // UNROLL
            if steps > 1:
                with eng.Fori(0, steps) as i:
                    for j in range(UNROLL):
                        body(i, j)
                for j in range(count - steps * UNROLL):
                    body(steps, j)
            else:
                for j in range(count):
                    body(0, j)

        block = ctx.enter_context(nc.Block())

        @block.sync
        def _(sp):
            for b in range(TB):
                sp.dma_start(h[:, b, :], x_d[b * P:(b + 1) * P, :]).then_inc(x_in[b], 16)
            sp.dma_start(kep[:, :], kep_d).then_inc(kep_in, 16)
            sp.dma_start(par, par_d).then_inc(small_in, 16)
            sp.dma_start(cst, cst_d).then_inc(small_in, 16)

            def load(slot, src):
                sp.dma_start(raw[:, slot, :], src).then_inc(loaded[slot], 16)

            for n in range(RING):
                load(n, wpre_d[n])

            for n in range(RING, T_W1V + 4 + RING):
                if is_split(n - RING):
                    sp.wait_ge(lo_done, splits(n - RING + 1))
                else:
                    sp.wait_ge(tile_used, n - RING + 1)
                load(n % RING, wpre_d[n])

            def stream(src, first, at_, count):
                def one(i, j):
                    sp.wait_ge(lo_done, i * UNROLL + splits(first + at_ + j - RING + 1))
                    load((first + at_ + j) % RING,
                         src[bass.ds(i * UNROLL + (at_ + j), 1)].rearrange("a p c -> (a p) c"))
                each_tile(sp, count, one)

            begin = T_W1V + 4 + RING
            stream(wpre_d, 0, begin, T_WQ + 8 - begin)
            sp.wait_ge(S("h_ready"), TB)
            for b in range(TB):
                sp.dma_start(out_d[b * P:(b + 1) * P, :], h[:, b, :]).then_inc(S("h_saved"), 16)
            stream(wpre_d, 0, T_WQ + 8, N_PRE - T_WQ - 8)
            stream(u_d, N_PRE, 0, NBLK)
            stream(v_d, N_PRE + NBLK, 0, HALF)
            sp.wait_ge(S("h_saved"), 16 * TB)
            sp.wait_ge(tile_used, N_PRE + NBLK + T // 32)
            for b in range(TB):
                sp.dma_start(h[:, b, :], out_d[b * P:(b + 1) * P, :]).then_inc(S("h_back"), 16)
            stream(v_d, N_PRE + NBLK, HALF, HALF)
            for b in range(TB):
                for f in range(2):
                    c = slice(f * 512, (f + 1) * 512)
                    sp.wait_ge(S("out_ready"), 2 * b + f + 1)
                    sp.dma_start(out_d[b * P:(b + 1) * P, c], h[:, b, c]).then_inc(S("stored"), 16)
            sp.wait_ge(S("stored"), 32 * TB)

        @block.tensor
        def _(pe):
            def need(n):
                pe.wait_ge(hi_done, splits(n + 1))
                pe.wait_ge(lo_done, splits(n + 1))

            def tposed(n, out, x_ready=None):
                need(n)
                s = n % SPLIT
                for k in range(KT):
                    if x_ready is not None:
                        pe.wait_ge(S("xlo_ready"), x_ready + k + 1)
                    wh, wl = hi[:, s, k * P:(k + 1) * P], lo[:, s, k * P:(k + 1) * P]
                    pe.matmul(out, wh, xhi[:, k, :], start=(k == 0), stop=False)
                    pe.matmul(out, wh, xlo[:, k, :], start=False, stop=False)
                    m = pe.matmul(out, wl, xhi[:, k, :], start=False, stop=(k == KT - 1))
                m.then_inc(tile_used, 1)

            def normal(n, i, outs):
                need(n)
                s = n % SPLIT
                for b in range(TB):
                    for kk in range(2):
                        k = 2 * i + kk
                        wh, wl = hi[:, s, kk * 512:kk * 512 + 512], lo[:, s, kk * 512:kk * 512 + 512]
                        xh, xl = xhi[:, k, b * P:(b + 1) * P], xlo[:, k, b * P:(b + 1) * P]
                        pe.matmul(outs[b], xh, wh, start=(k == 0), stop=False)
                        pe.matmul(outs[b], xh, wl, start=False, stop=False)
                        m = pe.matmul(outs[b], xl, wh, start=False, stop=(k == KT - 1))
                m.then_inc(tile_used, 1)

            def transpose_x(which):
                for k in range(KT):
                    for b in range(TB):
                        m = pe.matmul(bank[4 + k // 2][:, (k % 2) * T + b * P:(k % 2) * T + (b + 1) * P],
                                      h[:, b, k * P:(k + 1) * P], xs[:, b, 0:P], start=True, stop=True)
                    if k % 2:
                        m.then_inc(S("xT_ready"), 1)

            pe.wait_ge(kep_in, 16)
            pe.wait_ge(S("xs_ready"), 1)
            transpose_x(0)
            tposed(T_KC, bank[0][:, 0:T], x_ready=0)
            tposed(T_VC, bank[3][:, 0:T])
            for i in range(4):
                normal(T_KV + i, i, [bank[6][:, :], bank[7][:, :]])
            pe.wait_ge(S("gw_split"), 1)
            out = bank[2][0:24, 0:T]
            for k in range(KT):
                wh, wl = gwh[:, 24 * k:24 * k + 24], gwl[:, 24 * k:24 * k + 24]
                pe.matmul(out, wh, xhi[:, k, :], start=(k == 0), stop=False)
                pe.matmul(out, wh, xlo[:, k, :], start=False, stop=False)
                m = pe.matmul(out, wl, xhi[:, k, :], start=False, stop=(k == KT - 1))
            m.then_inc(S("gn_ready"), 1)
            for i in range(4):
                normal(T_Q + i, i, [bank[4][:, :], bank[5][:, :]])
            pe.wait_ge(S("gn_exp"), 1)
            pe.wait_ge(S("tok"), 1)
            for b in range(TB):
                m = pe.transpose(bank[3][:, 32 * b:32 * b + 24], gexpT[:, b * P:(b + 1) * P], ident[0:24, 0:24])
            m.then_inc(S("gnT_ready"), 1)
            for w, first in ((0, T_W1K), (1, T_W1V)):
                for i in range(4):
                    n = first + i
                    pe.wait_ge(loaded[n % RING], 16 * (n // RING + 1))
                    for jj in range(4):
                        j = 4 * i + jj
                        a = w * 480 + j * 30
                        m = pe.matmul(bank[1 + w][0:30, 0:CH], stok[:, a:a + 30],
                                      raw[:, n % RING, jj * CH:(jj + 1) * CH], start=(j == 0), stop=(j == 15))
                    m.then_inc(tile_used, 1)
            for i in range(4):
                if i == 1:
                    pe.wait_ge(S("hid"), 2)
                    for z in range(4):
                        m = pe.transpose(bank[1][:, CH + 32 * z:CH + 32 * z + 30], hidn[:, z * P:(z + 1) * P],
                                         ident[0:30, 0:30])
                    m.then_inc(S("hidT_ready"), 1)
                    pe.wait_ge(S("gates_n"), 1)
                if i == 2:
                    pe.wait_ge(S("ghid"), 1)
                    for w in range(2):
                        w2 = pv("w2k" if w == 0 else "w2v")
                        for g in range(NG):
                            for hb in range(2):
                                a = (w * 2 + hb) * 30 + g * NC_
                                m = pe.matmul(bank[1][0:NC_, P + (w * 2 + g) * HD:P + (w * 2 + g + 1) * HD],
                                              ghid[:, a:a + NC_], w2[:, hb * HD:(hb + 1) * HD],
                                              start=(hb == 0), stop=(hb == 1))
                    m.then_inc(S("cmp_ready"), 1)
                if i == 3:
                    pe.wait_ge(S("krot"), 1)
                    pe.wait_ge(S("vsw"), 1)
                    for s in range(4):
                        for b in range(TB):
                            m = pe.transpose(bank[6 + s // 2][:, (s % 2) * T + b * P:(s % 2) * T + (b + 1) * P],
                                             krdup[:, b, s, :], ident)
                    m.then_inc(S("kT_ready"), 1)
                    pe.wait_ge(S("qrot"), 1)
                    for a in range(4):
                        for b in range(TB):
                            m = pe.transpose(bank[4 + a // 2][:, (a % 2) * T + b * P:(a % 2) * T + (b + 1) * P],
                                             qrot[:, b, a * P:(a + 1) * P], ident)
                    m.then_inc(S("qT_ready"), 1)
                if i >= 2:
                    pe.wait_ge(S("qksb_out"), i - 1)
                b = bank[(0, 3)[i % 2]]
                tposed(T_QSB + 2 * i, b[:, 0:T])
                tposed(T_QSB + 2 * i + 1, b[:, T:2 * T])
            pe.wait_ge(S("kcrot"), 1)
            pe.wait_ge(S("qksb_out"), 3)
            for g in range(NG):
                m = pe.transpose(bank[0][:, 16 * g:16 * g + NC_],
                                 kcd[0:NC_, g * P:(g + 1) * P], ident[0:NC_, 0:NC_])
            m.then_inc(S("kcT_ready"), 1)
            def scores(hh):
                r0, a, g = 64 * (hh % 2), hh // 2, hh // 4
                r = slice(r0, r0 + HD)
                if hh == 0:
                    pe.wait_ge(S("qkT_out"), 4)
                    pe.wait_ge(S("kcT_out"), 1)
                else:
                    pe.wait_ge(S("masked"), hh)
                for br, o in ((0, bank[4]), (1, bank[5])):
                    k = kT[r, 2 * br + g, :]
                    pe.matmul(o[:, 0:P], qT[r, a, 0:P], k[:, 0:P], start=True, stop=True)
                    m = pe.matmul(o[:, P:384], qT[r, a, P:T], k[:, 0:T], start=True, stop=True)
                for b in range(TB):
                    m = pe.matmul(bank[4][:, 384 + NC_ * b:384 + NC_ * (b + 1)], qT[r, a, b * P:(b + 1) * P],
                                  kcT[r, g, 0:NC_], start=True, stop=True)
                m.then_inc(S("scores"), 1)

            def sticks(hh):
                r0, a = 64 * (hh % 2), hh // 2
                r = slice(r0, r0 + HD)
                if hh == 0:
                    pe.wait_ge(S("qksb_out"), 4)
                    pe.wait_ge(S("vsb_out"), 1)
                else:
                    pe.wait_ge(S("x_ready"), hh)
                pe.matmul(bank[2][:, 0:T], ksbT[r, a, 0:P], qsbT[r, a, :], start=True, stop=True)
                m = pe.matmul(bank[2][:, T:384], ksbT[r, a, P:T], qsbT[r, a, P:T], start=True, stop=True)
                m.then_inc(S("z_ready"), 1)

            def gate_tile(g):
                if g >= 2:
                    pe.wait_ge(S("gate_exp"), g - 1)
                else:
                    pe.wait_ge(S("vsb_out"), 2)
                tposed(T_GATE + g, bank[g % 2][:, 0:T])

            pe.wait_ge(S("vc_out"), 1)
            pe.wait_ge(S("kcrot"), 1)
            for i in range(4):
                normal(T_VSB + i, i, [bank[2][:, :], bank[1][:, :]])
                if i == 0:
                    scores(0)
            sticks(0)
            for hh in range(NH):
                r0, a, g = 64 * (hh % 2), hh // 2, hh // 4
                gate_tile(2 * hh)
                pe.wait_ge(S("probs"), hh + 1)
                if hh == 0:
                    pe.wait_ge(S("qksb_out"), 4)
                else:
                    pe.wait_ge(S("pT_out"), 2 * hh)
                    pe.wait_ge(S("cmpT_out"), hh)
                    pe.wait_ge(S("osb_out"), hh)
                q = hh % 2
                for br in range(2):
                    for c in range(3):
                        m = pe.transpose(bank[6 + br][:, c * P:(c + 1) * P],
                                         sm[:, q, 414 * br + c * P:414 * br + (c + 1) * P], ident)
                m.then_inc(S("pT"), 1)
                for b in range(TB):
                    m = pe.transpose(bank[3][0:NC_, b * P:(b + 1) * P],
                                     sm[:, q, 384 + NC_ * b:384 + NC_ * (b + 1)], ident)
                m.then_inc(S("cmpT"), 1)
                if hh + 1 < NH:
                    scores(hh + 1)
                pe.wait_ge(S("l_masked"), hh + 1)
                L = sbt[:, 1, :]
                pe.matmul(bank[2][:, 0:T], cv_("tri"), L[:, 0:T], start=True, stop=False)
                pe.matmul(bank[2][:, P:T], cv_("ones"), L[:, T:384], start=False, stop=True)
                m = pe.matmul(bank[2][:, T:384], cv_("tri"), L[:, T:384], start=True, stop=True)
                m.then_inc(S("after"), 1)
                if hh + 1 < NH:
                    gate_tile(2 * hh + 1)
                    sticks(hh + 1)
                pe.wait_ge(S("pT_out"), 2 * hh + 2)
                pe.wait_ge(S("cmpT_out"), hh + 1)
                o = bank[3][r0:r0 + HD, 0:T]
                for br in range(2):
                    vcol = slice((2 * br + g) * HD, (2 * br + g + 1) * HD)
                    p0 = 384 * br
                    pe.matmul(o, vsw[:, 0, vcol], pT[:, p0:p0 + T], start=(br == 0), stop=False)
                    pe.matmul(o[:, P:T], vsw[:, 1, vcol], pT[:, p0 + T:p0 + 384], start=False, stop=False)
                m = pe.matmul(o, vcs[0:NC_, g * HD:(g + 1) * HD], pT[0:NC_, 768:1024], start=False, stop=True)
                m.then_inc(S("onsa"), 1)
                pe.wait_ge(S("a_ready"), hh + 1)
                o = bank[3][r0:r0 + HD, T:2 * T]
                vcol = slice(hh * HD, (hh + 1) * HD)
                pe.matmul(o, vsb[:, 0, vcol], sbt[:, 4, 0:T], start=True, stop=False)
                m = pe.matmul(o[:, P:T], vsb[:, 1, vcol], sbt[:, 4, T:384], start=False, stop=True)
                m.then_inc(S("osb"), 1)
            gate_tile(2 * NH - 1)

            def branch(i):
                n = branch_tile(i)
                if i == 0:
                    pe.wait_ge(S("masked"), NH)
                if i >= 2:
                    pe.wait_ge(S("mrg_read"), i - 1)
                need(n)
                s = n % SPLIT
                for br in range(2):
                    if i == 0:
                        pe.wait_ge(S("oT_split"), br + 1)
                    out = bank[4 + i % 2][:, br * T:(br + 1) * T]
                    for k in range(4):
                        c0 = (br * 4 + k) * P
                        wh, wl = hi[:, s, c0:c0 + P], lo[:, s, c0:c0 + P]
                        pe.matmul(out, wh, ohi[br][:, k, :], start=(k == 0), stop=False)
                        pe.matmul(out, wh, olo[br][:, k, :], start=False, stop=False)
                        m = pe.matmul(out, wl, ohi[br][:, k, :], start=False, stop=(k == 3))
                m.then_inc(tile_used, 1)

            branch(0)
            for i in range(8):
                if i + 1 < 8:
                    branch(i + 1)
                n = out_tile(i)
                need(n)
                pe.wait_ge(S("mrg_split"), i + 1)
                if i == 0:
                    pe.wait_ge(S("gate_exp"), 16)
                s = n % SPLIT
                for b in range(TB):
                    c0 = (i % 2) * T + b * P
                    mh, ml = auxh[:, c0:c0 + P], auxl[:, c0:c0 + P]
                    three = ((mh, hi), (mh, lo), (ml, hi))
                    if i < 7:
                        for st_, (a_, w_) in enumerate(three):
                            for f in range(2):
                                m = pe.matmul(bank[2 * b + f][:, :], a_, w_[:, s, f * 512:(f + 1) * 512],
                                              start=(i == 0 and st_ == 0), stop=False)
                    else:
                        for f in range(2):
                            for st_, (a_, w_) in enumerate(three):
                                m = pe.matmul(bank[2 * b + f][:, :], a_, w_[:, s, f * 512:(f + 1) * 512],
                                              start=False, stop=(st_ == 2))
                            if 2 * b + f < 3:
                                m.then_inc(S("mixed"), 1)
                m.then_inc(tile_used, 1)

            def key_scores(j):
                pe.wait_ge(S("bank45_read"), j + 1)
                if j >= 2:
                    pe.wait_ge(S("sc_out"), j - 1)
                for p_ in range(2):
                    for b in range(TB):
                        c0 = p_ * T + b * P
                        m = pe.matmul(bank[6 + j % 2][:, c0:c0 + P], qst[:, j % 2, c0:c0 + P],
                                      pv("subk")[:, p_ * P:(p_ + 1) * P], start=True, stop=True)
                m.then_inc(S("key_scores"), 1)

            pe.wait_ge(S("xs_ready"), 2)
            pe.wait_ge(S("mrg_read"), 8)
            transpose_x(1)
            for i in range(NH):
                if i >= 2:
                    pe.wait_ge(S("bank45_read"), i - 1)
                if i == 0:
                    pe.wait_ge(S("xlo_ready"), KT + 4)
                for p_ in range(2):
                    tposed(T_WQ + 2 * i + p_, bank[4 + i % 2][:, p_ * T:(p_ + 1) * T], x_ready=KT if i + p_ == 0 else None)
                if i >= 1:
                    key_scores(i - 1)
            key_scores(NH - 1)

            V0 = N_PRE + NBLK

            def loop_need(i, n):
                pe.wait_ge(hi_done, i * UNROLL + splits(n + 1))
                pe.wait_ge(lo_done, i * UNROLL + splits(n + 1))

            def u_tile(i, j, base):
                n, pair = N_PRE + base + j, (base + j) // 2
                if (base + j) % 2 == 0:
                    pe.wait_ge(S("bank45_read"), i * (UNROLL // 2) + (pair + NH - 2))
                loop_need(i, n)
                s = n % SPLIT
                out = u_bank[pair % 3][:, ((base + j) % 2) * T:((base + j) % 2 + 1) * T]
                for k in range(KT):
                    wh, wl = hi[:, s, k * P:(k + 1) * P], lo[:, s, k * P:(k + 1) * P]
                    pe.matmul(out, wh, xhi[:, k, :], start=(k == 0), stop=False)
                    pe.matmul(out, wh, xlo[:, k, :], start=False, stop=False)
                    m = pe.matmul(out, wl, xhi[:, k, :], start=False, stop=(k == KT - 1))
                m.then_inc(tile_used, 1)

            def g_group(i, j, base):
                g = base + j
                pe.wait_ge(S("oneA_ready"), i * UNROLL + (g + 1))
                pe.wait_ge(S("oneB_ready"), i * UNROLL + (g + 1))
                pe.wait_ge(S("bank67_read"), i * UNROLL + (g + 1))
                for t in range(4):
                    m = pe.matmul(bank[6 + g % 2][:, 2 * t * HALF:2 * (t + 1) * HALF], oneB[:, g % 2, t, :],
                                  oneA[:, g % 2, t, :, :], start=True, stop=True)
                m.then_inc(S("g_ready"), 1)

            pe.wait_ge(S("bank45_read"), NH)
            each_tile(pe, ROUTER, lambda i, j: u_tile(i, j, 0))
            pe.wait_ge(S("router"), 1)
            for w, src in enumerate((i1f, i2f, gwt)):
                for b in range(TB):
                    m = pe.transpose(bank[6 + w // 2][:, (w % 2) * T + b * P:(w % 2) * T + (b + 1) * P],
                                     src[:, b * P:(b + 1) * P], ident)
            m.then_inc(S("routerT"), 1)

            for j in range(ROUTER, HALF):
                u_tile(0, j, 0)

            def g_and_u(i, j):
                g_group(i, j, 0)
                u_tile(i, j, HALF)

            each_tile(pe, NGRP, g_and_u)
            g_group(0, 0, NGRP)

            def v_tile(i, j, base, first=False, last=False):
                n = V0 + base + j
                s = n % SPLIT
                loop_need(i, n)
                pe.wait_ge(S("wlo_done"), i * UNROLL + (base + j + 1))
                for b in range(TB):
                    c0 = s * T + b * P
                    wh, wl = auxh[:, c0:c0 + P], auxl[:, c0:c0 + P]
                    three = ((wh, hi), (wh, lo), (wl, hi))
                    if not last:
                        for st_, (a_, w_) in enumerate(three):
                            for f in range(2):
                                m = pe.matmul(bank[2 * b + f][:, :], a_, w_[:, s, f * 512:(f + 1) * 512],
                                              start=(first and st_ == 0), stop=False, skip_group_check=True)
                    else:
                        for f in range(2):
                            for st_, (a_, w_) in enumerate(three):
                                m = pe.matmul(bank[2 * b + f][:, :], a_, w_[:, s, f * 512:(f + 1) * 512],
                                              start=False, stop=(st_ == 2), skip_group_check=True)
                            m.then_inc(S("sum_ready"), 1)
                if not last:
                    m.then_inc(tile_used, 1)

            def g_and_v(i, j):
                g_group(i, j, NGRP + 2)
                v_tile(i, j, 1)

            v_tile(0, 0, 0, first=True)
            g_group(0, 1, NGRP)
            each_tile(pe, NGRP - 2, g_and_v)
            each_tile(pe, NBLK - NGRP, lambda i, j: v_tile(i, j, NGRP - 1))
            v_tile(0, 0, NBLK - 1, last=True)

        @block.scalar
        def _(act):
            own = [0]

            def link(ins):
                own[0] += 1
                ins.then_inc(act_step, 1)
                act.wait_ge(act_step, own[0])

            def split_hi(n):
                act.wait_ge(loaded[n % RING], 16 * (n // RING + 1))
                if n >= SPLIT:
                    act.wait_ge(tile_used, slot_user(n) + 1)
                act.activation(hi[:, n % SPLIT, :], raw[:, n % RING, :], ACT.Copy).then_inc(hi_done, 1)

            def squares(b):
                act.activation(xs[:, b, :], h[:, b, :], ACT.Square, accum_out=st[:, b:b + 1]).then_inc(S("sq"), 1)

            def rstd(u, v):
                act.wait_ge(S("var"), u)
                link(act.activation(v, v, ACT.Ln))
                act.activation(v, v, ACT.Exp, scale=-0.5).then_inc(S("rs"), 1)

            def x_hi(k, which):
                act.wait_ge(S("xT_ready"), (which * KT + k) // 2 + 1)
                act.activation(xhi[:, k, :], bank[4 + k // 2][:, (k % 2) * T:(k % 2 + 1) * T], ACT.Copy,
                               scale=pv("g1" if which == 0 else "g2")[:, k:k + 1]).then_inc(S("xhi_ready"), 1)

            LN_EXP, GELU = "natural_log_exp_and_others", "gelu_apprx_tanh_and_others"
            act.preload_act_table_set(LN_EXP)
            for b in range(TB):
                act.wait_ge(x_in[b], 16)
                squares(b)
            rstd(1, st[:, 8:10])
            act.wait_ge(small_in, 32)
            act.activation(gwh, pv("gw"), ACT.Copy).then_inc(S("gw_hi"), 1)
            split_hi(0)
            for k in range(KT):
                x_hi(k, 0)
                if k == 1:
                    split_hi(1)
            for n in range(2, 9):
                split_hi(n)
            act.wait_ge(tile_used, T_KV + 4)
            for b in range(TB):
                m = act.activation(nrm_a[:, b * T:(b + 1) * T], bank[6 + b][:, 0:T], ACT.Square)
            m.then_inc(S("sqk"), 1)
            for b in range(TB):
                m = act.activation(vsw[:, b, :], bank[6 + b][:, T:512], ACT.Copy)
            m.then_inc(S("vsw"), 1)
            act.wait_ge(S("gn_ready"), 1)
            act.activation(gexpT, bank[2][0:24, 0:T], ACT.Exp, scale=-1.0).then_inc(S("gn_exp"), 1)
            split_hi(9)
            rstd(2, st[:, 16:24])
            act.wait_ge(tile_used, T_Q + 4)
            act.wait_ge(S("krot"), 1)
            for b in range(TB):
                m = act.activation(nrm_a[:, 0:512] if b == 0 else nrm_q, bank[4 + b][:, :], ACT.Square)
            m.then_inc(S("sqk"), 1)
            rstd(3, st[:, 32:48])
            act.preload_act_table_set(GELU)
            for w in range(2):
                act.wait_ge(tile_used, T_W1K + 4 * w + 4)
                act.activation(hidn[:, w * CH:(w + 1) * CH], bank[1 + w][0:30, 0:CH],
                               ACT.Gelu_apprx_tanh).then_inc(S("hid"), 1)
                if w == 0:
                    split_hi(18)
            split_hi(19)
            act.preload_act_table_set(LN_EXP)
            split_hi(20)
            act.wait_ge(S("hidT_ready"), 1)
            act.activation(ghid.rearrange("p (z c) -> p z c", z=4),
                           bank[1][:, CH:CH + P].rearrange("p (z c) -> p z c", z=4)[:, :, 0:30],
                           ACT.Copy).then_inc(S("ghid"), 1)
            split_hi(21)
            split_hi(22)

            def qksb_out(i):
                act.wait_ge(tile_used, T_QSB + 2 * i + 2)
                dst = (qsbT if i < 2 else ksbT)[:, 2 * (i % 2):2 * (i % 2) + 2, :]
                act.activation(dst, bank[(0, 3)[i % 2]][:, :].rearrange("p (a t) -> p a t", a=2), ACT.Copy,
                               scale=SCALE if i < 2 else 1.0).then_inc(S("qksb_out"), 1)

            qksb_out(0)
            split_hi(23)
            split_hi(24)
            act.wait_ge(S("cmp_ready"), 1)
            act.activation(nrm_c[0:NC_, :], bank[1][0:NC_, P:2 * P], ACT.Square).then_inc(S("sqk"), 1)
            act.activation(vcs[0:NC_, :], bank[1][0:NC_, 2 * P:3 * P], ACT.Copy).then_inc(S("vc_out"), 1)
            qksb_out(1)
            rstd(4, st[0:NC_, 24:26])
            split_hi(25)
            split_hi(26)
            qksb_out(2)
            act.wait_ge(S("kT_ready"), 1)
            for s in range(2):
                act.activation(kT[:, 2 * s:2 * s + 2, :], bank[6 + s][:, :].rearrange("p (a t) -> p a t", a=2),
                               ACT.Copy).then_inc(S("qkT_out"), 1)
            act.wait_ge(S("qT_ready"), 1)
            for s in range(2):
                act.activation(qT[:, 2 * s:2 * s + 2, :], bank[4 + s][:, :].rearrange("p (a t) -> p a t", a=2),
                               ACT.Copy).then_inc(S("qkT_out"), 1)
            split_hi(27)
            split_hi(28)
            qksb_out(3)
            act.wait_ge(S("kcT_ready"), 1)
            act.activation(kcT[:, :, 0:NC_], bank[0][:, 0:32].rearrange("p (g c) -> p g c", g=2)[:, :, 0:NC_],
                           ACT.Copy).then_inc(S("kcT_out"), 1)
            for n in range(29, 31):
                split_hi(n)

            def softplus(hh):
                act.wait_ge(S("z_ready"), hh + 1)
                if hh:
                    act.wait_ge(S("z_read"), hh)
                sp_ = sbt[:, 2, :]
                link(act.activation(sp_, bank[2][:, 0:384], ACT.Abs))
                link(act.activation(sp_, sp_, ACT.Exp, scale=-1.0))
                act.activation(sp_, sp_, ACT.Ln, bias=1.0).then_inc(S("softplus"), 1)

            def gate_exp(g):
                act.wait_ge(tile_used, T_GATE + g + 1)
                act.activation(gates[:, g, :], bank[g % 2][:, 0:T], ACT.Exp,
                               scale=-1.0).then_inc(S("gate_exp"), 1)

            def exps(hh):
                q = hh % 2
                act.wait_ge(S("negmax"), hh + 1)
                for c, (c0, w_) in enumerate(((0, P), (P, T), (414, P), (414 + P, T), (384, NC_), (384 + NC_, NC_))):
                    x_ = sm[:, q, c0:c0 + w_]
                    m = act.activation(x_, x_, ACT.Exp, bias=att[:, q, 6 + c:7 + c], scale=SCALE,
                                       accum_out=att[:, q, 12 + c:13 + c])
                m.then_inc(S("exped"), 1)

            def osb_out(hh):
                r0, a = 64 * (hh % 2), hh // 2
                act.wait_ge(S("osb"), hh + 1)
                act.activation(oT.rearrange("p (k a) t -> p k a t", k=2)[r0:r0 + HD, :, a, :],
                               bank[3][r0:r0 + HD, :].rearrange("p (k t) -> p k t", k=2), ACT.Copy).then_inc(S("osb_out"), 1)

            exps(0)
            split_hi(31)
            split_hi(32)
            act.wait_ge(tile_used, T_VSB + 4)
            act.activation(vsb[:, 0, :], bank[2][:, :], ACT.Copy).then_inc(S("vsb_out"), 1)
            act.activation(vsb[:, 1, :], bank[1][:, :], ACT.Copy).then_inc(S("vsb_out"), 1)
            softplus(0)
            for hh in range(NH):
                split_hi(T_GATE + 2 * hh + 3)
                act.wait_ge(S("pT"), hh + 1)
                if hh:
                    act.wait_ge(S("onsa"), hh)
                for br in range(2):
                    act.activation(pT[:, 384 * br:384 * (br + 1)], bank[6 + br][:, 0:384],
                                   ACT.Copy).then_inc(S("pT_out"), 1)
                gate_exp(2 * hh)
                act.wait_ge(S("x_ready"), hh + 1)
                act.activation(sbt[:, 0, :], sbt[:, 0, :], ACT.Exp).then_inc(S("x_exp"), 1)
                if hh + 1 < NH:
                    exps(hh + 1)
                    osb_out(hh)
                    softplus(hh + 1)
                    split_hi(T_GATE + 2 * hh + 4)
                    gate_exp(2 * hh + 1)
            osb_out(NH - 1)
            act.wait_ge(S("osb_out"), NH)
            act.activation(ohi[0], oT[:, 0:4, :], ACT.Copy).then_inc(S("oT_hi"), 1)
            act.wait_ge(tile_used, T_GATE + 16)
            act.activation(ohi[1], oT[:, 4:8, :], ACT.Copy).then_inc(S("oT_hi"), 1)
            split_hi(T_GATE + 2 * NH + 2)
            gate_exp(2 * NH - 1)

            def gate_sigmoid(i):
                two = gates.rearrange("p (r a) t -> p r a t", r=2)[:, :, i, :]
                if i == 0:
                    act.wait_ge(S("gate_exp"), 16)
                link(act.activation(two, two, ACT.Ln, bias=1.0))
                act.activation(two, two, ACT.Exp, scale=-1.0).then_inc(S("gate_sig"), 1)

            gate_sigmoid(0)
            for i in range(8):
                act.wait_ge(S("merged"), i + 1)
                if i >= 2:
                    act.wait_ge(tile_used, out_tile(i - 2) + 1)
                act.activation(auxh[:, (i % 2) * T:(i % 2 + 1) * T], mrg[:, i % 2, 512:768],
                               ACT.Copy).then_inc(S("mrg_hi"), 1)
                for n in mix_splits(i)[:2]:
                    split_hi(n)
                if i + 1 < 8:
                    gate_sigmoid(i + 1)
            for b in range(TB):
                act.wait_ge(S("h_ready"), b + 1)
                squares(b)
            rstd(5, st[:, 8:10])
            split_hi(mix_splits(7)[2])
            for k in range(KT):
                x_hi(k, 1)
            for i in range(NH):
                split_hi(T_WQ + 2 * i + 3)
                split_hi(T_WQ + 2 * i + 4)
                if i >= 2:
                    act.wait_ge(S("key_scores"), i - 1)
                act.activation(qst[:, i % 2, :], bank[4 + i % 2][:, :], ACT.Copy).then_inc(S("bank45_read"), 1)

            V0 = N_PRE + NBLK

            def loop_hi(i, n):
                act.wait_ge(loaded[n % RING], i * (16 * (UNROLL // RING)) + 16 * (n // RING + 1))
                act.wait_ge(tile_used, i * UNROLL + (n - SPLIT + 1))
                act.activation(hi[:, n % SPLIT, :], raw[:, n % RING, :], ACT.Copy).then_inc(hi_done, 1)

            def gelu_pair(i, j, base):
                if (base + j) % 2:
                    act.wait_ge(tile_used, i * UNROLL + (N_PRE + base + j + 1))
                    act.activation(big[:, bass.ds(i * (UNROLL * T) + (base + j - 1) * T, 2 * T)],
                                   u_bank[(base + j) // 2 % 3][:, :], ACT.Gelu_apprx_tanh).then_inc(S("bank45_read"), 1)

            def one_hot_b(i, j, base):
                g = base + j
                act.wait_ge(S("dist"), i * UNROLL + (g + 1))
                B = oneB[:, g % 2, :, :].bitcast(F32)
                act.activation(oneB[:, g % 2, :, :], B, ACT.Square).then_inc(S("dist_sq"), 1)
                act.wait_ge(S("dist_sq"), i * UNROLL + (g + 1))
                act.activation(oneB[:, g % 2, :, :], B, ACT.Relu, bias=1.0,
                               scale=-1.0).then_inc(S("oneB_ready"), 1)

            def w_hi(i, b):
                s = (V0 + b) % SPLIT
                act.activation(auxh[:, s * T:(s + 1) * T], big[:, bass.ds(i * (UNROLL * T) + b * T, T)],
                               ACT.Copy).then_inc(S("whi_done"), 1)

            def u_step(i, j):
                loop_hi(i, N_PRE + j + SPLIT)
                gelu_pair(i, j, 0)

            def u_step_g(i, j):
                one_hot_b(i, j, 1)
                loop_hi(i, N_PRE + HALF + j + SPLIT)
                gelu_pair(i, j, HALF)

            act.preload_act_table_set(GELU)
            act.wait_ge(S("h_saved"), 16 * TB)
            each_tile(act, ROUTER - 2, u_step)
            act.preload_act_table_set(LN_EXP)
            act.wait_ge(S("router_d"), 1)
            act.activation(gwt, gwt, ACT.Exp).then_inc(S("router_exp"), 1)
            act.preload_act_table_set(GELU)
            for j in range(ROUTER - 2, ROUTER):
                u_step(0, j)
            act.wait_ge(S("bank67_read"), 2)
            act.activation(gw2[:, :, 0], eT[:, 2, :], ACT.Copy).then_inc(S("gw2_hi"), 1)
            one_hot_b(0, 0, 0)
            for j in range(ROUTER, HALF):
                u_step(0, j)
            each_tile(act, HALF - 1, u_step_g)
            one_hot_b(0, 0, NGRP)
            act.wait_ge(S("weighed"), 1 + NGRP)
            w_hi(0, 0)
            loop_hi(0, N_PRE + NBLK - 1 + SPLIT)
            gelu_pair(0, HALF - 1, HALF)

            def v_step_g(i, j):
                one_hot_b(i, j, NGRP + 2)
                loop_hi(i, V0 + j + SPLIT)
                w_hi(i, j + SPLIT)

            def v_step(i, j):
                loop_hi(i, V0 + HALF + j + SPLIT)
                w_hi(i, HALF + j + SPLIT)

            for b in range(1, SPLIT):
                w_hi(0, b)
            one_hot_b(0, 1, NGRP)
            each_tile(act, HALF - SPLIT, v_step_g)
            one_hot_b(0, HALF - 1, NGRP)
            loop_hi(0, V0 + HALF)
            loop_hi(0, V0 + HALF + 1)
            act.wait_ge(S("weighed"), 1 + 2 * NGRP)
            w_hi(0, HALF)
            loop_hi(0, V0 + HALF + 2)
            w_hi(0, HALF + 1)
            w_hi(0, HALF + 2)
            each_tile(act, HALF - SPLIT, v_step)

        @block.vector
        def _(dve):
            own = [0]

            def link(ins):
                own[0] += 1
                ins.then_inc(dve_step, 1)
                dve.wait_ge(dve_step, own[0])

            def split_lo(n):
                dve.wait_ge(hi_done, splits(n + 1))
                dve.tensor_tensor(lo[:, n % SPLIT, :], raw[:, n % RING, :], hi[:, n % SPLIT, :].bitcast(F32),
                                  ALU.subtract).then_inc(lo_done, 1)

            def sharpen(v, y, t):
                link(dve.tensor_tensor(t, y, y, ALU.mult))
                link(dve.tensor_tensor(t, t, v, ALU.mult))
                link(dve.tensor_scalar(t, t, -0.5, 1.5, ALU.mult, ALU.add))
                link(dve.tensor_tensor(y, y, t, ALU.mult))

            def var(ssq, v, y, n):
                link(dve.tensor_scalar(v, ssq, 1.0 / n, EPS, ALU.mult, ALU.add))
                dve.tensor_copy(y, v).then_inc(S("var"), 1)

            def norm_x(which):
                dve.wait_ge(S("sq"), 2 * which + 2)
                if which:
                    dve.wait_ge(S("xlo_ready"), KT)
                var(st[:, 0:2], st[:, 2:4], st[:, 8:10], D)
                dve.wait_ge(S("rs"), 1 if which == 0 else 5)
                sharpen(st[:, 2:4], st[:, 8:10], st[:, 4:6])
                for b in range(TB):
                    m = dve.tensor_scalar(xs[:, b, 0:P], ident, st[:, 8 + b:9 + b], None, ALU.mult)
                m.then_inc(S("xs_ready"), 1)

            def x_lo(k, which):
                dve.wait_ge(S("xhi_ready"), which * KT + 2 * (k // 2) + 2)
                dve.scalar_tensor_tensor(xlo[:, k, :], bank[4 + k // 2][:, (k % 2) * T:(k % 2 + 1) * T],
                                         pv("g1" if which == 0 else "g2")[:, k:k + 1],
                                         xhi[:, k, :].bitcast(F32), ALU.mult, ALU.subtract).then_inc(S("xlo_ready"), 1)

            dve.wait_ge(kep_in, 16)
            norm_x(0)
            dve.wait_ge(small_in, 32)
            split_lo(0)
            for k in range(KT):
                x_lo(k, 0)
                if k == 3:
                    split_lo(1)
            for n in range(2, 4):
                split_lo(n)
            dve.wait_ge(S("gw_hi"), 1)
            dve.tensor_tensor(gwl, pv("gw"), gwh.bitcast(F32), ALU.subtract).then_inc(S("gw_split"), 1)
            cosT = cv_("cos").rearrange("p (b d) -> p b d", b=2)
            sinT = cv_("sin").rearrange("p (b d) -> p b d", b=2)
            for b in range(TB):
                for dst_c, dst_s, g_ in [(gcq[:, b, :], gsq[:, b, :], pv("qg"))] + [
                        (gck[:, b, s, :], gsk[:, b, s, :], pv("kgs")[:, s * HD:(s + 1) * HD]) for s in range(2)]:
                    dve.tensor_tensor(dst_c, cosT[:, b, :], g_, ALU.mult)
                    dve.tensor_tensor(dst_s[:, 0:32], sinT[:, b, 0:32], g_[:, 32:64], ALU.mult)
                    dve.tensor_tensor(dst_s[:, 32:64], sinT[:, b, 32:64], g_[:, 0:32], ALU.mult)
                split_lo(4 + b)
            dve.tensor_tensor(gcc, cv_("cosc"), pv("kgc"), ALU.mult)
            dve.tensor_tensor(gsc[:, 0:32], cv_("sinc")[:, 0:32], pv("kgc")[:, 32:64], ALU.mult)
            link(dve.tensor_tensor(gsc[:, 32:64], cv_("sinc")[:, 32:64], pv("kgc")[:, 0:32], ALU.mult))
            tok = stok.rearrange("p (w j g c) -> p w j g c", w=2, j=16, g=2)
            for w in range(2):
                dve.wait_ge(tile_used, w + 1)
                pos = pv("posk" if w == 0 else "posv")
                for g in range(NG):
                    for l2 in range(2):
                        src = bank[3 * w][g * HD:(g + 1) * HD, l2:T]
                        win = bass.AP(src.tensor, src.offset, [list(src.ap[0]), [2, 16], [16, NC_]])
                        r = slice(l2 * HD, (l2 + 1) * HD)
                        m = dve.tensor_tensor(tok[r, w, :, g, :], win,
                                              pos[r, :].unsqueeze(2).broadcast_to([HD, 16, NC_]), ALU.add)
                if w:
                    m.then_inc(S("tok"), 1)
                split_lo(6 + w)
            split_lo(8)

            def rotate(p_, n, a_, b_, src, y, gc, gs, outs, done):
                nh = src.shape[1]
                yb = y.unsqueeze(2).broadcast_to([p_, nh, HD])
                link(dve.tensor_tensor(n, src, yb, ALU.mult))
                dve.tensor_tensor(a_, n, gc, ALU.mult)
                dve.tensor_tensor(b_[:, :, 0:32], n[:, :, 32:64], gs[:, :, 0:32], ALU.mult)
                link(dve.tensor_tensor(b_[:, :, 32:64], n[:, :, 0:32], gs[:, :, 32:64], ALU.mult))
                for k, o in enumerate(outs):
                    m = dve.tensor_tensor(o, a_, b_, ALU.add)
                if done is None:
                    link(m)
                else:
                    m.then_inc(done, 1)

            def heads(ap_, nh):
                return ap_.rearrange("p (a d) -> p a d", a=nh)

            def per_slot(tab, p_, rep):
                return tab.unsqueeze(2).broadcast_to([p_, tab.shape[1], rep, HD])

            dve.wait_ge(S("sqk"), 1)
            link(dve.tensor_reduce(st[:, 48:56], heads(nrm_a, 8), AXX, ALU.add))
            var(st[:, 48:56], st[:, 48:56], st[:, 16:24], HD)
            split_lo(9)
            dve.wait_ge(S("rs"), 2)
            sharpen(st[:, 48:56], st[:, 16:24], st[:, 56:64])
            for b in range(TB):
                n, a_, b_ = (heads(z[:, 0:T], 4) for z in (nrm_n, nrm_q, nrm_b))
                yb = st[:, 16 + 4 * b:20 + 4 * b].unsqueeze(2).broadcast_to([P, 4, HD])
                link(dve.tensor_tensor(n, heads(bank[6 + b][:, 0:T], 4), yb, ALU.mult))
                for s in range(2):
                    gc = gck[:, b, s, :].unsqueeze(1).broadcast_to([P, 2, HD])
                    gs = gsk[:, b, s, :].unsqueeze(1).broadcast_to([P, 2, HD])
                    two = slice(2 * s, 2 * s + 2)
                    dve.tensor_tensor(a_[:, two, :], n[:, two, :], gc, ALU.mult)
                    dve.tensor_tensor(b_[:, two, 0:32], n[:, two, 32:64], gs[:, :, 0:32], ALU.mult)
                    m = dve.tensor_tensor(b_[:, two, 32:64], n[:, two, 0:32], gs[:, :, 32:64], ALU.mult)
                link(m)
                for d_ in range(2):
                    m = dve.tensor_tensor(krdup[:, b, :, d_ * HD:(d_ + 1) * HD], a_, b_, ALU.add)
                if b:
                    m.then_inc(S("krot"), 1)
                else:
                    link(m)
            dve.wait_ge(S("krot"), 1)
            dve.wait_ge(S("sqk"), 2)
            dve.tensor_reduce(st[:, 48:56], heads(nrm_a, 8), AXX, ALU.add)
            link(dve.tensor_reduce(st[:, 56:64], heads(nrm_q, 8), AXX, ALU.add))
            var(st[:, 48:64], st[:, 48:64], st[:, 32:48], HD)
            dve.wait_ge(S("gnT_ready"), 1)
            link(dve.tensor_scalar(gsig.rearrange("p (b c) -> p b c", b=2),
                                   bank[3][:, 0:64].rearrange("p (b c) -> p b c", b=2)[:, :, 0:24], 1.0, None, ALU.add))
            link(dve.reciprocal(gsig, gsig))
            gsv = gsig.rearrange("p (b r h) -> p b r h", b=2, r=3)
            for br, c0 in ((1, 0), (2, 2), (0, 4)):
                m = dve.tensor_copy(ggate[:, :, c0:c0 + 2], gsv[:, :, br, :].rearrange("p b h -> p h b"))
            link(m)
            dve.tensor_scalar(ggate[:, :, 4:5], ggate[:, :, 4:5], cv_("hasc"), None, ALU.mult).then_inc(S("gates_n"), 1)
            dve.wait_ge(S("rs"), 3)
            sharpen(st[:, 48:64], st[:, 32:48], st[:, 0:16])
            for b in range(TB):
                n, a_, b_ = (heads(z, 8) for z in (nrm_n, nrm_a, nrm_b))
                rotate(P, n, a_, b_, heads(bank[4 + b][:, :], 8), st[:, 32 + 8 * b:40 + 8 * b],
                       gcq[:, b, :].unsqueeze(1).broadcast_to([P, 8, HD]),
                       gsq[:, b, :].unsqueeze(1).broadcast_to([P, 8, HD]),
                       [heads(qrot[:, b, :], 8)], S("qrot") if b else None)
            dve.wait_ge(S("qrot"), 1)
            for n in range(18, 25):
                split_lo(n)
            dve.wait_ge(S("sqk"), 3)
            link(dve.tensor_reduce(st[0:NC_, 26:28], heads(nrm_c[0:NC_, :], 2), AXX, ALU.add))
            var(st[0:NC_, 26:28], st[0:NC_, 26:28], st[0:NC_, 24:26], HD)
            dve.wait_ge(S("rs"), 4)
            sharpen(st[0:NC_, 26:28], st[0:NC_, 24:26], st[0:NC_, 28:30])
            n, a_, b_ = (heads(z[0:NC_, 0:P], 2) for z in (nrm_n, nrm_q, nrm_b))
            kd = kcd[0:NC_, :].rearrange("p (g c) -> p g c", g=2)
            rotate(NC_, n, a_, b_, heads(bank[1][0:NC_, P:2 * P], 2), st[0:NC_, 24:26],
                   gcc[0:NC_, :].unsqueeze(1).broadcast_to([NC_, 2, HD]),
                   gsc[0:NC_, :].unsqueeze(1).broadcast_to([NC_, 2, HD]),
                   [kd[:, :, 0:HD], kd[:, :, HD:2 * HD]], S("kcrot"))
            dve.wait_ge(S("kcrot"), 1)
            dve.wait_ge(S("gates_n"), 1)
            for n in range(25, 30):
                split_lo(n)

            def mask_scores(hh):
                q = hh % 2
                dve.wait_ge(S("scores"), hh + 1)
                if hh >= 2:
                    dve.wait_ge(S("cmpT"), hh - 1)
                dve.tensor_tensor(sm[:, q, 0:414], bank[4][:, 0:414], cv_("mask"), ALU.add)
                dve.tensor_tensor(sm[:, q, 414:798], bank[5][:, 0:384], cv_("mask")[:, 0:384],
                                  ALU.add).then_inc(S("masked"), 1)
                dve.wait_ge(S("masked"), hh + 1)
                both = sm[:, q, :].rearrange("p (r c) -> p r c", c=414)
                mx = att[:, q, 0:4].rearrange("p (r b) -> p r b", b=2)
                dve.tensor_reduce(mx[:, :, 0:1], both[:, :, 0:P], AXX, ALU.max)
                dve.tensor_reduce(mx[:, :, 1:2], both[:, :, P:384], AXX, ALU.max)
                link(dve.tensor_reduce(att[:, q, 4:6], sm[:, q, 384:414].rearrange("p (b c) -> p b c", b=2), AXX, ALU.max))
                dve.tensor_scalar(att[:, q, 6:12], att[:, q, 0:6], -SCALE, None, ALU.mult).then_inc(S("negmax"), 1)

            def stick_logs(hh):
                dve.wait_ge(S("softplus"), hh + 1)
                if hh:
                    dve.wait_ge(S("a_ready"), hh)
                dve.scalar_tensor_tensor(sbt[:, 0, :], bank[2][:, 0:384], 0.0, sbt[:, 2, :], ALU.max, ALU.add)
                dve.scalar_tensor_tensor(sbt[:, 3, :], bank[2][:, 0:384], 0.0, sbt[:, 2, :], ALU.min,
                                         ALU.subtract).then_inc(S("z_read"), 1)

            def normalise(hh):
                q = hh % 2
                dve.wait_ge(S("exped"), hh + 1)
                link(dve.reciprocal(att[:, q, 18:24], att[:, q, 12:18]))
                link(dve.tensor_tensor(att[:, q, 18:24], att[:, q, 18:24], ggate[:, hh, :], ALU.mult))
                for c, (c0, w_) in enumerate(((0, P), (P, T), (414, P), (414 + P, T), (384, NC_), (384 + NC_, NC_))):
                    x_ = sm[:, q, c0:c0 + w_]
                    m = dve.tensor_scalar(x_, x_, att[:, q, 18 + c:19 + c], None, ALU.mult)
                m.then_inc(S("probs"), 1)

            mask_scores(0)
            split_lo(30)
            normalise(0)
            split_lo(31)
            split_lo(32)
            stick_logs(0)
            for hh in range(NH):
                split_lo(T_GATE + 2 * hh + 3)
                dve.wait_ge(S("cmpT"), hh + 1)
                if hh:
                    dve.wait_ge(S("onsa"), hh)
                dve.tensor_copy(pT[0:NC_, 768:1024], bank[3][0:NC_, 0:T]).then_inc(S("cmpT_out"), 1)
                if hh + 1 < NH:
                    mask_scores(hh + 1)
                dve.wait_ge(S("after"), hh + 1)
                dve.tensor_tensor(sbt[:, 0, :], sbt[:, 3, :], bank[2][:, 0:384], ALU.add).then_inc(S("x_ready"), 1)
                if hh + 1 < NH:
                    normalise(hh + 1)
                    stick_logs(hh + 1)
                    split_lo(T_GATE + 2 * hh + 4)
            for br in range(2):
                dve.wait_ge(S("oT_hi"), br + 1)
                dve.tensor_tensor(olo[br], oT[:, 4 * br:4 * br + 4, :], ohi[br].bitcast(F32),
                                  ALU.subtract).then_inc(S("oT_split"), 1)
            split_lo(T_GATE + 2 * NH + 2)
            for i in range(8):
                q = i % 2
                dve.wait_ge(S("gate_sig"), i + 1)
                dve.wait_ge(tile_used, branch_tile(i) + 1)
                if i >= 2:
                    dve.wait_ge(S("mrg_hi"), i - 1)
                ab = mrg[:, q, 0:512].rearrange("p (r t) -> p r t", r=2)
                gate = gates.rearrange("p (r a) t -> p r a t", r=2)[:, :, i, :]
                dve.tensor_tensor(ab, bank[4 + q][:, :].rearrange("p (r t) -> p r t", r=2), gate,
                                  ALU.mult).then_inc(S("mrg_read"), 1)
                dve.wait_ge(S("mrg_read"), i + 1)
                dve.tensor_tensor(mrg[:, q, 512:768], mrg[:, q, 0:T], mrg[:, q, T:512], ALU.add).then_inc(S("merged"), 1)
                dve.wait_ge(S("mrg_hi"), i + 1)
                dve.tensor_tensor(auxl[:, q * T:(q + 1) * T], mrg[:, q, 512:768],
                                  auxh[:, q * T:(q + 1) * T].bitcast(F32), ALU.subtract).then_inc(S("mrg_split"), 1)
                for n in mix_splits(i)[:1 if i == 7 else 2]:
                    split_lo(n)
            for b in range(TB):
                for f in range(2):
                    if 2 * b + f < 3:
                        dve.wait_ge(S("mixed"), 2 * b + f + 1)
                    else:
                        dve.wait_ge(tile_used, T_WQ)
                    c = slice(f * 512, (f + 1) * 512)
                    m = dve.tensor_tensor(h[:, b, c], h[:, b, c], bank[2 * b + f][:, :], ALU.add)
                m.then_inc(S("h_ready"), 1)
            split_lo(mix_splits(7)[1])
            norm_x(1)
            split_lo(mix_splits(7)[2])
            for k in range(KT):
                x_lo(k, 1)

            def sc_out(j):
                dve.wait_ge(S("key_scores"), j + 1)
                dst = sc.rearrange("p (b h s k) -> p h s b k", b=2, h=8, s=2)[:, j]
                dve.tensor_copy(dst, bank[6 + j % 2][:, :].rearrange("p (s b k) -> p s b k", s=2, b=2)).then_inc(S("sc_out"), 1)

            def query_splits():
                for i in range(NH):
                    split_lo(T_WQ + 2 * i + 3)
                    split_lo(T_WQ + 2 * i + 4)
                    if i:
                        sc_out(i - 1)
                        if i <= EARLY:
                            dve.wait_ge(S("sc_out"), i)
                            choose_keys(i - 1)
                sc_out(NH - 1)

            def loop_lo(i, n):
                dve.wait_ge(hi_done, i * UNROLL + splits(n + 1))
                dve.tensor_tensor(lo[:, n % SPLIT, :], raw[:, n % RING, :], hi[:, n % SPLIT, :].bitcast(F32),
                                  ALU.subtract).then_inc(lo_done, 1)

            def chains(ops):
                first = own[0]
                for k, op in enumerate(ops):
                    if k >= 2:
                        dve.wait_ge(dve_step, first + k - 1)
                    own[0] += 1
                    op().then_inc(dve_step, 1)
                dve.wait_ge(dve_step, own[0])

            def top16(pair, w_):
                ops = [lambda c=c, s_=s_, v_=v_: dve.max(v_[:, 0:8], s_) for c, (s_, v_) in enumerate(pair)]
                ops += [lambda c=c, s_=s_, v_=v_: dve.max_index(sti[c][:, 0:8], v_[:, 0:8], s_)
                        for c, (s_, v_) in enumerate(pair)]
                ops += [lambda c=c, s_=s_, v_=v_: dve.match_replace(stg2[c][:, 0:w_], v_[:, 0:8], s_, -3e38)
                        for c, (s_, v_) in enumerate(pair)]
                ops += [lambda c=c, v_=v_: dve.max(v_[:, 8:16], stg2[c][:, 0:w_]) for c, (s_, v_) in enumerate(pair)]
                ops += [lambda c=c, v_=v_: dve.max_index(sti[c][:, 8:16], v_[:, 8:16], stg2[c][:, 0:w_])
                        for c, (s_, v_) in enumerate(pair)]
                return ops

            nxt_tile = [0]

            def spread(upto):
                while nxt_tile[0] < upto:
                    loop_lo(0, N_PRE + nxt_tile[0] + SPLIT)
                    nxt_tile[0] += 1

            def choose_keys(c):
                k2 = [slice((2 * c + p_) * 16, (2 * c + p_ + 1) * 16) for p_ in range(2)]
                ops = top16([(sc[:, (2 * c + p_) * P:(2 * c + p_ + 1) * P], tkv[:, k2[p_]]) for p_ in range(2)], P)
                ops += [lambda p_=p_: dve.tensor_copy(tki[:, k2[p_]], sti[p_]) for p_ in range(2)]
                chains(ops)

            query_splits()
            dve.wait_ge(S("sc_out"), NH)
            for c in range(EARLY, 16):
                choose_keys(c)
                spread(TILES_KEYS * (c + 1 - EARLY) // (16 - EARLY))
            dve.tensor_copy(smx[:, 0:1], tkv[:, 0:1]).then_inc(S("keys_chosen"), 1)
            for c in range(0, 16, 2):
                cc = (c, c + 1)
                c16 = [slice(z * 16, z * 16 + 16) for z in cc]
                dve.wait_ge(S("pair_sums"), c + 2)
                chains(top16([(stg[cc[x] % 4], cval[:, c16[x]]) for x in range(2)], 256))
                spread(TILES_KEYS + (TILES_PAIRS * (c + 1)) // 16)
                for x in range(2):
                    dve.tensor_scalar(sta[x], sti[x], 4, None, ALU.logical_shift_right).then_inc(S("pairs_chosen"), 1)
                    m = dve.tensor_scalar(stb[x], sti[x], 15, None, ALU.bitwise_and)
                link(m)
                for x in range(2):
                    dve.tensor_copy(caf[:, c16[x]], sta[x])
                    m = dve.tensor_copy(cbf[:, c16[x]], stb[x])
                link(m)
                spread(TILES_KEYS + (TILES_PAIRS * (c + 2)) // 16)
            places = iota16.unsqueeze(1).broadcast_to([P, 16, 16])
            eq = [[z.rearrange("p (k a) -> p k a", k=16) for z in two] for two in eqt]

            def sum_picked(c):
                dve.wait_ge(S("picked"), 2 * (c + 1))
                for side, dst in enumerate((i1f, i2f)):
                    dve.tensor_reduce(dst[:, c * 16:c * 16 + 16], eq[c % 2][side], AXX, ALU.add).then_inc(S("key_numbers"), 1)

            for c in range(16):
                if c >= 2:
                    dve.wait_ge(S("key_numbers"), 2 * (c - 1))
                for side, pl in enumerate((caf, cbf)):
                    dve.tensor_tensor(eq[c % 2][side], places,
                                      pl[:, c * 16:c * 16 + 16].unsqueeze(2).broadcast_to([P, 16, 16]),
                                      ALU.is_equal).then_inc(S("placed"), 1)
                spread(TILES_KEYS + TILES_PAIRS + (TILES_NUMBERS * (c + 1)) // 16)
                if c:
                    sum_picked(c - 1)
            sum_picked(15)
            dve.wait_ge(S("key_numbers"), 32)
            cv3 = cval.rearrange("p (c k) -> p c k", k=16)
            g3 = gwt.rearrange("p (c k) -> p c k", k=16)
            dve.tensor_tensor(g3, cv3, cv3[:, :, 0:1].broadcast_to([P, 16, 16]), ALU.subtract).then_inc(S("router_d"), 1)
            dve.wait_ge(S("router_exp"), 1)
            link(dve.tensor_reduce(smx[:, 0:16], g3, AXX, ALU.add))
            link(dve.reciprocal(smx[:, 16:32], smx[:, 0:16]))
            dve.tensor_tensor(g3, g3, smx[:, 16:32].unsqueeze(2).broadcast_to([P, 16, 16]), ALU.mult).then_inc(S("router"), 1)
            spread(ROUTER)
            dve.wait_ge(S("routerT"), 1)
            dve.tensor_copy(eT[:, 0:2, :], bank[6][:, :].rearrange("p (w t) -> p w t", w=2)).then_inc(S("bank67_read"), 1)
            dve.tensor_copy(eT[:, 2, :], bank[7][:, 0:T]).then_inc(S("bank67_read"), 1)
            dve.wait_ge(S("bank67_read"), 2)

            by_token = big[:, :].rearrange("p (e t) -> p t e", t=T)

            def keys_equal(i, j, base):
                g = base + j
                e0 = 0 if g < NGRP else HALF
                if g >= 2:
                    dve.wait_ge(S("oneA_ready"), i * UNROLL + (g - 1))
                i1 = eT[:, 0, bass.ds(i * (4 * UNROLL) + 4 * (g % NGRP), 4)].unsqueeze(2).broadcast_to([P, 4, HALF])
                dve.tensor_tensor(same[:, g % 2, :, :], iota[:, e0:e0 + HALF].unsqueeze(1).broadcast_to([P, 4, HALF]),
                                  i1, ALU.is_equal).then_inc(S("same"), 1)

            def rows_a(i, j, base):
                g = base + j
                dve.wait_ge(S("same"), i * UNROLL + (g + 1))
                eq_ = same[:, g % 2, :, :].unsqueeze(2).broadcast_to([P, 4, 2, HALF])
                w_ = gw2[:, bass.ds(i * (4 * UNROLL) + 4 * (g % NGRP), 4), :].bitcast(F32)
                dve.tensor_tensor(oneA[:, g % 2, :, :, :], eq_, w_.unsqueeze(3).broadcast_to([P, 4, 2, HALF]),
                                  ALU.mult).then_inc(S("oneA_ready"), 1)

            def add_parts(i, j, base):
                g = base + j
                dve.wait_ge(S("g_ready"), i * UNROLL + (g + 1))
                dve.wait_ge(S("weighed"), i * UNROLL + (g + 1))
                parts = bank[6 + g % 2][:, :].rearrange("p (t r e) -> p t e r", t=4, r=2)
                dve.tensor_reduce(gsum[:, :, :], parts, AXX, ALU.add).then_inc(S("bank67_read"), 1)

            def weigh(i, j, base):
                g = base + j
                e0 = 0 if g < NGRP else HALF
                dve.wait_ge(S("bank67_read"), i * UNROLL + (g + 3))
                w4 = by_token[:, bass.ds(i * (4 * UNROLL) + 4 * (g % NGRP), 4), e0:e0 + HALF]
                dve.tensor_tensor(w4, gsum[:, :, :], w4, ALU.mult).then_inc(S("weighed"), 1)

            dve.wait_ge(S("gw2_hi"), 1)
            link(dve.tensor_tensor(gw2[:, :, 1], eT[:, 2, :], gw2[:, :, 0].bitcast(F32), ALU.subtract))
            keys_equal(0, 0, 0)
            keys_equal(0, 1, 0)
            rows_a(0, 0, 0)
            keys_equal(0, 2, 0)
            rows_a(0, 1, 0)
            for j in range(ROUTER, HALF):
                loop_lo(0, N_PRE + j + SPLIT)
            dve.wait_ge(S("bank45_read"), NH + HALF // 2)
            dve.tensor_copy(gsum[:, 0, 0:1], eT[:, 2, 0:1]).then_inc(S("weighed"), 1)

            def group_step(i, j, base, keys=True, rows=True):
                add_parts(i, j, base)
                if keys:
                    keys_equal(i, j, base + 3)
                weigh(i, j, base)
                if rows:
                    rows_a(i, j, base + 2)

            def u_step_g(i, j):
                group_step(i, j, 0)
                loop_lo(i, N_PRE + HALF + j + SPLIT)

            each_tile(dve, NGRP - 4, u_step_g)
            for j in range(NGRP - 4, NGRP):
                u_step_g(0, j)

            V0 = N_PRE + NBLK
            dve.wait_ge(S("bank45_read"), NH + NBLK // 2)
            group_step(0, 0, NGRP)

            def v_step_g(i, j):
                group_step(i, j, NGRP + 1)
                loop_lo(i, V0 + j + SPLIT)

            each_tile(dve, NGRP - 4, v_step_g)
            for j in range(NGRP - 4, NGRP - 1):
                group_step(0, j, NGRP + 1, keys=False, rows=j == NGRP - 4)
                loop_lo(0, V0 + j + SPLIT)
            loop_lo(0, V0 + NGRP - 1 + SPLIT)
            each_tile(dve, HALF - SPLIT, lambda i, j: loop_lo(i, V0 + HALF + j + SPLIT))
            dve.wait_ge(S("h_back"), 16 * TB)
            for b in range(TB):
                for f in range(2):
                    dve.wait_ge(S("sum_ready"), 2 * b + f + 1)
                    c = slice(f * 512, (f + 1) * 512)
                    dve.tensor_tensor(h[:, b, c], h[:, b, c], bank[2 * b + f][:, :], ALU.add).then_inc(S("out_ready"), 1)

        @block.gpsimd
        def _(pool):
            for hh in range(NH):
                pool.wait_ge(S("z_read"), hh + 1)
                if hh:
                    pool.wait_ge(S("after"), hh)
                pool.tensor_tensor(sbt[:, 1, :], sbt[:, 0, :], cv_("msb"), ALU.mult).then_inc(S("l_masked"), 1)
                pool.wait_ge(S("x_exp"), hh + 1)
                if hh:
                    pool.wait_ge(S("osb"), hh)
                pool.tensor_tensor(sbt[:, 4, :], sbt[:, 0, :], cv_("msb"), ALU.mult).then_inc(S("a_ready"), 1)

            pool.wait_ge(S("keys_chosen"), 1)
            for c in range(16):
                if c >= 4:
                    pool.wait_ge(S("pairs_chosen"), c - 3)
                s1 = tkv[:, c * 32:c * 32 + 16].unsqueeze(2).broadcast_to([P, 16, 16])
                s2 = tkv[:, c * 32 + 16:c * 32 + 32].unsqueeze(1).broadcast_to([P, 16, 16])
                pool.tensor_tensor(stg[c % 4].rearrange("p (a b) -> p a b", a=16), s1, s2,
                                   ALU.add).then_inc(S("pair_sums"), 1)
            for c in range(16):
                for side in range(2):
                    pool.wait_ge(S("placed"), 2 * c + side + 1)
                    e3 = eqt[c % 2][side].rearrange("p (k a) -> p k a", k=16)
                    at_ = c * 32 + 16 * side
                    pool.tensor_tensor(e3, e3, tki[:, at_:at_ + 16].unsqueeze(1).broadcast_to([P, 16, 16]),
                                       ALU.mult).then_inc(S("picked"), 1)

            def distances(i, j, base):
                g = base + j
                if g >= 2:
                    pool.wait_ge(S("g_ready"), i * UNROLL + (g - 1))
                i2 = eT[:, 1, bass.ds(i * (4 * UNROLL) + 4 * (g % NGRP), 4)].unsqueeze(2).broadcast_to([P, 4, P])
                pool.tensor_tensor(oneB[:, g % 2, :, :], iota.unsqueeze(1).broadcast_to([P, 4, P]), i2,
                                   ALU.subtract).then_inc(S("dist"), 1)

            pool.wait_ge(S("bank67_read"), 2)
            distances(0, 0, 0)
            distances(0, 1, 0)
            each_tile(pool, NGRP - 2, lambda i, j: distances(i, j, 2))
            for g in range(2):
                distances(0, g, NGRP)
            V0 = N_PRE + NBLK

            def w_lo(i, b):
                s = (V0 + b) % SPLIT
                pool.wait_ge(S("whi_done"), i * UNROLL + (b + 1))
                pool.tensor_tensor(auxl[:, s * T:(s + 1) * T], big[:, bass.ds(i * (UNROLL * T) + b * T, T)],
                                   auxh[:, s * T:(s + 1) * T].bitcast(F32), ALU.subtract).then_inc(S("wlo_done"), 1)

            def v_step_g(i, j):
                distances(i, j, NGRP + 3)
                w_lo(i, SPLIT + j)

            w_lo(0, 0)
            distances(0, 2, NGRP)
            for b in range(1, SPLIT):
                w_lo(0, b)
            each_tile(pool, HALF - SPLIT, v_step_g)
            for b in range(HALF, HALF + SPLIT):
                w_lo(0, b)
            each_tile(pool, HALF - SPLIT, lambda i, j: w_lo(i, HALF + SPLIT + j))

    return nc


def lay_out(a):
    f = np.float32
    win = a["w_in"][0]
    col = {}
    at = 0
    for name, n in (("q", 512), ("kc", 128), ("vc", 128), ("ks", 128), ("vs", 128), ("kw", 128), ("vw", 128),
                    ("gn", 24), ("qsb", 512), ("ksb", 512), ("vsb", 512), ("br", 2 * D)):
        col[name] = win[:, at:at + n]
        at += n
    assert at == win.shape[1]

    def stationary(w):
        return w.reshape(KT, P, -1, P).transpose(2, 1, 0, 3).reshape(-1, P, 1024)

    def moving(w):
        return w.reshape(4, 2, P, 512).transpose(0, 2, 1, 3).reshape(4, P, 1024)

    def compress(w):
        return w.reshape(4, 4, P, CH).transpose(0, 2, 1, 3).reshape(4, P, 1024)

    bn, bs, wo = a["w_branch_nsa"][0], a["w_branch_sb"][0], a["w_out"][0]
    both = np.concatenate([bn, bs], 0)
    br = stationary(both)
    wo = wo.reshape(8, P, D)
    mix = np.stack([br[0]] + [t for i in range(7) for t in (br[i + 1], wo[i])] + [wo[7]], 0)
    wpre = np.concatenate([
        stationary(col["kc"]), stationary(col["vc"]),
        moving(np.concatenate([col["ks"], col["kw"], col["vs"], col["vw"]], 1)), moving(col["q"]),
        compress(a["cmp_k_w1"][0]), compress(a["cmp_v_w1"][0]),
        stationary(col["qsb"]), stationary(col["ksb"]), moving(col["vsb"]), stationary(col["br"]),
        mix, stationary(a["peer_w_query"][0])], 0)
    assert wpre.shape[0] == N_PRE
    u = a["peer_u"][0].reshape(NBLK, P, KT, P).transpose(0, 3, 2, 1).reshape(NBLK, P, 1024)
    v = a["peer_v"][0].reshape(NBLK, P, D)

    par = np.zeros((P, NPAR), f)

    def put(name, x):
        at, n = PAR[name]
        par[:, at:at + n] = x

    put("g1", a["norm1_g"][0].reshape(KT, P).T)
    put("g2", a["norm2_g"][0].reshape(KT, P).T)
    put("qg", a["q_norm_g"][0][None])
    put("kgc", a["k_norm_g"][0, 0][None])
    put("kgs", a["k_norm_g"][0, 1:3].reshape(1, 128))
    put("posk", a["cmp_pos_k"][0].reshape(16, P).T)
    put("posv", a["cmp_pos_v"][0].reshape(16, P).T)
    put("w2k", a["cmp_k_w2"][0].reshape(2, P, HD).transpose(1, 0, 2).reshape(P, 128))
    put("w2v", a["cmp_v_w2"][0].reshape(2, P, HD).transpose(1, 0, 2).reshape(P, 128))
    put("subk", a["peer_subkeys"][0].transpose(2, 0, 1).reshape(P, 256))
    put("gw", col["gn"].reshape(KT, P, 24).transpose(1, 0, 2).reshape(P, 192))
    return np.ascontiguousarray(wpre), np.ascontiguousarray(u), np.ascontiguousarray(v), par


def constants():
    f = np.float32
    cst, kep = np.zeros((P, NCST), f), np.zeros((P, NKEP), f)

    def put(name, x):
        at, n = CST[name]
        cst[:, at:at + n] = x

    half = HD // 2
    freqs = (f(10000.0) ** (-np.arange(half, dtype=f) / f(half))).astype(f)

    def table(pos):
        ang = pos.astype(f)[:, None] * freqs[None]
        c, s = np.cos(ang).astype(f), np.sin(ang).astype(f)
        return np.concatenate([c, c], 1), np.concatenate([-s, s], 1)

    c, s = table(np.arange(T))
    put("cos", c.reshape(TB, P, HD).transpose(1, 0, 2).reshape(P, 128))
    put("sin", s.reshape(TB, P, HD).transpose(1, 0, 2).reshape(P, 128))
    c, s = table(np.arange(P) * 16 + CL - 1)
    put("cosc", c)
    put("sinc", s)
    r, k = np.arange(P)[:, None], np.arange(P)[None]
    put("tri", np.where(r > k, -1.0, 0.0))
    put("ones", -1.0)
    causal = np.where(k <= r, 0.0, NEG)
    end = np.arange(NC_)[None] * 16 + CL - 1
    put("mask", np.concatenate([causal, np.zeros((P, P)), causal, np.where(end <= r, 0.0, NEG),
                                np.where(end <= r + P, 0.0, NEG)], 1))
    strict = np.where(r < k, 1.0, 0.0)
    put("msb", np.concatenate([strict, np.ones((P, P)), strict], 1))
    put("hasc", np.where(r >= CL - 1, 1.0, 0.0))
    kep[:, KEP["ident"][0]:KEP["ident"][0] + P] = np.eye(P)
    kep[:, KEP["iota"][0]:KEP["iota"][0] + P] = k
    kep[:, KEP["iota16"][0]:KEP["iota16"][0] + 16] = np.arange(16)[None]
    return cst, kep


def kernel(**inputs):
    import concourse.bacc as bacc
    from concourse.bass_utils import run_bass_kernel_spmd

    a = {k: np.asarray(v) for k, v in inputs.items()}
    wpre, u, v, par = lay_out(a)
    cst, kep = constants()
    arrays = dict(x_d=np.ascontiguousarray(a["x"][0]), wpre_d=wpre, u_d=u, v_d=v, par_d=par, cst_d=cst, kep_d=kep)
    nc = bacc.Bacc("TRN2", target_bir_lowering=False, num_devices=1)
    args = [nc.dram_tensor(k, x.shape, mybir.dt.from_np(x.dtype), kind="ExternalInput").ap() for k, x in arrays.items()]
    args.append(nc.dram_tensor("out_d", (T, D), F32, kind="ExternalOutput").ap())
    build(nc, *args)
    r = run_bass_kernel_spmd(nc, [arrays], core_ids=[0])
    return r.results[0]["out_d"].reshape(1, T, D)
```
